# Optimizing a Trainium2 kernel written in Bass

```python
import jax, jax.numpy as jnp
from jax import lax
import numpy as np

D_MODEL = 1024
BATCH = 1
SEQ = 256
DEPTH = 2

ROPE_THETA = 10000.0
LN_EPS = 1e-5
RMS_EPS = 1e-6
DEEPNORM_ALPHA = (2 * DEPTH) ** 0.25
DEEPNORM_BETA = (8 * DEPTH) ** -0.25
NEG_BIG = -1e30
FORCE_SCORE = 1e4

HEAD_DIM = 64
SWA_Q_HEADS = 8
SWA_KV_HEADS = 2
SWA_WINDOW = 128
NSA_Q_HEADS = 8
NSA_KV_HEADS = 2
NSA_CMP_LEN = 32
NSA_CMP_STRIDE = 16
NSA_CMP_HIDDEN = 128
NSA_SEL_LEN = 64
NSA_N_SEL = 16
NSA_WINDOW = 512
NSA_QUERY_BLOCK = 64
BAND_QUERY_BLOCK = 128
MIX0_WIDTH = (SWA_Q_HEADS + NSA_Q_HEADS) * HEAD_DIM
MIX0_SPLITS = (
    SWA_Q_HEADS * HEAD_DIM,
    SWA_KV_HEADS * HEAD_DIM,
    SWA_KV_HEADS * HEAD_DIM,
    NSA_Q_HEADS * HEAD_DIM,
    NSA_KV_HEADS * HEAD_DIM,
    NSA_KV_HEADS * HEAD_DIM,
    NSA_KV_HEADS * HEAD_DIM,
    NSA_KV_HEADS * HEAD_DIM,
    NSA_KV_HEADS * HEAD_DIM,
    NSA_KV_HEADS * HEAD_DIM,
    3 * NSA_Q_HEADS,
)
MIX0_IN = sum(MIX0_SPLITS)

MLA_HEADS = 16
MLA_NOPE = 64
MLA_ROPE = 32
MLA_V = 64
MLA_Q_LORA = 384
MLA_KV_LORA = 256
MLA_QUERY_BLOCK = 128
MLA_IN = MLA_Q_LORA + MLA_KV_LORA + MLA_ROPE

N_EXPERTS = 64
MOE_GROUPS = 8
MOE_TOPK_GROUPS = 4
MOE_TOP_K = 6
D_EXPERT = 256
D_SHARED = 256
MOE_ROUTED_SCALE = 2.5
MOE_ROW_BLOCK = 256

N_EVEN = (DEPTH + 1) // 2
N_ODD = DEPTH // 2

kernel_name = "hybrid_swa_nsa_mla_moe_deepnorm"

def _rope(x, pos):
    d = x.shape[-1]
    half = d // 2
    inv_freq = ROPE_THETA ** (-2.0 * jnp.arange(half, dtype=jnp.float32) / d)
    ang = pos.astype(jnp.float32)[:, None] * inv_freq[None, :]
    cos = jnp.cos(ang)[:, None, :].astype(x.dtype)
    sin = jnp.sin(ang)[:, None, :].astype(x.dtype)
    x1, x2 = x[..., :half], x[..., half:]
    return jnp.concatenate([x1 * cos - x2 * sin, x1 * sin + x2 * cos], axis=-1)

def _layer_norm(x, g, b):
    xf = x.astype(jnp.float32)
    mu = xf.mean(-1, keepdims=True)
    xc = xf - mu
    var = (xc * xc).mean(-1, keepdims=True)
    return (xc * lax.rsqrt(var + LN_EPS) * g.astype(jnp.float32) + b.astype(jnp.float32)).astype(x.dtype)

def _rms_norm(x, g):
    xf = x.astype(jnp.float32)
    y = xf * lax.rsqrt((xf * xf).mean(-1, keepdims=True) + RMS_EPS)
    return (y * g.astype(jnp.float32)).astype(x.dtype)

def _banded_attention(q, k, v, window, sinks):
    B, S, G, R, d = q.shape
    C = BAND_QUERY_BLOCK
    n_blk = S // C
    L = window + C
    scale = d ** -0.5
    kp = jnp.pad(k, ((0, 0), (window, 0), (0, 0), (0, 0)))
    vp = jnp.pad(v, ((0, 0), (window, 0), (0, 0), (0, 0)))
    q_blocks = q.reshape(B, n_blk, C, G, R, d).swapaxes(0, 1)

    def step(args):
        i, qb = args
        start = i * C
        kb = lax.dynamic_slice_in_dim(kp, start, L, axis=1)
        vb = lax.dynamic_slice_in_dim(vp, start, L, axis=1)
        s = jnp.einsum('bqgrd,bkgd->bgrqk', qb, kb).astype(jnp.float32) * scale
        tq = start + jnp.arange(C)
        tk = start - window + jnp.arange(L)
        diff = tq[:, None] - tk[None, :]
        mask = (diff >= 0) & (diff < window) & (tk[None, :] >= 0)
        s = jnp.where(mask, s, -jnp.inf)
        if sinks is not None:
            sink = jnp.broadcast_to(sinks.astype(jnp.float32).reshape(1, G, R, 1, 1), s.shape[:-1] + (1,))
            p = jax.nn.softmax(jnp.concatenate([sink, s], axis=-1), axis=-1)[..., 1:]
        else:
            p = jax.nn.softmax(s, axis=-1)
        return jnp.einsum('bgrqk,bkgd->bqgrd', p.astype(vb.dtype), vb)

    o = lax.map(step, (jnp.arange(n_blk), q_blocks))
    return o.swapaxes(0, 1).reshape(B, S, G, R, d)

def _causal_attention(q, k, v):
    B, S, H, dq = q.shape
    dv = v.shape[-1]
    C = MLA_QUERY_BLOCK
    n_blk = S // C
    scale = dq ** -0.5
    q_blocks = q.reshape(B, n_blk, C, H, dq).swapaxes(0, 1)
    tk = jnp.arange(S)

    def step(args):
        i, qb = args
        tq = i * C + jnp.arange(C)
        s = jnp.einsum('bqhd,bkhd->bhqk', qb, k).astype(jnp.float32) * scale
        s = jnp.where(tk[None, :] <= tq[:, None], s, -jnp.inf)
        p = jax.nn.softmax(s, axis=-1)
        return jnp.einsum('bhqk,bkhd->bqhd', p.astype(v.dtype), v)

    o = lax.map(step, (jnp.arange(n_blk), q_blocks))
    return o.swapaxes(0, 1).reshape(B, S, H, dv)

def _compress(t, pe, w1, w2):
    B, S, G, d = t.shape
    n_cmp = (S - NSA_CMP_LEN) // NSA_CMP_STRIDE + 1
    idx = np.arange(n_cmp)[:, None] * NSA_CMP_STRIDE + np.arange(NSA_CMP_LEN)[None, :]
    blk = t[:, idx] + pe[:, None, :]
    blk = blk.transpose(0, 1, 3, 2, 4).reshape(B, n_cmp, G, NSA_CMP_LEN * d)
    return jax.nn.gelu(blk @ w1) @ w2

def _nsa_cmp_sel(q, kc, vc, ks, vs):
    B, S, G, R, d = q.shape
    n_cmp = kc.shape[1]
    n_sb = S // NSA_SEL_LEN
    n_sel = min(NSA_N_SEL, n_sb)
    C = NSA_QUERY_BLOCK
    n_qb = S // C
    scale = d ** -0.5
    cs = np.arange(n_cmp) * NSA_CMP_STRIDE
    bs = np.arange(n_sb) * NSA_SEL_LEN
    ov = np.clip(np.minimum(cs[:, None] + NSA_CMP_LEN, bs[None, :] + NSA_SEL_LEN)
                 - np.maximum(cs[:, None], bs[None, :]), 0, None) / NSA_CMP_LEN
    overlap = jnp.asarray(ov, dtype=jnp.float32)
    cmp_end = jnp.asarray(cs + NSA_CMP_LEN - 1)
    ks_blk = ks.reshape(B, n_sb, NSA_SEL_LEN, G, d).transpose(0, 3, 1, 2, 4)
    vs_blk = vs.reshape(B, n_sb, NSA_SEL_LEN, G, d).transpose(0, 3, 1, 2, 4)
    bi = jnp.arange(B)[:, None, None, None]
    gi = jnp.arange(G)[None, :, None, None]
    blk_ids = jnp.arange(n_sb)
    q_blocks = q.reshape(B, n_qb, C, G, R, d).swapaxes(0, 1)

    def step(args):
        i, qb = args
        tq = i * C + jnp.arange(C)
        s_c = jnp.einsum('bqgrd,bngd->bgrqn', qb, kc).astype(jnp.float32) * scale
        mask_c = cmp_end[None, :] <= tq[:, None]
        s_c = jnp.where(mask_c, s_c, NEG_BIG)
        p_c = jnp.exp(s_c - s_c.max(-1, keepdims=True)) * mask_c
        p_c = p_c / jnp.maximum(p_c.sum(-1, keepdims=True), 1e-30)
        o_c = jnp.einsum('bgrqn,bngd->bqgrd', p_c.astype(vc.dtype), vc)
        imp = jnp.einsum('bgrqn,nm->bgqm', p_c, overlap)
        cur = tq // NSA_SEL_LEN
        forced = ((blk_ids[None, :] == 0) | (blk_ids[None, :] == cur[:, None])
                  | (blk_ids[None, :] == cur[:, None] - 1))
        future = blk_ids[None, :] * NSA_SEL_LEN > tq[:, None]
        score = jnp.where(forced, FORCE_SCORE, jnp.where(future, -1.0, imp))
        _, idx = lax.top_k(score, n_sel)
        kg = ks_blk[bi, gi, idx]
        vg = vs_blk[bi, gi, idx]
        tk = idx[..., None] * NSA_SEL_LEN + jnp.arange(NSA_SEL_LEN)
        mask_s = (tk <= tq[None, None, :, None, None])[:, :, None]
        s_s = jnp.einsum('bqgrd,bgqnld->bgrqnl', qb, kg).astype(jnp.float32) * scale
        s_s = jnp.where(mask_s, s_s, -jnp.inf)
        p_s = jax.nn.softmax(s_s.reshape(B, G, R, C, n_sel * NSA_SEL_LEN), axis=-1).reshape(s_s.shape)
        o_s = jnp.einsum('bgrqnl,bgqnld->bqgrd', p_s.astype(vg.dtype), vg)
        return o_c, o_s

    o_c, o_s = lax.map(step, (jnp.arange(n_qb), q_blocks))
    o_c = o_c.swapaxes(0, 1).reshape(B, S, G, R, d)
    o_s = o_s.swapaxes(0, 1).reshape(B, S, G, R, d)
    return o_c, o_s

def _swa_nsa_mixer(x, w_in, sinks, pe_k, w_ck1, w_ck2, pe_v, w_cv1, w_cv2, w_out):
    B, S, _ = x.shape
    pos = jnp.arange(S)
    parts = jnp.split(x @ w_in, [int(c) for c in np.cumsum(MIX0_SPLITS)[:-1]], axis=-1)
    qa, ka, va, qb, kc, vc, ksl, vsl, kw, vw, gates = parts
    heads = lambda t, h: t.reshape(B, S, h, HEAD_DIM)
    ra = SWA_Q_HEADS // SWA_KV_HEADS
    rb = NSA_Q_HEADS // NSA_KV_HEADS
    qa = _rope(heads(qa, SWA_Q_HEADS), pos).reshape(B, S, SWA_KV_HEADS, ra, HEAD_DIM)
    ka = _rope(heads(ka, SWA_KV_HEADS), pos)
    o_swa = _banded_attention(qa, ka, heads(va, SWA_KV_HEADS), SWA_WINDOW, sinks)
    qb = _rope(heads(qb, NSA_Q_HEADS), pos).reshape(B, S, NSA_KV_HEADS, rb, HEAD_DIM)
    k_cmp = _compress(heads(kc, NSA_KV_HEADS), pe_k, w_ck1, w_ck2)
    n_cmp = k_cmp.shape[1]
    k_cmp = _rope(k_cmp, jnp.arange(n_cmp) * NSA_CMP_STRIDE + NSA_CMP_LEN - 1)
    v_cmp = _compress(heads(vc, NSA_KV_HEADS), pe_v, w_cv1, w_cv2)
    k_sel = _rope(heads(ksl, NSA_KV_HEADS), pos)
    o_cmp, o_sel = _nsa_cmp_sel(qb, k_cmp, v_cmp, k_sel, heads(vsl, NSA_KV_HEADS))
    o_win = _banded_attention(qb, _rope(heads(kw, NSA_KV_HEADS), pos), heads(vw, NSA_KV_HEADS),
                              NSA_WINDOW, None)
    g = jax.nn.sigmoid(gates.astype(jnp.float32)).astype(x.dtype).reshape(B, S, 3, NSA_KV_HEADS, rb, 1)
    o_nsa = g[:, :, 0] * o_cmp + g[:, :, 1] * o_sel + g[:, :, 2] * o_win
    o = jnp.concatenate([o_swa.reshape(B, S, -1), o_nsa.reshape(B, S, -1)], axis=-1)
    return o @ w_out

def _mla_mixer(x, w_in, q_norm, kv_norm, w_uq, w_ukv, w_out):
    B, S, _ = x.shape
    pos = jnp.arange(S)
    c_q, c_kv, k_r = jnp.split(x @ w_in, [MLA_Q_LORA, MLA_Q_LORA + MLA_KV_LORA], axis=-1)
    q = (_rms_norm(c_q, q_norm) @ w_uq).reshape(B, S, MLA_HEADS, MLA_NOPE + MLA_ROPE)
    kv = (_rms_norm(c_kv, kv_norm) @ w_ukv).reshape(B, S, MLA_HEADS, MLA_NOPE + MLA_V)
    q = jnp.concatenate([q[..., :MLA_NOPE], _rope(q[..., MLA_NOPE:], pos)], axis=-1)
    k_rope = _rope(k_r.reshape(B, S, 1, MLA_ROPE), pos)
    k = jnp.concatenate([kv[..., :MLA_NOPE], jnp.broadcast_to(k_rope, (B, S, MLA_HEADS, MLA_ROPE))], axis=-1)
    o = _causal_attention(q, k, kv[..., MLA_NOPE:])
    return o.reshape(B, S, MLA_HEADS * MLA_V) @ w_out

def _moe(x, router_w, router_bias, w_gate, w_up, w_down, sh_gate, sh_up, sh_down):
    B, S, D = x.shape
    n_tok = B * S
    xf = x.reshape(n_tok, D)
    s = jax.nn.sigmoid((xf @ router_w).astype(jnp.float32))
    sb = s + router_bias.astype(jnp.float32)
    grp = sb.reshape(n_tok, MOE_GROUPS, N_EXPERTS // MOE_GROUPS)
    grp_score = lax.top_k(grp, 2)[0].sum(-1)
    _, gidx = lax.top_k(grp_score, MOE_TOPK_GROUPS)
    gmask = jnp.any(gidx[:, :, None] == jnp.arange(MOE_GROUPS)[None, None, :], axis=1)
    emask = jnp.repeat(gmask, N_EXPERTS // MOE_GROUPS, axis=1)
    _, eidx = lax.top_k(jnp.where(emask, sb, -jnp.inf), MOE_TOP_K)
    gate = jnp.take_along_axis(s, eidx, axis=1)
    gate = gate / gate.sum(-1, keepdims=True) * MOE_ROUTED_SCALE
    n_rows = n_tok * MOE_TOP_K
    flat_e = eidx.reshape(-1)
    flat_t = jnp.repeat(jnp.arange(n_tok), MOE_TOP_K)
    order = jnp.argsort(flat_e)
    e_s = flat_e[order]
    counts = jnp.bincount(flat_e, length=N_EXPERTS)
    padded = (counts + MOE_ROW_BLOCK - 1) // MOE_ROW_BLOCK * MOE_ROW_BLOCK
    starts = jnp.cumsum(counts) - counts
    pad_ends = jnp.cumsum(padded)
    pad_starts = pad_ends - padded
    dest = pad_starts[e_s] + jnp.arange(n_rows) - starts[e_s]
    n_blk = -(-(n_rows + N_EXPERTS * (MOE_ROW_BLOCK - 1)) // MOE_ROW_BLOCK)
    n_pad_rows = n_blk * MOE_ROW_BLOCK
    row_tok = jnp.zeros((n_pad_rows,), jnp.int32).at[dest].set(flat_t[order])
    row_w = jnp.zeros((n_pad_rows,), x.dtype).at[dest].set(gate.reshape(-1)[order].astype(x.dtype))
    blk_exp = jnp.minimum(jnp.searchsorted(pad_ends, jnp.arange(n_blk) * MOE_ROW_BLOCK, side='right'),
                          N_EXPERTS - 1)

    def body(acc, blk):
        tok, w, e = blk
        xb = xf[tok]
        h = jax.nn.silu(xb @ w_gate[e]) * (xb @ w_up[e])
        return acc.at[tok].add((h @ w_down[e]) * w[:, None]), None

    routed, _ = lax.scan(body, jnp.zeros_like(xf),
                         (row_tok.reshape(n_blk, MOE_ROW_BLOCK), row_w.reshape(n_blk, MOE_ROW_BLOCK), blk_exp))
    shared = (jax.nn.silu(xf @ sh_gate) * (xf @ sh_up)) @ sh_down
    return (routed + shared).reshape(B, S, D)

def setup_inputs(seed: int = 0) -> dict:
    key = jax.random.key(seed)
    keys = iter(jax.random.split(key, 40))

    def nrm(shape, scale):
        return jax.random.normal(next(keys), shape, jnp.float32) * scale

    d = D_MODEL
    return {
        'x': nrm((BATCH, SEQ, d), 1.0),
        'swa_nsa_w_in': nrm((N_EVEN, d, MIX0_IN), d ** -0.5),
        'swa_sinks': nrm((N_EVEN, SWA_Q_HEADS), 1.0),
        'nsa_cmp_pe_k': nrm((N_EVEN, NSA_CMP_LEN, HEAD_DIM), 0.5),
        'nsa_cmp_k_w1': nrm((N_EVEN, NSA_CMP_LEN * HEAD_DIM, NSA_CMP_HIDDEN), (NSA_CMP_LEN * HEAD_DIM) ** -0.5),
        'nsa_cmp_k_w2': nrm((N_EVEN, NSA_CMP_HIDDEN, HEAD_DIM), NSA_CMP_HIDDEN ** -0.5),
        'nsa_cmp_pe_v': nrm((N_EVEN, NSA_CMP_LEN, HEAD_DIM), 0.5),
        'nsa_cmp_v_w1': nrm((N_EVEN, NSA_CMP_LEN * HEAD_DIM, NSA_CMP_HIDDEN), (NSA_CMP_LEN * HEAD_DIM) ** -0.5),
        'nsa_cmp_v_w2': nrm((N_EVEN, NSA_CMP_HIDDEN, HEAD_DIM), NSA_CMP_HIDDEN ** -0.5),
        'swa_nsa_w_out': nrm((N_EVEN, MIX0_WIDTH, d), MIX0_WIDTH ** -0.5 * DEEPNORM_BETA),
        'mla_w_in': nrm((N_ODD, d, MLA_IN), d ** -0.5),
        'mla_q_norm': 1.0 + nrm((N_ODD, MLA_Q_LORA), 0.01),
        'mla_kv_norm': 1.0 + nrm((N_ODD, MLA_KV_LORA), 0.01),
        'mla_w_uq': nrm((N_ODD, MLA_Q_LORA, MLA_HEADS * (MLA_NOPE + MLA_ROPE)), MLA_Q_LORA ** -0.5),
        'mla_w_ukv': nrm((N_ODD, MLA_KV_LORA, MLA_HEADS * (MLA_NOPE + MLA_V)), MLA_KV_LORA ** -0.5),
        'mla_w_out': nrm((N_ODD, MLA_HEADS * MLA_V, d), (MLA_HEADS * MLA_V) ** -0.5 * DEEPNORM_BETA),
        'ln_mix_g': 1.0 + nrm((DEPTH, d), 0.01),
        'ln_mix_b': nrm((DEPTH, d), 0.01),
        'ln_ffn_g': 1.0 + nrm((DEPTH, d), 0.01),
        'ln_ffn_b': nrm((DEPTH, d), 0.01),
        'router_w': nrm((DEPTH, d, N_EXPERTS), d ** -0.5),
        'router_bias': nrm((DEPTH, N_EXPERTS), 0.01),
        'expert_w_gate': nrm((DEPTH, N_EXPERTS, d, D_EXPERT), d ** -0.5),
        'expert_w_up': nrm((DEPTH, N_EXPERTS, d, D_EXPERT), d ** -0.5),
        'expert_w_down': nrm((DEPTH, N_EXPERTS, D_EXPERT, d), D_EXPERT ** -0.5 * DEEPNORM_BETA),
        'shared_w_gate': nrm((DEPTH, d, D_SHARED), d ** -0.5),
        'shared_w_up': nrm((DEPTH, d, D_SHARED), d ** -0.5),
        'shared_w_down': nrm((DEPTH, D_SHARED, d), D_SHARED ** -0.5 * DEEPNORM_BETA),
    }

def reference(x, swa_nsa_w_in, swa_sinks, nsa_cmp_pe_k, nsa_cmp_k_w1, nsa_cmp_k_w2, nsa_cmp_pe_v,
              nsa_cmp_v_w1, nsa_cmp_v_w2, swa_nsa_w_out, mla_w_in, mla_q_norm, mla_kv_norm, mla_w_uq,
              mla_w_ukv, mla_w_out, ln_mix_g, ln_mix_b, ln_ffn_g, ln_ffn_b, router_w, router_bias,
              expert_w_gate, expert_w_up, expert_w_down, shared_w_gate, shared_w_up, shared_w_down):
    for layer in range(DEPTH):
        j = layer // 2
        if layer % 2 == 0:
            h = _swa_nsa_mixer(x, swa_nsa_w_in[j], swa_sinks[j], nsa_cmp_pe_k[j], nsa_cmp_k_w1[j],
                               nsa_cmp_k_w2[j], nsa_cmp_pe_v[j], nsa_cmp_v_w1[j], nsa_cmp_v_w2[j],
                               swa_nsa_w_out[j])
        else:
            h = _mla_mixer(x, mla_w_in[j], mla_q_norm[j], mla_kv_norm[j], mla_w_uq[j], mla_w_ukv[j],
                           mla_w_out[j])
        x = _layer_norm(DEEPNORM_ALPHA * x + h, ln_mix_g[layer], ln_mix_b[layer])
        f = _moe(x, router_w[layer], router_bias[layer], expert_w_gate[layer], expert_w_up[layer],
                 expert_w_down[layer], shared_w_gate[layer], shared_w_up[layer], shared_w_down[layer])
        x = _layer_norm(DEEPNORM_ALPHA * x + f, ln_ffn_g[layer], ln_ffn_b[layer])
    return x


_drawn_inputs = setup_inputs


def setup_inputs(seed=0):
    import zlib

    import numpy as np

    out = dict(_drawn_inputs(seed))
    spreads = {}
    factors = {'swa_sinks': 2.91, 'mla_q_norm': 7.863, 'mla_kv_norm': 8.0}
    for name, (base, spread) in spreads.items():
        noise = np.random.default_rng([zlib.crc32(name.encode()), seed]).standard_normal(out[name].shape)
        drawn = base * np.exp(spread * noise) if base else spread * noise
        out[name] = __import__('jax').numpy.asarray(drawn.astype(out[name].dtype))
    for name, factor in factors.items():
        out[name] = (out[name] * factor).astype(out[name].dtype)
    return out
```

```python
from contextlib import ExitStack

import numpy as np

import concourse.bass as bass
from concourse import mybir

F32 = mybir.dt.float32
ALU = mybir.AluOpType
ACT = mybir.ActivationFunctionType
AX_X = mybir.AxisListType.X

P = 128
S, D = 256, 1024
TC = S // P
KC = D // P
HD, HALF = 64, 32
G, R = 2, 4
MIX0 = (512, 128, 128, 512, 128, 128, 128, 128, 128, 128, 24)
COL = [int(c) for c in np.cumsum((0,) + MIX0)]
(C_QA, C_KA, C_VA, C_QB, C_KC, C_VC, C_KS, C_VS, C_KW, C_VW, C_GT) = COL[:11]
IN0 = COL[11]
NGATE = MIX0[10]
CMP_LEN, CMP_STRIDE, CMP_HID = 32, 16, 128
NCMP = (S - CMP_LEN) // CMP_STRIDE + 1
WINDOW = 128
MH, NOPE, ROPE, MV = 16, 64, 32, 64
DQK = NOPE + ROPE
QL, KVL = 384, 256
IN1 = QL + KVL + ROPE
NE, NG, EPG, TOPG, TOPK, DE = 64, 8, 8, 4, 6, 256
ROUTED_SCALE = 2.5
LN_EPS, RMS_EPS = 1e-5, 1e-6
ALPHA = (2 * 2) ** 0.25
THETA = 10000.0
NEG = -1e30
LOWEST, PICKED = -3e38, 3e38
GELU_C = 2.0 * float(np.sqrt(2.0 / np.pi))
NSLOT = 4
SLOT = 3 * D * DE // P

K_ID, K_CAUSAL, K_SWA, K_COS, K_SIN = 0, 128, 384, 640, 768
K_COS1, K_SIN1, K_CCOS, K_CSIN, K_CADD, K_CMUL = 896, 960, 1024, 1088, 1152, 1182
NCONST = 1212


def constants():
    c = np.zeros((P, NCONST), np.float32)
    q = np.arange(P)[:, None]
    k = np.arange(P)[None, :]
    c[:, K_ID:K_ID + P] = np.eye(P)
    c[:, K_CAUSAL + P:K_CAUSAL + 2 * P] = np.where(k <= q, 0.0, NEG)
    c[:, K_SWA:K_SWA + P] = np.where(k > q, 0.0, NEG)
    c[:, K_SWA + P:K_SWA + 2 * P] = np.where(k <= q, 0.0, NEG)

    def table(pos, d):
        inv = np.float32(THETA) ** (np.float32(-2.0) * np.arange(d // 2, dtype=np.float32) / np.float32(d))
        ang = pos.astype(np.float32)[:, None] * inv.astype(np.float32)[None, :]
        return np.tile(np.cos(ang), 2), np.tile(np.sin(ang), 2)

    for tc in range(TC):
        pos = np.arange(tc * P, tc * P + P)
        for (kc, ks), d in (((K_COS, K_SIN), HD), ((K_COS1, K_SIN1), ROPE)):
            cos, sin = table(pos, d)
            c[:, kc + tc * d:kc + tc * d + d] = cos
            c[:, ks + tc * d:ks + tc * d + d] = sin
    cos, sin = table(np.arange(NCMP) * CMP_STRIDE + CMP_LEN - 1, HD)
    c[:NCMP, K_CCOS:K_CCOS + HD] = cos
    c[:NCMP, K_CSIN:K_CSIN + HD] = sin
    end = np.arange(NCMP) * CMP_STRIDE + CMP_LEN - 1
    for tc in range(TC):
        seen = end[None, :] <= (np.arange(P) + tc * P)[:, None]
        c[:, K_CADD + tc * NCMP:K_CADD + (tc + 1) * NCMP] = np.where(seen, 0.0, NEG)
        c[:, K_CMUL + tc * NCMP:K_CMUL + (tc + 1) * NCMP] = seen
    return c


SEMS = (
    ["const_in", "x_in", "pe_in", "cmpw_in", "small0_in", "small1_in"]
    + [f"win_in{c}" for c in range(KC)]
    + [f"{n}{L}" for L in range(2) for n in (
        "ln_mix_in", "ln_ffn_in", "wout_in", "shared_in", "router_in",
        "proj_pe", "proj_act", "proj_dve", "rope_dve", "qk_pe", "qk_act",
        "score_pe", "max_dve", "exp_act", "ptr_pe", "ptr_act", "pv_pe", "o_dve",
        "out_pe", "out_free", "lnmix_dve", "lnffn_dve", "logit_pe", "sig_act", "gate_dve",
        "gu_pe", "silu_act", "h_dve", "ht_pe", "ht_act", "down_pe", "acc_pe",
        "slot_in0_", "slot_in1_", "slot_in2_", "slot_in3_",
    )]
    + ["xt_pe", "xt_act", "xt_dve", "pet_pe", "pet_act", "gates_pe", "gates_act", "gates_dve", "kcv_pe", "kcv_act", "blk_dve",
       "hid_pe", "hid_act", "gelu_dve", "gin_dve", "gexp_act", "cmp_dve", "kv2_pe", "kcn_dve", "kct_pe", "kct_dve",
       "vbd_dve", "zero_pool", "csc_pe", "csub_dve", "cexp_act", "cp_dve", "cpt_pe", "cpt_act",
       "sink_dve", "sink_act", "win1_in", "wuq_in", "wukv_in",
       "var_dve", "root_pool", "power_pool", "rms_dve", "cnt_pe", "cnt_act", "q_pe", "q_act", "kv_pe", "kv_act",
       "krope_dve", "krt_pe", "krt_act", "qrope_dve", "kfull_act", "act_chain", "dve_chain", "out_done"]
)


def bass_hybrid_block(nc, x, w_in0, sinks, pe_k, ck1, ck2, pe_v, cv1, cv2, w_out0, w_in1, q_norm,
                      kv_norm, w_uq, w_ukv, w_out1, ln_mix_g, ln_mix_b, ln_ffn_g, ln_ffn_b,
                      router_w, router_bias, e_gate, e_up, e_down, s_gate, s_up, s_down, const, out):
    ctx = ExitStack()
    with ctx:
        def sb(name, cols):
            return ctx.enter_context(nc.sbuf_tensor(name, [P, cols], F32))

        sem = {n: ctx.enter_context(nc.semaphore(n)) for n in SEMS}
        cst = sb("cst", NCONST)
        xn = sb("x_rows", TC * D)
        xt = sb("x_cols", KC * S)
        ring = sb("ring", NSLOT * SLOT)
        wbig = sb("wbig", 8 * D)
        lnp = sb("lnp", 2 * D)
        arena = sb("arena", 10800)
        tmp = sb("tmp", 1280)
        rw = sb("rw", KC * NE)
        rbias = sb("rbias", NE)
        small = sb("small", 256)

        PS = [ctx.enter_context(nc.psum_tensor(f"psum{i}", [P, 1024], F32)) for i in range(4)]
        BANK = [PS[i // 2][:, 512 * (i % 2):512 * (i % 2) + 512] for i in range(8)]

        def v(ap, **k):
            names = list(k)
            return ap.rearrange("p (" + " ".join(names) + ") -> p " + " ".join(names), **k)

        ident = cst[:, K_ID:K_ID + P]
        xrow = v(xn[:, :], t=TC, d=D)
        xcol = v(xt[:, :], c=KC, t=S)
        slot = [ring[:, i * SLOT:(i + 1) * SLOT] for i in range(NSLOT)]
        lng, lnb = lnp[:, 0:D], lnp[:, D:2 * D]
        wout = v(wbig[:, :], c=KC, d=D)

        def expert(w):
            gu = w[:, 0:2 * KC * DE].rearrange("p (m c f) -> p c m f", m=2, c=KC)
            return gu, w[:, 2 * KC * DE:SLOT].rearrange("p (c d) -> p c d", c=DE // P)

        at = [0]

        def take(n):
            at[0] += n
            return small[:, at[0] - n:at[0]]

        stats, mv = take(12), take(2)
        var, root, power = take(2), take(2), take(2)
        gates = take(TC * NGATE)
        nmax = take(12 * R)
        sums = take(12 * R)
        rec = take(16)
        nsink, sinkb = take(8), take(8)
        esink = take(16)
        kcmpt = take(NCMP)
        ssq = take(4)

        qkv = v(arena[:, 0:TC * IN0], t=TC, n=IN0)
        a0 = TC * IN0
        NB = 11
        rope = v(arena[:, a0:a0 + TC * NB * P], t=TC, n=NB * P)
        s0 = [arena[:, a0 + i * 1024:a0 + (i + 1) * 1024] for i in range(2)]
        a1 = a0 + TC * NB * P
        qkt = v(arena[:, a1:a1 + NB * S], b=NB, t=S)
        ot0 = v(arena[:, a1:a1 + KC * S], c=KC, t=S)
        a2 = a1 + NB * S
        kcv = v(arena[:, a2:a2 + 4 * S], b=4, t=S)
        pt0 = arena[:, a2:a2 + 1024]
        last = slot[3]
        cw1 = [v(last[:, i * 2048:(i + 1) * 2048], l=16, h=CMP_HID) for i in range(2)]
        b0 = 4096
        cw2 = [last[:, b0 + i * HD:b0 + (i + 1) * HD] for i in range(2)]
        pen = last[:, b0 + 128:b0 + 256]
        pet = v(last[:, b0 + 256:b0 + 320], k=2, l=CMP_LEN)
        blk = [last[:, b0 + 320 + i * 480:b0 + 800 + i * 480].rearrange("p (l g n) -> p l g n", l=16, g=G) for i in range(2)]
        vbd = [v(last[:, i * 256:(i + 1) * 256], j=R, d=HD) for i in range(2)]
        cs = v(last[:, 512:512 + 256], t=TC, h=8, n=16)
        cp = v(last[:, 768:768 + 512], t=TC, h=8, n=32)
        cpt = v(last[:, 1280:1280 + 512], u=4, q=P)
        kcn = last[:, 1792:1792 + 128]
        cu = last[:, 1920:2048]
        hidw = [last[:, 5376 + i * 64:5376 + (i + 1) * 64] for i in range(6)]
        crec = last[:, 5760:5776]

        uq = v(slot[0][:, 0:QL // P * MH * DQK], c=QL // P, n=MH * DQK)
        ukv = v(slot[1][:, 0:KVL // P * MH * 128], c=KVL // P, n=MH * 128)
        win1 = v(slot[2][:, 0:KC * IN1], c=KC, n=IN1)
        qn1 = v(slot[2][:, 0:TC * MH * DQK], t=TC, n=MH * DQK)
        qt1 = v(slot[3][:, 0:MH * S], h=MH, t=S)
        c1 = v(slot[3][:, MH * S:MH * S + TC * IN1], t=TC, n=IN1)
        kt1 = v(arena[:, 0:MH * S], h=MH, t=S)
        kv1 = v(arena[:, MH * S:MH * S + TC * MH * 128], t=TC, n=MH * 128)
        e0 = MH * S + TC * MH * 128
        ct1 = v(arena[:, e0:e0 + 5 * S], c=5, t=S)
        pt1 = arena[:, e0 + 5 * S:e0 + 5 * S + 1024]
        krt = arena[0:ROPE, e0 + 5 * S + 1024:e0 + 5 * S + 1024 + S]
        s1 = [xt[:, i * 1024:(i + 1) * 1024] for i in range(2)]
        nrm = ukv_norm = lnp
        atto = [v(xt[:, :], t=TC, n=D), v(slot[3][:, MH * S:MH * S + TC * D], t=TC, n=D)]
        attot = [ot0, xcol]

        hh = [arena[:, i * DE:(i + 1) * DE] for i in range(2)]
        sg = [arena[:, 512 + i * DE:512 + (i + 1) * DE] for i in range(2)]
        ht = [v(arena[:, 1024 + i * 256:1280 + i * 256], c=2, t=P) for i in range(2)]
        gate = v(arena[:, 2048:2048 + TC * NE], t=TC, e=NE)
        rs = v(arena[:, 2304:2304 + TC * NE], t=TC, e=NE)
        rsb = v(arena[:, 2432:2432 + TC * NE], t=TC, e=NE)
        top8 = arena[:, 2560:2560 + 128].rearrange("p (t g k) -> p t g k", t=TC, g=NG)
        gsc = v(arena[:, 2688:2688 + 32], t=TC, k=16)
        gpick = v(arena[:, 2720:2720 + 32], t=TC, k=16)
        gsel = v(arena[:, 2752:2752 + 16], t=TC, k=NG)
        gneg = v(arena[:, 2768:2768 + 16], t=TC, k=NG)
        m8 = v(arena[:, 2784:2784 + 16], t=TC, k=8)
        esc = v(arena[:, 2816:2816 + 144], t=TC, k=72)
        epick = v(arena[:, 2960:2960 + 144], t=TC, k=72)
        gsum = arena[:, 3104:3106]

        SRC = [xrow, atto[0], xrow, xrow, atto[1], xrow]
        DST = [xcol, attot[0], xcol, xcol, attot[1], xcol]

        def unit0(n):
            branch, qc, g = n // 4, n // 2 % 2, n % 2
            qb, kb, vc = [(0, 4, C_VA), (5, 9, C_VS), (5, 10, C_VW)][branch]
            rows = slice(HD * g, HD * g + HD)
            return dict(
                n=n, qc=qc, scale=HD ** -0.5, mask=K_SWA if branch == 0 else K_CAUSAL, sink=branch == 0,
                q=[qkt[rows, qb + j, qc * P:(qc + 1) * P] for j in range(R)],
                k=[qkt[rows, kb, 0:(qc + 1) * P]] * R,
                v=[[qkv[:, c, vc + HD * g:vc + HD * g + HD]] * R for c in range(qc + 1)])

        def unit1(n):
            qc, hg = n // 4, n % 4
            hs = range(4 * hg, 4 * hg + 4)
            return dict(
                n=n, qc=qc, scale=DQK ** -0.5, mask=K_CAUSAL, sink=False,
                q=[qt1[0:DQK, h, qc * P:(qc + 1) * P] for h in hs],
                k=[kt1[0:DQK, h, 0:(qc + 1) * P] for h in hs],
                v=[[kv1[:, c, h * 128 + NOPE:(h + 1) * 128] for h in hs] for c in range(qc + 1)])

        UNITS = [[unit0(n) for n in range(12)], [unit1(n) for n in range(8)]]
        SBUFS = [s0, s1]
        PTBUF = [pt0, pt1]

        block = ctx.enter_context(nc.Block())

        def router_loads(sp, L):
            sp.dma_start(v(rw[:, :], c=KC, e=NE), router_w[L].rearrange("(p c) e -> p c e", c=KC)).then_inc(sem[f"router_in{L}"], 16)
            sp.dma_start(rbias[:, :], router_bias[L:L + 1, :].partition_broadcast(P)[:, 0, :]).then_inc(sem[f"router_in{L}"], 16)

        def norm_loads(sp, name, g, b, L):
            sp.dma_start(lng, g[L:L + 1, :].partition_broadcast(P)[:, 0, :]).then_inc(sem[name], 16)
            sp.dma_start(lnb, b[L:L + 1, :].partition_broadcast(P)[:, 0, :]).then_inc(sem[name], 16)

        def load_parts(sp, dst, g, u, d, s):
            for i, w in enumerate((g, u)):
                sp.dma_start(dst[:, i * KC * DE:(i + 1) * KC * DE], w.rearrange("(p c) f -> p (c f)", c=KC)).then_inc(s, 16)
            sp.dma_start(dst[:, 2 * KC * DE:SLOT], d.rearrange("(p c) n -> p (c n)", c=DE // P)).then_inc(s, 16)

        def load_shared(sp, L):
            load_parts(sp, wbig[:, 0:SLOT], s_gate[L], s_up[L], s_down[L], sem[f"shared_in{L}"])

        def load_expert(sp, L, k, e):
            def one(w):
                return w[L, bass.ds(e, 1)].rearrange("a k n -> (a k) n")
            load_parts(sp, slot[k], one(e_gate), one(e_up), one(e_down), sem[f"slot_in{k}_{L}"])

        def refill_loop(sp, L):
            with sp.Fori(1, NE // NSLOT) as i:
                for k in range(NSLOT):
                    sp.wait_ge(sem[f"down_pe{L}"], i * (2 * NSLOT) + (2 * k + 4 - 2 * NSLOT))
                    load_expert(sp, L, k, i * NSLOT + k)

        @block.sync
        def _(sp):
            def rows(w, c):
                return w.rearrange("(p c) n -> p c n", c=c)

            sp.dma_start(cst[:, :], const).then_inc(sem["const_in"], 16)
            sp.dma_start(xrow, x[0].rearrange("(t p) d -> p t d", p=P)).then_inc(sem["x_in"], 16)
            w0 = rows(w_in0[0], KC)
            win0 = v(ring[:, 0:KC * IN0], c=KC, n=IN0)
            for c in range(KC):
                sp.dma_start(win0[:, c, :], w0[:, c, :]).then_inc(sem[f"win_in{c}"], 16)
            for i, (pe, w1, w2) in enumerate(((pe_k, ck1, ck2), (pe_v, cv1, cv2))):
                sp.dma_start(pen[0:CMP_LEN, i * HD:(i + 1) * HD], pe[0]).then_inc(sem["pe_in"], 16)
                for lh in range(2):
                    sp.dma_start(cw1[i][HD * lh:HD * lh + HD, :, :],
                                 w1[0, lh * 1024:lh * 1024 + 1024, :].rearrange("(l d) h -> d l h", d=HD))\
                      .then_inc(sem["cmpw_in"], 16)
                sp.dma_start(cw2[i], w2[0]).then_inc(sem["cmpw_in"], 16)
            sp.dma_start(sinkb, sinks.partition_broadcast(P)[:, 0, :]).then_inc(sem["small0_in"], 16)
            router_loads(sp, 0)
            norm_loads(sp, "ln_mix_in0", ln_mix_g, ln_mix_b, 0)
            sp.dma_start(wout, rows(w_out0[0], KC)).then_inc(sem["wout_in0"], 16)
            sp.wait_ge(sem["proj_pe0"], 8)
            sp.wait_ge(sem["gates_pe"], 1)
            for k in range(3):
                load_expert(sp, 0, k, k)
            sp.wait_ge(sem["out_pe0"], TC)
            load_shared(sp, 0)
            load_expert(sp, 0, 3, 3)
            sp.wait_ge(sem["lnmix_dve0"], TC)
            norm_loads(sp, "ln_ffn_in0", ln_ffn_g, ln_ffn_b, 0)
            refill_loop(sp, 0)
            sp.wait_ge(sem["down_pe0"], 2 * (NE - NSLOT + 0) + 4)
            sp.dma_start(uq, rows(w_uq[0], QL // P)).then_inc(sem["wuq_in"], 16)
            sp.wait_ge(sem["down_pe0"], 2 * (NE - NSLOT + 1) + 4)
            sp.dma_start(ukv, rows(w_ukv[0], KVL // P)).then_inc(sem["wukv_in"], 16)
            sp.wait_ge(sem["down_pe0"], 2 * (NE - NSLOT + 2) + 4)
            sp.dma_start(win1, rows(w_in1[0], KC)).then_inc(sem["win1_in"], 16)
            sp.dma_start(wout, rows(w_out1[0], KC)).then_inc(sem["wout_in1"], 16)
            sp.wait_ge(sem["gate_dve0"], 1)
            router_loads(sp, 1)
            sp.wait_ge(sem["lnffn_dve0"], TC)
            sp.dma_start(lnp[:, 0:QL], q_norm.partition_broadcast(P)[:, 0, :]).then_inc(sem["small1_in"], 16)
            sp.dma_start(lnp[:, QL:QL + KVL], kv_norm.partition_broadcast(P)[:, 0, :]).then_inc(sem["small1_in"], 16)
            sp.wait_ge(sem["rms_dve"], TC)
            norm_loads(sp, "ln_mix_in1", ln_mix_g, ln_mix_b, 1)
            sp.wait_ge(sem["q_pe"], 6)
            load_expert(sp, 1, 0, 0)
            sp.wait_ge(sem["kv_pe"], 8)
            load_expert(sp, 1, 1, 1)
            sp.wait_ge(sem["qk_pe1"], 16)
            load_expert(sp, 1, 2, 2)
            sp.wait_ge(sem["out_pe1"], TC)
            load_shared(sp, 1)
            load_expert(sp, 1, 3, 3)
            sp.wait_ge(sem["lnmix_dve1"], TC)
            norm_loads(sp, "ln_ffn_in1", ln_ffn_g, ln_ffn_b, 1)
            refill_loop(sp, 1)
            orows = out[0].rearrange("(t p) d -> p t d", p=P)
            for tc in range(TC):
                sp.wait_ge(sem["lnffn_dve1"], tc + 1)
                sp.dma_start(orows[:, tc, :], xrow[:, tc, :]).then_inc(sem["out_done"], 16)
            sp.wait_ge(sem["out_done"], 16 * TC)

        def pe_columns(pe, st):
            for b in range(4):
                for c in (2 * b, 2 * b + 1):
                    for tc in range(TC):
                        o = (c % 2) * S + tc * P
                        mm = pe.transpose(BANK[b][:, o:o + P], SRC[st][:, tc, c:c + (P - 1) * KC + 1:KC], ident)
                mm.then_inc(sem["xt_pe"], 1)

        def columns_ready(eng, st):
            eng.wait_ge(sem["xt_act"], 2 * st + 2)
            eng.wait_ge(sem["xt_dve"], 2 * st + 2)

        def pe_attention(pe, L):
            units = UNITS[L]
            n = len(units)
            for u in range(n + 2):
                if u < n:
                    U = units[u]
                    if u >= 2:
                        pe.wait_ge(sem[f"max_dve{L}"], 2 * (u - 1))
                    sc = v(PS[u % 2][:, 0:R * (U["qc"] + 1) * P], j=R, k=(U["qc"] + 1) * P)
                    for j in range(R):
                        mm = pe.matmul(sc[:, j, :], U["q"][j], U["k"][j], start=True, stop=True)
                    mm.then_inc(sem[f"score_pe{L}"], 1)
                if u >= 2:
                    U = units[u - 2]
                    pe.wait_ge(sem[f"ptr_act{L}"], u - 1)
                    if U["n"] // 2 >= 2:
                        pe.wait_ge(sem[f"o_dve{L}"], U["n"] // 2 - 1)
                    w = (U["qc"] + 1) * P
                    pt = v(PTBUF[L][:, 0:R * w], j=R, k=w)
                    ob = BANK[6 + U["n"] // 2 % 2]
                    for j in range(R):
                        o = (U["n"] % 2) * R * HD + j * HD
                        for c in range(U["qc"] + 1):
                            mm = pe.matmul(ob[:, o:o + HD], pt[:, j, c * P:(c + 1) * P], U["v"][c][j],
                                           start=c == 0, stop=c == U["qc"])
                    mm.then_inc(sem[f"pv_pe{L}"], 1)
                if 1 <= u <= n:
                    U = units[u - 1]
                    pe.wait_ge(sem[f"exp_act{L}"], u)
                    if u >= 2:
                        pe.wait_ge(sem[f"ptr_act{L}"], u - 1)
                    w = (U["qc"] + 1) * P
                    s = v(SBUFS[L][(u - 1) % 2][:, 0:R * w], j=R, k=w)
                    po = v(PS[2][:, 0:R * w], j=R, k=w)
                    for j in range(R):
                        for c in range(U["qc"] + 1):
                            mm = pe.transpose(po[:, j, c * P:(c + 1) * P], s[:, j, c * P:(c + 1) * P], ident)
                    mm.then_inc(sem[f"ptr_pe{L}"], 1)

        def pe_out(pe, L):
            pe.wait_ge(sem[f"wout_in{L}"], 16)
            columns_ready(pe, 1 + 3 * L)
            for tc in range(TC):
                for half in range(2):
                    for c in range(KC):
                        mm = pe.matmul(PS[2 + tc][:, half * 512:(half + 1) * 512], attot[L][:, c, tc * P:(tc + 1) * P],
                                       wout[:, c, half * 512:(half + 1) * 512], start=c == 0, stop=c == KC - 1)
                mm.then_inc(sem[f"out_pe{L}"], 1)

        def pe_logits(pe, L):
            columns_ready(pe, 2 + 3 * L)
            pe.wait_ge(sem[f"router_in{L}"], 32)
            r = v(rw[:, :], c=KC, e=NE)
            for tc in range(TC):
                for c in range(KC):
                    mm = pe.matmul(BANK[0][:, tc * NE:(tc + 1) * NE], xcol[:, c, tc * P:(tc + 1) * P], r[:, c, :],
                                   start=c == 0, stop=c == KC - 1)
            mm.then_inc(sem[f"logit_pe{L}"], 1)

        def pe_gate_up(pe, L, tc, w, free=None):
            if free is not None:
                pe.wait_ge(sem[f"h_dve{L}"], free)
            gu = expert(w)[0]
            for c in range(KC):
                mm = pe.matmul(v(BANK[tc], m=2, f=DE), xcol[:, c, tc * P:(tc + 1) * P], gu[:, c, :, :],
                               start=c == 0, stop=c == KC - 1)
            mm.then_inc(sem[f"gu_pe{L}"], 1)

        def pe_turn(pe, L, tc, ready, free=None):
            pe.wait_ge(sem[f"h_dve{L}"], ready)
            if free is not None:
                pe.wait_ge(sem[f"ht_act{L}"], free)
            for c in range(2):
                mm = pe.transpose(BANK[2 + tc][:, c * P:(c + 1) * P], hh[tc][:, c:c + 2 * P - 1:2], ident)
            mm.then_inc(sem[f"ht_pe{L}"], 1)

        def pe_down(pe, L, tc, w, ready, first=False, last=False, used=None):
            pe.wait_ge(sem[f"ht_act{L}"], ready)
            dn = expert(w)[1]
            for half in range(2):
                for c in range(2):
                    mm = pe.matmul(PS[2 + tc][:, half * 512:(half + 1) * 512], ht[tc][:, c, :],
                                   dn[:, c, half * 512:(half + 1) * 512],
                                   start=first and c == 0, stop=last and c == 1, skip_group_check=True)
            mm.then_inc(sem[f"down_pe{L}"], 1)
            return mm

        def pe_moe_steps(pe, L):
            sh = wbig[:, 0:SLOT]
            pe.wait_ge(sem[f"shared_in{L}"], 48)
            pe.wait_ge(sem[f"sig_act{L}"], 1)
            pe_gate_up(pe, L, 0, sh)
            pe_gate_up(pe, L, 1, sh)
            pe_turn(pe, L, 0, 1)

            def group(base, n, prev, first):
                for e in range(NSLOT):
                    before = slot[e - 1] if e else prev
                    pe.wait_ge(sem[f"slot_in{e}_{L}"], n * 48)
                    for tc in range(TC):
                        s = base + 2 * e + tc
                        pe_gate_up(pe, L, tc, slot[e], s - 1)
                        pe_turn(pe, L, 1 - tc, s, None if first and e == 0 and tc == 0 else s - 2)
                        pe_down(pe, L, tc, before, s - 1, first=first and e == 0)

            group(2, 1, sh, True)
            with pe.Fori(1, NE // NSLOT) as i:
                group(i * (2 * NSLOT) + 2, i + 1, slot[NSLOT - 1], False)
            s = 2 + 2 * NE
            pe_turn(pe, L, 1, s, s - 2)
            pe_down(pe, L, 0, slot[NSLOT - 1], s - 1, last=True)
            pe_down(pe, L, 1, slot[NSLOT - 1], s, last=True)

        @block.tensor
        def _(pe):
            pe.wait_ge(sem["const_in"], 16)
            pe.wait_ge(sem["x_in"], 16)
            pe_columns(pe, 0)
            columns_ready(pe, 0)
            win0 = v(ring[:, 0:KC * IN0], c=KC, n=IN0)
            for c in range(KC):
                pe.wait_ge(sem[f"win_in{c}"], 16)
                for b in range(8):
                    n, tc = b // 2, b % 2
                    mm = pe.matmul(BANK[b], xcol[:, c, tc * P:(tc + 1) * P], win0[:, c, n * 512:(n + 1) * 512],
                                   start=c == 0, stop=c == KC - 1)
                    if c == KC - 1:
                        mm.then_inc(sem["proj_pe0"], 1)
            pe.wait_ge(sem["proj_act0"], 1)
            for tc in range(TC):
                for c in range(KC):
                    mm = pe.matmul(BANK[0][:, tc * 32:tc * 32 + NGATE], xcol[:, c, tc * P:(tc + 1) * P],
                                   win0[:, c, C_GT:C_GT + NGATE], start=c == 0, stop=c == KC - 1)
            mm.then_inc(sem["gates_pe"], 1)
            pe.wait_ge(sem["proj_act0"], 4)
            pe.wait_ge(sem["proj_dve0"], 4)
            for i, c in enumerate((C_KC, C_VC)):
                for g in range(G):
                    for tc in range(TC):
                        o = g * S + tc * P
                        mm = pe.transpose(BANK[2 + i][0:HD, o:o + P], qkv[:, tc, c + g * HD:c + (g + 1) * HD], ident)
                mm.then_inc(sem["kcv_pe"], 1)
            pe.wait_ge(sem["pe_in"], 32)
            for i in range(2):
                mm = pe.transpose(BANK[1][0:HD, i * CMP_LEN:(i + 1) * CMP_LEN], pen[0:CMP_LEN, i * HD:(i + 1) * HD],
                                  ident[0:CMP_LEN, 0:CMP_LEN])
            mm.then_inc(sem["pet_pe"], 1)
            pe.wait_ge(sem["rope_dve0"], TC)
            for u in range(6):
                bank = BANK[(4, 5, 6, 7, 2, 3)[u]]
                if u >= 4:
                    pe.wait_ge(sem["kcv_act"], u - 3)
                for b in range(2 * u, min(2 * u + 2, NB)):
                    for tc in range(TC):
                        o = (b % 2) * S + tc * P
                        mm = pe.transpose(bank[:, o:o + P], rope[:, tc, b * P:(b + 1) * P], ident)
                mm.then_inc(sem["qk_pe0"], 1)
            pe.wait_ge(sem["cmpw_in"], 96)
            pe.wait_ge(sem["blk_dve"], 8)
            pe.wait_ge(sem["pet_act"], 1)
            for i in range(2):
                for l in range(16):
                    mm = pe.matmul(BANK[1][:, i * 32:i * 32 + G * NCMP], cw1[i][:, l, :],
                                   blk[i][:, l, :, :].rearrange("p g n -> p (g n)"), start=l == 0, stop=l == 15)
            mm.then_inc(sem["hid_pe"], 1)
            pe.wait_ge(sem["gelu_dve"], 1)
            for i in range(2):
                for g in range(G):
                    o = 128 + i * 128 + g * HD
                    mm = pe.matmul(BANK[1][0:NCMP, o:o + HD], hidw[5][:, i * 32 + g * NCMP:i * 32 + (g + 1) * NCMP],
                                   cw2[i], start=True, stop=True)
            mm.then_inc(sem["kv2_pe"], 1)
            pe.wait_ge(sem["kcn_dve"], 1)
            pe.transpose(BANK[0][:, 0:NCMP], kcn[0:NCMP, :], ident[0:NCMP, 0:NCMP]).then_inc(sem["kct_pe"], 1)
            pe.wait_ge(sem["kct_dve"], 1)
            pe.wait_ge(sem["qk_act0"], 6)
            for h in range(8):
                for tc in range(TC):
                    rows = slice(HD * (h // R), HD * (h // R) + HD)
                    o = tc * R * 16 + h % R * 16
                    mm = pe.matmul(BANK[(0, 5)[h // R]][:, o:o + NCMP], qkt[rows, 5 + h % R, tc * P:(tc + 1) * P],
                                   kcmpt[rows, :], start=True, stop=True)
            mm.then_inc(sem["csc_pe"], 1)
            pe.wait_ge(sem["cp_dve"], 1)
            for i in range(4):
                tc, g = i // 2, i % 2
                mm = pe.transpose(BANK[1][:, i * P:(i + 1) * P], cp[:, tc, g * R:(g + 1) * R, :], ident)
            mm.then_inc(sem["cpt_pe"], 1)
            pe.wait_ge(sem["cpt_act"], 1)
            pe.wait_ge(sem["vbd_dve"], 1)
            for tc in range(TC):
                for g in range(G):
                    mm = pe.matmul(BANK[4 + tc][:, g * 256:(g + 1) * 256], cpt[:, tc * 2 + g, :],
                                   vbd[g].rearrange("p j d -> p (j d)"), start=True, stop=True)
            mm.then_inc(sem["csc_pe"], 1)
            pe.wait_ge(sem["cmp_dve"], 1)
            pe_attention(pe, 0)
            pe.wait_ge(sem["o_dve0"], 6)
            pe_columns(pe, 1)
            pe_out(pe, 0)
            pe.wait_ge(sem["lnmix_dve0"], TC)
            pe_columns(pe, 2)
            pe_logits(pe, 0)
            pe_moe_steps(pe, 0)
            pe.wait_ge(sem["lnffn_dve0"], TC)
            pe_columns(pe, 3)
            columns_ready(pe, 3)
            pe.wait_ge(sem["win1_in"], 16)
            for tc in range(TC):
                for n, w in ((0, 512), (512, IN1 - 512)):
                    for c in range(KC):
                        mm = pe.matmul(PS[2 + tc][:, n:n + w], xcol[:, c, tc * P:(tc + 1) * P], win1[:, c, n:n + w],
                                       start=c == 0, stop=c == KC - 1)
                mm.then_inc(sem["proj_pe1"], 1)
            pe.wait_ge(sem["rms_dve"], TC)
            for c in range(5):
                for tc in range(TC):
                    o = (c % 2) * S + tc * P
                    if c < 3:
                        src = c1[:, tc, c:c + 3 * P - 2:3]
                    else:
                        src = c1[:, tc, QL + c - 3:QL + c - 3 + 2 * P - 1:2]
                    mm = pe.transpose(BANK[c // 2][:, o:o + P], src, ident)
                if c % 2 or c == 4:
                    mm.then_inc(sem["cnt_pe"], 1)
            pe.wait_ge(sem["krope_dve"], TC)
            for tc in range(TC):
                mm = pe.transpose(BANK[3][0:ROPE, tc * P:(tc + 1) * P], c1[:, tc, QL + KVL:IN1], ident)
            mm.then_inc(sem["krt_pe"], 1)
            pe.wait_ge(sem["cnt_act"], 3)
            pe.wait_ge(sem["krt_act"], 1)
            pe.wait_ge(sem["wuq_in"], 16)
            for i in range(6):
                tc, n = i // 3, i % 3
                for c in range(3):
                    mm = pe.matmul(BANK[i], ct1[:, c, tc * P:(tc + 1) * P], uq[:, c, n * 512:(n + 1) * 512],
                                   start=c == 0, stop=c == 2)
                mm.then_inc(sem["q_pe"], 1)
            pe.wait_ge(sem["wukv_in"], 16)
            for i in range(8):
                tc, n = i // 4, i % 4
                b = (i + 6) % 8
                if i >= 2:
                    pe.wait_ge(sem["q_act"], i - 1)
                for c in range(2):
                    mm = pe.matmul(BANK[b], ct1[:, 3 + c, tc * P:(tc + 1) * P], ukv[:, c, n * 512:(n + 1) * 512],
                                   start=c == 0, stop=c == 1)
                mm.then_inc(sem["kv_pe"], 1)
            pe.wait_ge(sem["kv_act"], 8)
            pe.wait_ge(sem["qrope_dve"], TC)
            for u in range(16):
                if u >= 4:
                    pe.wait_ge(sem["qk_act1"], u - 3)
                hs = [u // 2 * 2, u // 2 * 2 + 1]
                hs = [2 * (u % 8), 2 * (u % 8) + 1]
                for i, h in enumerate(hs):
                    for tc in range(TC):
                        o = i * S + tc * P
                        if u < 8:
                            mm = pe.transpose(BANK[u % 4][0:NOPE, o:o + P], kv1[:, tc, h * 128:h * 128 + NOPE], ident)
                        else:
                            mm = pe.transpose(BANK[u % 4][0:DQK, o:o + P], qn1[:, tc, h * DQK:(h + 1) * DQK], ident)
                mm.then_inc(sem["qk_pe1"], 1)
            pe.wait_ge(sem["qk_act1"], 16)
            pe.wait_ge(sem["kfull_act"], 1)
            pe_attention(pe, 1)
            pe.wait_ge(sem["o_dve1"], 4)
            pe_columns(pe, 4)
            pe_out(pe, 1)
            pe.wait_ge(sem["lnmix_dve1"], TC)
            pe_columns(pe, 5)
            pe_logits(pe, 1)
            pe_moe_steps(pe, 1)

        def act_columns(act, st):
            for b in (0, 2):
                act.wait_ge(sem["xt_pe"], 4 * st + b + 1)
                nc.scalar.copy(DST[st][:, 2 * b:2 * b + 2, :], v(BANK[b], c=2, t=S)).then_inc(sem["xt_act"], 1)

        def act_attention(act, L):
            units = UNITS[L]
            n = len(units)
            for u in range(n + 1):
                if u < n:
                    U = units[u]
                    w = (U["qc"] + 1) * P
                    s = v(SBUFS[L][u % 2][:, 0:R * w], j=R, k=w)
                    act.wait_ge(sem[f"max_dve{L}"], 2 * u + 2)
                    for j in range(R):
                        i = u * R + j
                        ins = nc.scalar.activation(s[:, j, :], s[:, j, :], ACT.Exp, bias=nmax[:, i:i + 1],
                                                   accum_out=sums[:, i:i + 1])
                    ins.then_inc(sem[f"exp_act{L}"], 1)
                    if U["sink"] and u == 3:
                        act.wait_ge(sem["sink_dve"], 5)
                        nc.scalar.activation(esink, esink, ACT.Exp).then_inc(sem["sink_act"], 1)
                if u >= 1:
                    U = units[u - 1]
                    w = (U["qc"] + 1) * P
                    act.wait_ge(sem[f"ptr_pe{L}"], u)
                    if u >= 2:
                        act.wait_ge(sem[f"pv_pe{L}"], u - 1)
                    nc.scalar.copy(PTBUF[L][:, 0:R * w], PS[2][:, 0:R * w]).then_inc(sem[f"ptr_act{L}"], 1)

        def act_logits(act, L):
            act.wait_ge(sem[f"logit_pe{L}"], 1)
            nc.scalar.activation(rs, v(BANK[0][:, 0:TC * NE], t=TC, e=NE), ACT.Exp, scale=-1.0).then_inc(sem[f"sig_act{L}"], 1)

        def act_moe(act, L):
            def silu(s, tc, free=None):
                act.wait_ge(sem[f"gu_pe{L}"], s + 1)
                if free is not None:
                    act.wait_ge(sem[f"h_dve{L}"], free)
                nc.scalar.activation(sg[tc], BANK[tc][:, 0:DE], ACT.Silu).then_inc(sem[f"silu_act{L}"], 1)

            def turn(s, tc, free=None):
                act.wait_ge(sem[f"ht_pe{L}"], s + 1)
                if free is not None:
                    act.wait_ge(sem[f"down_pe{L}"], free)
                nc.scalar.copy(ht[tc], v(BANK[2 + tc][:, 0:2 * P], c=2, t=P)).then_inc(sem[f"ht_act{L}"], 1)

            silu(0, 0)
            silu(1, 1)
            turn(0, 0)

            def group(base, first):
                for e in range(NSLOT):
                    for tc in range(TC):
                        s = base + 2 * e + tc
                        silu(s, tc, s - 1)
                        turn(s - 1, 1 - tc, None if first and e == 0 and tc == 0 else s - 2)

            group(2, True)
            with act.Fori(1, NE // NSLOT) as i:
                group(i * (2 * NSLOT) + 2, False)
            turn(1 + 2 * NE, 1, 2 * NE)

        @block.scalar
        def _(act):
            act_columns(act, 0)
            for i in range(4):
                act.wait_ge(sem["proj_pe0"], 2 * i + 1)
                nc.scalar.copy(qkv[:, 0, i * 512:(i + 1) * 512], BANK[2 * i]).then_inc(sem["proj_act0"], 1)
            act.wait_ge(sem["gates_pe"], 1)
            nc.scalar.activation(v(gates, t=TC, n=NGATE), v(BANK[0][:, 0:64], t=TC, n=32)[:, :, 0:NGATE], ACT.Exp, scale=-1.0)\
                .then_inc(sem["gates_act"], 1)
            for i in range(2):
                act.wait_ge(sem["kcv_pe"], i + 1)
                nc.scalar.copy(kcv[0:HD, 2 * i:2 * i + 2, :], v(BANK[2 + i][0:HD, :], g=G, t=S)).then_inc(sem["kcv_act"], 1)
            act.wait_ge(sem["pet_pe"], 1)
            nc.scalar.copy(pet[0:HD, :, :], v(BANK[1][0:HD, 0:2 * CMP_LEN], k=2, l=CMP_LEN)).then_inc(sem["pet_act"], 1)
            for u in range(6):
                act.wait_ge(sem["qk_pe0"], u + 1)
                bank = BANK[(4, 5, 6, 7, 2, 3)[u]]
                w = min(2, NB - 2 * u)
                nc.scalar.copy(qkt[:, 2 * u:2 * u + w, :], v(bank[:, 0:w * S], b=w, t=S)).then_inc(sem["qk_act0"], 1)
            act.wait_ge(sem["hid_pe"], 1)
            hv = [v(h, k=2, n=32)[:, :, 0:G * NCMP] for h in hidw]
            nc.scalar.copy(hv[0], v(BANK[1][:, 0:64], k=2, n=32)[:, :, 0:G * NCMP]).then_inc(sem["hid_act"], 1)
            act.wait_ge(sem["gin_dve"], 1)
            nc.scalar.activation(hv[3], hv[2], ACT.Exp, scale=-GELU_C).then_inc(sem["gexp_act"], 1)
            act.wait_ge(sem["csub_dve"], 1)
            nc.scalar.activation(cs[:, :, :, 0:NCMP], cs[:, :, :, 0:NCMP], ACT.Exp).then_inc(sem["cexp_act"], 1)
            act.wait_ge(sem["cpt_pe"], 1)
            nc.scalar.copy(cpt, v(BANK[1], u=4, q=P)).then_inc(sem["cpt_act"], 1)
            act_attention(act, 0)
            act_columns(act, 1)
            act_columns(act, 2)
            act_logits(act, 0)
            act_moe(act, 0)
            act_columns(act, 3)
            for tc in range(TC):
                act.wait_ge(sem["proj_pe1"], tc + 1)
                nc.scalar.copy(c1[:, tc, :], PS[2 + tc][:, 0:IN1]).then_inc(sem["proj_act1"], 1)
            for i in range(3):
                act.wait_ge(sem["cnt_pe"], i + 1)
                w = 2 if i < 2 else 1
                nc.scalar.copy(ct1[:, 2 * i:2 * i + w, :], v(BANK[i][:, 0:w * S], c=w, t=S)).then_inc(sem["cnt_act"], 1)
            act.wait_ge(sem["krt_pe"], 1)
            nc.scalar.copy(krt, BANK[3][0:ROPE, 0:S]).then_inc(sem["krt_act"], 1)
            for i in range(6):
                act.wait_ge(sem["q_pe"], i + 1)
                nc.scalar.copy(qn1[:, i // 3, i % 3 * 512:(i % 3 + 1) * 512], BANK[i]).then_inc(sem["q_act"], 1)
            for i in range(8):
                act.wait_ge(sem["kv_pe"], i + 1)
                nc.scalar.copy(kv1[:, i // 4, i % 4 * 512:(i % 4 + 1) * 512], BANK[(i + 6) % 8]).then_inc(sem["kv_act"], 1)
            for u in range(16):
                act.wait_ge(sem["qk_pe1"], u + 1)
                h = 2 * (u % 8)
                if u < 8:
                    nc.scalar.copy(kt1[0:NOPE, h:h + 2, :], v(BANK[u % 4][0:NOPE, :], h=2, t=S)).then_inc(sem["qk_act1"], 1)
                else:
                    nc.scalar.copy(qt1[0:DQK, h:h + 2, :], v(BANK[u % 4][0:DQK, :], h=2, t=S)).then_inc(sem["qk_act1"], 1)
            act_attention(act, 1)
            act_columns(act, 4)
            act_columns(act, 5)
            act_logits(act, 1)
            act_moe(act, 1)

        @block.gpsimd
        def _(pool):
            pool.memset(power, -0.5).then_inc(sem["power_pool"], 1)
            pool.wait_ge(sem["hid_pe"], 1)
            pool.memset(last[:, 0:512], 0.0).then_inc(sem["zero_pool"], 1)
            pool.memset(last[:, 768:768 + 512], 0.0).then_inc(sem["zero_pool"], 1)
            pool.wait_ge(sem["power_pool"], 1)
            for i, n in enumerate([1, 1, 1, 1, 2, 2, 1, 1, 1, 1]):
                pool.wait_ge(sem["var_dve"], i + 1)
                pool.tensor_tensor(root[:, 0:n], var[:, 0:n], power[:, 0:n], ALU.pow).then_inc(sem["root_pool"], 1)

        @block.vector
        def _(dve):
            chain = [0]

            def link(ins):
                chain[0] += 1
                ins.then_inc(sem["dve_chain"], 1)
                dve.wait_ge(sem["dve_chain"], chain[0])

            marks = {}

            def mark(ins, name):
                ins.then_inc(sem[name], 1)
                marks[name] = marks.get(name, 0) + 1

            def settle(name):
                dve.wait_ge(sem[name], marks[name])

            V = nc.vector

            def columns(st):
                for b in (1, 3):
                    dve.wait_ge(sem["xt_pe"], 4 * st + b + 1)
                    mark(V.tensor_copy(DST[st][:, 2 * b:2 * b + 2, :], v(BANK[b], c=2, t=S)), "xt_dve")

            def bc(ap, shape):
                return ap.to_broadcast(shape)

            def apply_rope(src, dsts, cos, sin, heads, half, done=None):
                d = 2 * half
                n = heads * d
                t = v(tmp[:, 0:n], h=heads, d=d)
                u = v(tmp[:, 640:640 + n], h=heads, d=d)
                pr = src.shape[0]
                t, u = t[0:pr], u[0:pr]
                cb = cos[:, None, :].to_broadcast([pr, heads, d])
                sbc = sin[:, None, :].to_broadcast([pr, heads, d])
                V.tensor_tensor(t, src, cb, ALU.mult)
                link(V.tensor_tensor(u, src, sbc, ALU.mult))
                ins = None
                for a, b, (o1, o2), view in dsts:
                    V.tensor_tensor(o1, view(t[:, a:b, 0:half]), view(u[:, a:b, half:d]), ALU.subtract)
                    ins = V.tensor_tensor(o2, view(t[:, a:b, half:d]), view(u[:, a:b, 0:half]), ALU.add)
                    if b < heads or done is None:
                        link(ins)
                if done is not None:
                    mark(ins, done)
                    settle(done)

            roots = [0]

            def inverse_root(issue):
                roots[0] += 1
                mark(issue(), "var_dve")
                dve.wait_ge(sem["root_pool"], roots[0])

            def layer_norm(L, part, st):
                dve.wait_ge(sem[f"ln_{part}_in{L}"], 32)
                for tc in range(TC):
                    if part == "mix":
                        dve.wait_ge(sem[f"out_pe{L}"], tc + 1)
                    else:
                        dve.wait_ge(sem[f"down_pe{L}"], 2 + 2 * NE)
                    r = xrow[:, tc, :]
                    link(V.scalar_tensor_tensor(r, r, ALPHA, PS[2 + tc][:, :], ALU.mult, ALU.add))
                    V.bn_stats(stats[:, 0:6], r[:, 0:512])
                    link(V.bn_stats(stats[:, 6:12], r[:, 512:1024]))
                    link(V.bn_aggr(mv, stats))
                    inverse_root(lambda: V.tensor_scalar(var[:, 0:1], mv[:, 1:2], LN_EPS, None, ALU.add))
                    link(V.tensor_scalar(r, r, mv[:, 0:1], root[:, 0:1], ALU.subtract, ALU.mult))
                    link(V.tensor_tensor(r, r, lng, ALU.mult))
                    mark(V.tensor_tensor(r, r, lnb, ALU.add), f"ln{part}_dve{L}")

            def attention(L):
                units = UNITS[L]
                n = len(units)
                for u in range(n + 4):
                    if u < n:
                        U = units[u]
                        w = (U["qc"] + 1) * P
                        s = v(SBUFS[L][u % 2][:, 0:R * w], j=R, k=w)
                        sc = v(PS[u % 2][:, 0:R * w], j=R, k=w)
                        mask = cst[:, U["mask"] + 2 * P - w:U["mask"] + 2 * P]
                        dve.wait_ge(sem[f"score_pe{L}"], u + 1)
                        if u >= 2:
                            dve.wait_ge(sem[f"ptr_pe{L}"], u - 1)
                        ins = V.scalar_tensor_tensor(s, sc, U["scale"], mask[:, None, :].to_broadcast([P, R, w]),
                                                     ALU.mult, ALU.add)
                        mark(ins, f"max_dve{L}")
                        dve.wait_ge(sem[f"max_dve{L}"], 2 * u + 1)
                        m = nmax[:, u * R:(u + 1) * R]
                        ins = V.tensor_reduce(m, s, AX_X, ALU.max, negate=True)
                        if U["sink"]:
                            link(ins)
                            sk = nsink[:, u % 2 * R:(u % 2 + 1) * R]
                            ins = V.tensor_tensor(m, m, sk, ALU.min)
                            mark(ins, f"max_dve{L}")
                            dve.wait_ge(sem[f"max_dve{L}"], 2 * u + 2)
                            mark(V.tensor_tensor(esink[:, u * R:(u + 1) * R], m, sk, ALU.subtract), "sink_dve")
                        else:
                            mark(ins, f"max_dve{L}")
                    if u >= 4 and u % 2 == 0 or u == n + 3:
                        pair = (u - 4) // 2 if u < n + 3 else n // 2 - 1
                        if u >= n + 3 or u < n + 3:
                            output(L, pair) if pair not in done[L] else None
                            done[L].add(pair)

            done = [set(), set()]

            def output(L, pair):
                dve.wait_ge(sem[f"pv_pe{L}"], 2 * pair + 2)
                ob = v(BANK[6 + pair % 2], h=8, d=HD)
                s8 = sums[:, pair * 8:pair * 8 + 8]
                r8 = rec[:, pair % 2 * 8:pair % 2 * 8 + 8]
                if L:
                    qc, part = pair // 2, pair % 2 * 512
                else:
                    qc, part = pair % 2, 0 if pair < 2 else 512
                if L == 0 and pair < 2:
                    dve.wait_ge(sem["sink_act"], 1)
                    link(V.tensor_tensor(s8, s8, esink[:, pair * 8:pair * 8 + 8], ALU.add))
                link(V.reciprocal(r8, s8))
                if L == 0 and pair >= 2:
                    gt = gates[:, qc * NGATE + 8 * (pair // 2):qc * NGATE + 8 * (pair // 2) + 8]
                    link(V.tensor_tensor(r8, r8, gt, ALU.mult))
                dst = v(atto[L][:, qc, part:part + 512], h=8, d=HD)
                rb = r8[:, :, None].to_broadcast([P, 8, HD])
                if L == 0 and pair >= 2:
                    o = v(tmp[:, 0:512], h=8, d=HD)
                    link(V.tensor_tensor(o, ob, rb, ALU.mult))
                    mark(V.tensor_tensor(dst, dst, o, ALU.add), f"o_dve{L}")
                    dve.wait_ge(sem[f"o_dve{L}"], pair + 1)
                else:
                    mark(V.tensor_tensor(dst, ob, rb, ALU.mult), f"o_dve{L}")

            def routing(L):
                dve.wait_ge(sem[f"sig_act{L}"], 1)
                dve.wait_ge(sem[f"router_in{L}"], 32)
                link(V.tensor_scalar(rs, rs, 1.0, None, ALU.add))
                link(V.reciprocal(rs, rs))
                link(V.tensor_tensor(rsb, rs, rbias[:, None, :].to_broadcast([P, TC, NE]), ALU.add))
                for tc in range(TC):
                    for g in range(NG):
                        ins = V.max(top8[:, tc, g, :], rsb[:, tc, g * EPG:(g + 1) * EPG])
                V.memset(esc[:, :, NE:], LOWEST)
                V.memset(gsc[:, :, NG:], LOWEST)
                link(ins)
                link(V.tensor_tensor(gsc[:, :, 0:NG], top8[:, :, :, 0], top8[:, :, :, 1], ALU.add))
                for tc in range(TC):
                    ins = V.max(m8[:, tc, :], gsc[:, tc, 0:NG])
                link(ins)
                link(V.memset(m8[:, :, TOPG:], LOWEST))
                for tc in range(TC):
                    ins = V.match_replace(gpick[:, tc, :], m8[:, tc, :], gsc[:, tc, :], PICKED)
                link(ins)
                link(V.tensor_scalar(gsel, gpick[:, :, 0:NG], PICKED / 2, None, ALU.is_ge))
                link(V.tensor_scalar(gneg, gsel, 1.0, -NEG, ALU.subtract, ALU.mult))
                for tc in range(TC):
                    e3 = v(esc[:, tc, 0:NE], g=NG, k=EPG)
                    V.tensor_tensor(e3, v(rsb[:, tc, :], g=NG, k=EPG), gsel[:, tc, :, None].to_broadcast([P, NG, EPG]), ALU.mult).then_inc(sem["dve_chain"], 1)
                    chain[0] += 1
                dve.wait_ge(sem["dve_chain"], chain[0])
                for tc in range(TC):
                    e3 = v(esc[:, tc, 0:NE], g=NG, k=EPG)
                    ins = V.tensor_tensor(e3, e3, gneg[:, tc, :, None].to_broadcast([P, NG, EPG]), ALU.add)
                link(ins)
                for tc in range(TC):
                    ins = V.max(m8[:, tc, :], esc[:, tc, 0:NE])
                link(ins)
                link(V.memset(m8[:, :, TOPK:], LOWEST))
                for tc in range(TC):
                    ins = V.match_replace(epick[:, tc, :], m8[:, tc, :], esc[:, tc, :], PICKED)
                link(ins)
                link(V.tensor_scalar(gate, epick[:, :, 0:NE], PICKED / 2, None, ALU.is_ge))
                link(V.tensor_tensor(gate, gate, rs, ALU.mult))
                link(V.tensor_reduce(gsum, gate, AX_X, ALU.add))
                link(V.reciprocal(gsum, gsum))
                for tc in range(TC):
                    ins = V.tensor_scalar(gate[:, tc, :], gate[:, tc, :], gsum[:, tc:tc + 1], ROUTED_SCALE, ALU.mult, ALU.mult)
                mark(ins, f"gate_dve{L}")
                dve.wait_ge(sem[f"gate_dve{L}"], 1)

            def moe(L):
                def hidden(s, tc, e=None, free=None):
                    dve.wait_ge(sem[f"silu_act{L}"], s + 1)
                    if free is not None:
                        dve.wait_ge(sem[f"ht_pe{L}"], free)
                    up = BANK[tc][:, DE:2 * DE]
                    if e is None:
                        ins = V.tensor_tensor(hh[tc], sg[tc], up, ALU.mult)
                    else:
                        ins = V.scalar_tensor_tensor(hh[tc], sg[tc], gate[:, tc, bass.ds(e, 1)], up, ALU.mult, ALU.mult)
                    mark(ins, f"h_dve{L}")

                hidden(0, 0)
                hidden(1, 1)
                with dve.Fori(0, NE) as e:
                    for tc in range(TC):
                        s = e * 2 + 2 + tc
                        hidden(s, tc, e, s - 1)

            dve.wait_ge(sem["small0_in"], 16)
            mark(V.tensor_scalar(nsink, sinkb, -1.0, None, ALU.mult), "sink_dve")
            columns(0)
            for i in range(4):
                dve.wait_ge(sem["proj_pe0"], 2 * i + 2)
                mark(V.tensor_copy(qkv[:, 1, i * 512:(i + 1) * 512], BANK[2 * i + 1]), "proj_dve0")
            dve.wait_ge(sem["proj_act0"], 4)
            dve.wait_ge(sem["proj_dve0"], 4)
            same = lambda a: a
            by_group = lambda a: a.rearrange("p (g j) d -> p g j d", g=G)
            for tc in range(TC):
                cos = cst[:, K_COS + tc * HD:K_COS + (tc + 1) * HD]
                sin = cst[:, K_SIN + tc * HD:K_SIN + (tc + 1) * HD]

                def out_q(b):
                    o = rope[:, tc, b * P:(b + R) * P].rearrange("p (j g d) -> p g j d", j=R, g=G)
                    return o[:, :, :, 0:HALF], o[:, :, :, HALF:HD]

                def out_k(b):
                    o = v(rope[:, tc, b * P:(b + 1) * P], g=G, d=HD)
                    return o[:, :, 0:HALF], o[:, :, HALF:HD]

                apply_rope(v(qkv[:, tc, C_QA:C_VA], h=10, d=HD),
                           [(0, 8, out_q(0), by_group), (8, 10, out_k(4), same)], cos, sin, 10, HALF)
                apply_rope(v(qkv[:, tc, C_QB:C_KC], h=8, d=HD), [(0, 8, out_q(5), by_group)], cos, sin, 8, HALF)
                apply_rope(v(qkv[:, tc, C_KS:C_VS], h=2, d=HD), [(0, 2, out_k(9), same)], cos, sin, 2, HALF)
                apply_rope(v(qkv[:, tc, C_KW:C_VW], h=2, d=HD), [(0, 2, out_k(10), same)], cos, sin, 2, HALF,
                           "rope_dve0")
            dve.wait_ge(sem["gates_act"], 1)
            link(V.tensor_scalar(gates, gates, 1.0, None, ALU.add))
            mark(V.reciprocal(gates, gates), "gates_dve")
            dve.wait_ge(sem["kcv_act"], 2)
            dve.wait_ge(sem["pet_act"], 1)
            for i in range(2):
                for lh in range(2):
                    for g in range(G):
                        src = kcv[0:HD, 2 * i + g, lh * 16:lh * 16 + NCMP * CMP_STRIDE]\
                            .rearrange("p (n l) -> p l n", l=CMP_STRIDE)
                        pos = pet[0:HD, i, lh * 16:(lh + 1) * 16]
                        mark(V.tensor_tensor(blk[i][HD * lh:HD * lh + HD, :, g, :], src,
                                             pos[:, :, None].to_broadcast([HD, 16, NCMP]), ALU.add), "blk_dve")
            hv = [v(h, k=2, n=32)[:, :, 0:G * NCMP] for h in hidw]
            dve.wait_ge(sem["hid_act"], 1)
            link(V.tensor_tensor(hv[1], hv[0], hv[0], ALU.mult))
            link(V.tensor_scalar(hv[1], hv[1], 0.044715, 1.0, ALU.mult, ALU.add))
            mark(V.tensor_tensor(hv[2], hv[1], hv[0], ALU.mult), "gin_dve")
            dve.wait_ge(sem["gexp_act"], 1)
            link(V.tensor_scalar(hv[4], hv[3], 1.0, None, ALU.add))
            link(V.reciprocal(hv[4], hv[4]))
            mark(V.tensor_tensor(hv[5], hv[0], hv[4], ALU.mult), "gelu_dve")
            dve.wait_ge(sem["kv2_pe"], 1)
            dve.wait_ge(sem["zero_pool"], 2)
            cos, sin = cst[0:NCMP, K_CCOS:K_CCOS + HD], cst[0:NCMP, K_CSIN:K_CSIN + HD]
            ck = v(kcn[0:NCMP, :], g=G, d=HD)
            apply_rope(v(BANK[1][0:NCMP, 128:256], g=G, d=HD),
                       [(0, 2, (ck[:, :, 0:HALF], ck[:, :, HALF:HD]), same)], cos, sin, 2, HALF, "kcn_dve")
            for g in range(G):
                for j in range(R):
                    ins = V.tensor_copy(vbd[g][32 * j:32 * j + NCMP, j, :], BANK[1][0:NCMP, 256 + g * HD:256 + (g + 1) * HD])
            mark(ins, "vbd_dve")
            dve.wait_ge(sem["kct_pe"], 1)
            mark(V.tensor_copy(kcmpt, BANK[0][:, 0:NCMP]), "kct_dve")
            dve.wait_ge(sem["csc_pe"], 1)
            c8 = cs[:, :, :, 0:NCMP]
            for tc in range(TC):
                add = cst[:, K_CADD + tc * NCMP:K_CADD + (tc + 1) * NCMP]
                for g in range(G):
                    sc = v(BANK[(0, 5)[g]][:, 0:128], t=TC, j=R, n=16)
                    ins = V.scalar_tensor_tensor(c8[:, tc, g * R:(g + 1) * R, :], sc[:, tc, :, 0:NCMP], HD ** -0.5,
                                                 add[:, None, :].to_broadcast([P, R, NCMP]), ALU.mult, ALU.add)
            link(ins)
            cm = v(crec, t=TC, h=8)
            link(V.tensor_reduce(cm, c8, AX_X, ALU.max))
            mark(V.tensor_tensor(c8, c8, cm[:, :, :, None].to_broadcast([P, TC, 8, NCMP]), ALU.subtract), "csub_dve")
            dve.wait_ge(sem["cexp_act"], 1)
            for tc in range(TC):
                mul = cst[:, K_CMUL + tc * NCMP:K_CMUL + (tc + 1) * NCMP]
                ins = V.tensor_tensor(cp[:, tc, :, 0:NCMP], c8[:, tc], mul[:, None, :].to_broadcast([P, 8, NCMP]), ALU.mult)
            mark(ins, "cp_dve")
            dve.wait_ge(sem["cp_dve"], 1)
            link(V.tensor_reduce(cm, cp[:, :, :, 0:NCMP], AX_X, ALU.add))
            link(V.tensor_scalar(crec, crec, 1e-30, None, ALU.max))
            link(V.reciprocal(crec, crec))
            link(V.tensor_tensor(cm, cm, v(gates, t=TC, n=NGATE)[:, :, 0:8], ALU.mult))
            dve.wait_ge(sem["csc_pe"], 2)
            for tc in range(TC):
                ins = V.tensor_tensor(v(atto[0][:, tc, 512:1024], h=8, d=HD), v(BANK[4 + tc], h=8, d=HD),
                                      cm[:, tc, :, None].to_broadcast([P, 8, HD]), ALU.mult)
            mark(ins, "cmp_dve")
            settle("cmp_dve")
            attention(0)
            columns(1)
            layer_norm(0, "mix", 2)
            columns(2)
            routing(0)
            moe(0)
            layer_norm(0, "ffn", 3)
            columns(3)
            dve.wait_ge(sem["small1_in"], 32)
            for tc in range(TC):
                dve.wait_ge(sem["proj_act1"], tc + 1)
                parts = ((0, QL), (QL, QL + KVL))
                link(V.tensor_tensor(tmp[:, 0:QL + KVL], c1[:, tc, 0:QL + KVL], c1[:, tc, 0:QL + KVL], ALU.mult))
                for i, (a, b) in enumerate(parts):
                    link(V.tensor_reduce(ssq[:, i:i + 1], tmp[:, a:b], AX_X, ALU.add))
                a, b = parts[0]
                link(V.tensor_scalar(var[:, 0:1], ssq[:, 0:1], 1.0 / (b - a), RMS_EPS, ALU.mult, ALU.add))
                a, b = parts[1]
                inverse_root(lambda: V.tensor_scalar(var[:, 1:2], ssq[:, 1:2], 1.0 / (b - a), RMS_EPS, ALU.mult, ALU.add))
                for i, (a, b) in enumerate(parts):
                    r = c1[:, tc, a:b]
                    link(V.tensor_scalar(r, r, root[:, i:i + 1], None, ALU.mult))
                    ins = V.tensor_tensor(r, r, lnp[:, a:b], ALU.mult)
                mark(ins, "rms_dve")
            for tc in range(TC):
                cos = cst[:, K_COS1 + tc * ROPE:K_COS1 + (tc + 1) * ROPE]
                sin = cst[:, K_SIN1 + tc * ROPE:K_SIN1 + (tc + 1) * ROPE]
                o = v(c1[:, tc, QL + KVL:IN1], h=1, d=ROPE)
                apply_rope(o, [(0, 1, (o[:, :, 0:16], o[:, :, 16:32]), same)], cos, sin, 1, 16, "krope_dve")
            dve.wait_ge(sem["krt_act"], 1)
            mark(V.tensor_copy(kt1[NOPE:DQK, :, :], krt[:, None, :].to_broadcast([ROPE, MH, S])), "kfull_act")
            for tc in range(TC):
                dve.wait_ge(sem["q_act"], 3 * tc + 3)
                cos = cst[:, K_COS1 + tc * ROPE:K_COS1 + (tc + 1) * ROPE]
                sin = cst[:, K_SIN1 + tc * ROPE:K_SIN1 + (tc + 1) * ROPE]
                o = v(qn1[:, tc, :], h=MH, d=DQK)[:, :, NOPE:DQK]
                apply_rope(o, [(0, MH, (o[:, :, 0:16], o[:, :, 16:32]), same)], cos, sin, MH, 16, "qrope_dve")
            attention(1)
            columns(4)
            layer_norm(1, "mix", 5)
            columns(5)
            routing(1)
            moe(1)
            layer_norm(1, "ffn", 6)


_INS = ['x', 'swa_nsa_w_in', 'swa_sinks', 'nsa_cmp_pe_k', 'nsa_cmp_k_w1', 'nsa_cmp_k_w2', 'nsa_cmp_pe_v',
        'nsa_cmp_v_w1', 'nsa_cmp_v_w2', 'swa_nsa_w_out', 'mla_w_in', 'mla_q_norm', 'mla_kv_norm', 'mla_w_uq',
        'mla_w_ukv', 'mla_w_out', 'ln_mix_g', 'ln_mix_b', 'ln_ffn_g', 'ln_ffn_b', 'router_w', 'router_bias',
        'expert_w_gate', 'expert_w_up', 'expert_w_down', 'shared_w_gate', 'shared_w_up', 'shared_w_down']


def kernel(**inputs):
    import concourse.bacc as bacc
    from concourse.bass_utils import run_bass_kernel_spmd

    nc = bacc.Bacc("TRN2", target_bir_lowering=False, num_devices=1)
    arrays, args = {}, []
    for name in _INS + ["constants"]:
        a = constants() if name == "constants" else np.ascontiguousarray(inputs[name])
        arrays[f"in_{name}"] = a
        args.append(nc.dram_tensor(f"in_{name}", a.shape, mybir.dt.from_np(a.dtype), kind="ExternalInput").ap())
    out = nc.dram_tensor("out_0", (1, S, D), F32, kind="ExternalOutput").ap()
    bass_hybrid_block(nc, *args, out)
    r = run_bass_kernel_spmd(nc, [arrays], core_ids=[0])
    return r.results[0]["out_0"]
```

```python
from contextlib import ExitStack

import numpy as np

import concourse.bass as bass
from concourse import mybir

F32 = mybir.dt.float32
F32R = mybir.dt.float32r
U32 = mybir.dt.uint32
ALU = mybir.AluOpType
ACT = mybir.ActivationFunctionType
AX_X = mybir.AxisListType.X

P = 128
S, D = 256, 1024
TC = S // P
KC = D // P
HD, HALF = 64, 32
G, R = 2, 4
MIX0 = (512, 128, 128, 512, 128, 128, 128, 128, 128, 128, 24)
COL = [int(c) for c in np.cumsum((0,) + MIX0)]
(C_QA, C_KA, C_VA, C_QB, C_KC, C_VC, C_KS, C_VS, C_KW, C_VW, C_GT) = COL[:11]
IN0 = COL[11]
NGATE = MIX0[10]
CMP_LEN, CMP_STRIDE, CMP_HID = 32, 16, 128
NCMP = (S - CMP_LEN) // CMP_STRIDE + 1
WINDOW = 128
MH, NOPE, ROPE, MV = 16, 64, 32, 64
DQK = NOPE + ROPE
QL, KVL = 384, 256
IN1 = QL + KVL + ROPE
NE, NG, EPG, TOPG, TOPK, DE = 64, 8, 8, 4, 6, 256
ROUTED_SCALE = 2.5
LN_EPS, RMS_EPS = 1e-5, 1e-6
ALPHA = (2 * 2) ** 0.25
THETA = 10000.0
NEG = -1e30
LOWEST, PICKED = -3e38, 3e38
GELU_C = 2.0 * float(np.sqrt(2.0 / np.pi))
NSLOT = 4
SUMS = 2
NPAIR = NSLOT // 2
SLOT = 3 * D * DE // P

K_ID, K_CAUSAL, K_SWA, K_COS, K_SIN = 0, 128, 384, 640, 768
K_COS1, K_SIN1, K_CCOS, K_CSIN, K_CADD, K_CMUL = 896, 960, 1024, 1088, 1152, 1182
NCONST = 1212


CAP = 64
M_BEFORE, M_ONES, M_IOTA, M_TOK, M_PASS = 0, 128, 256, 576, 578
NMOEC = 581
NOWHERE = 4096.0
NCHUNK = 4
CW = 2 * KC * DE // NCHUNK
GROUPS = NE // NSLOT


def mixture_constants():
    c = np.zeros((P, NMOEC), np.float32)
    c[:, M_BEFORE:M_BEFORE + P] = np.arange(P)[:, None] < np.arange(P)[None, :]
    c[:, M_ONES:M_ONES + P] = 1.0
    c[:, M_IOTA:M_IOTA + 320] = np.arange(320)[None, :]
    c[:, M_TOK:M_TOK + TC] = np.arange(P)[:, None] + P * np.arange(TC)[None, :] - NOWHERE
    c[:, M_PASS:M_PASS + 3] = CAP * np.arange(1, 4)[None, :]
    return c


def constants():
    c = np.zeros((P, NCONST), np.float32)
    q = np.arange(P)[:, None]
    k = np.arange(P)[None, :]
    c[:, K_ID:K_ID + P] = np.eye(P)
    c[:, K_CAUSAL + P:K_CAUSAL + 2 * P] = np.where(k <= q, 0.0, NEG)
    c[:, K_SWA:K_SWA + P] = np.where(k > q, 0.0, NEG)
    c[:, K_SWA + P:K_SWA + 2 * P] = np.where(k <= q, 0.0, NEG)

    def table(pos, d):
        inv = np.float32(THETA) ** (np.float32(-2.0) * np.arange(d // 2, dtype=np.float32) / np.float32(d))
        ang = pos.astype(np.float32)[:, None] * inv.astype(np.float32)[None, :]
        return np.tile(np.cos(ang), 2), np.tile(np.sin(ang), 2)

    for tc in range(TC):
        pos = np.arange(tc * P, tc * P + P)
        for (kc, ks), d in (((K_COS, K_SIN), HD), ((K_COS1, K_SIN1), ROPE)):
            cos, sin = table(pos, d)
            c[:, kc + tc * d:kc + tc * d + d] = cos
            c[:, ks + tc * d:ks + tc * d + d] = sin
    cos, sin = table(np.arange(NCMP) * CMP_STRIDE + CMP_LEN - 1, HD)
    c[:NCMP, K_CCOS:K_CCOS + HD] = cos
    c[:NCMP, K_CSIN:K_CSIN + HD] = sin
    end = np.arange(NCMP) * CMP_STRIDE + CMP_LEN - 1
    for tc in range(TC):
        seen = end[None, :] <= (np.arange(P) + tc * P)[:, None]
        c[:, K_CADD + tc * NCMP:K_CADD + (tc + 1) * NCMP] = np.where(seen, 0.0, NEG)
        c[:, K_CMUL + tc * NCMP:K_CMUL + (tc + 1) * NCMP] = seen
    return c


BOTH = dict(
    ln_mix_in=32, ln_ffn_in=32, wout_in=16, shared_in=48, router_in=32, moec_in=16, qk_pe=6, qk_act=6, score_pe=12,
    max_dve=24, exp_act=12, ptr_pe=12, ptr_act=12, pv_pe=12, o_dve=6, out_pe=2, lnmix_dve=2, lnffn_dve=2,
    logit_pe=1, sig_act=1, gate_dve=1, sgu_pe=2, ssilu_act=2, sh_dve=2, sht_pe=2, sht_act=2, sdown_pe=2,
    rank_pe=1, rank_dve=1, groups_dve=1, acc_dve=2, **{f"sum{tc}{j}_in": 16 for tc in range(TC) for j in range(SUMS)}, xt_pe=12, xt_act=6, xt_dve=6)
EACH = ["pick_dve", "slots_pe", "gates_dve", "gather_pe", "xhi_act", "xlo_dve",
        "hi_act", "lo_dve", "gu_pe", "top_act", "sum_dve", "silu_act", "h_dve", "ht_pe", "ht_act", "down_pe",
        "ya_act", "yd_dve"] + [f"scatter{k}_out" for k in range(NPAIR)] + [f"{part}{k}_in" for part in ("gu", "dn") for k in range(NSLOT)]
SEMS = (
    ["const_in", "x_in", "pe_in", "cmpw_in", "small1_in"]
    + [f"win_in{c}" for c in range(4)]
    + list(BOTH) + [f"{n}{L}" for L in range(2) for n in EACH]
    + ["proj_pe0", "proj_act0", "proj_dve0", "rope_dve0", "proj_pe1", "proj_act1",
       "pet_pe", "pet_act", "gates_pe", "gates_act", "kcv_pe", "kcv_act", "blk_dve",
       "hid_pe", "hid_act", "gelu_dve", "gin_dve", "gexp_act", "cmp_dve", "kv2_pe", "kcn_dve", "kct_pe", "kct_dve",
       "vbd_dve", "zero_pool", "csc_pe", "csub_dve", "cexp_act", "cp_dve", "cpt_pe", "cpt_act",
       "sink_dve", "sink_act", "win1_in", "wuq_in", "wukv_in",
       "var_dve", "root_pool", "power_pool", "rms_dve", "cnt_pe", "cnt_act", "q_pe", "q_act", "kv_pe", "kv_act",
       "krope_dve", "krt_pe", "krt_act", "qrope_dve", "kfull_dve", "dve_chain", "out_done"]
)


def bass_hybrid_block(nc, x, w_in0, sinks, pe_k, ck1, ck2, pe_v, cv1, cv2, w_out0, w_in1, q_norm,
                      kv_norm, w_uq, w_ukv, w_out1, ln_mix_g, ln_mix_b, ln_ffn_g, ln_ffn_b,
                      router_w, router_bias, e_gate, e_up, e_down, s_gate, s_up, s_down, const, moe_const, out):
    ctx = ExitStack()
    with ctx:
        def sb(name, cols):
            return ctx.enter_context(nc.sbuf_tensor(name, [P, cols], F32))

        sem = {n: ctx.enter_context(nc.semaphore(n)) for n in SEMS}
        cst = sb("cst", NCONST)
        xn = sb("x_rows", TC * D)
        at_room = (nc.sbuf_base + 31) // 32 * 32
        room = sb("room", KC * S + 8 * D)
        xt, wbig = room[:, 0:KC * S], room[:, KC * S:KC * S + 8 * D]
        xe = nc.alloc_sbuf_tensor_at("x_parts", [P, 2 * KC * P], F32R, offset=at_room)\
            .rearrange("p (e c m) -> p e c m", e=2, c=KC)
        whi = nc.alloc_sbuf_tensor_at("w_high", [P, 2 * KC * DE], F32R, offset=at_room + 8192)
        wlo = nc.alloc_sbuf_tensor_at("w_low", [P, 2 * KC * DE], F32R, offset=at_room + 8192 + 16384)
        ring = sb("ring", NSLOT * SLOT)
        lnp = sb("lnp", 2 * D)
        arena = sb("arena", 10800)
        tmp = sb("tmp", 1280)
        rw = sb("rw", KC * NE)
        rbias = sb("rbias", NE)
        small = sb("small", 256)

        PS = [ctx.enter_context(nc.psum_tensor(f"psum{i}", [P, 1024], F32)) for i in range(4)]
        BANK = [PS[i // 2][:, 512 * (i % 2):512 * (i % 2) + 512] for i in range(8)]

        def v(ap, **k):
            names = list(k)
            return ap.rearrange("p (" + " ".join(names) + ") -> p " + " ".join(names), **k)

        ident = cst[:, K_ID:K_ID + P]
        xrow = v(xn[:, :], t=TC, d=D)
        xcol = v(xt, c=KC, t=S)
        slot = [ring[:, i * SLOT:(i + 1) * SLOT] for i in range(NSLOT)]
        lng, lnb = lnp[:, 0:D], lnp[:, D:2 * D]
        wout = v(wbig, c=KC, d=D)

        def expert(w):
            gu = w[:, 0:2 * KC * DE].rearrange("p (m c f) -> p c m f", m=2, c=KC)
            return gu, w[:, 2 * KC * DE:SLOT].rearrange("p (c d) -> p c d", c=DE // P)

        at = [0]

        def take(n):
            at[0] += n
            return small[:, at[0] - n:at[0]]

        stats, mv = take(12), take(2)
        var, root, power = take(2), take(2), take(2)
        gates = take(TC * NGATE)
        nmax = take(12 * R)
        sums = take(12 * R)
        rec = take(16)
        nsink, sinkb = take(8), take(8)
        esink = take(16)
        kcmpt = take(NCMP)
        ssq = take(4)

        qkv = v(arena[:, 0:TC * IN0], t=TC, n=IN0)
        a0 = TC * IN0
        NB = 11
        rope = v(arena[:, a0:a0 + TC * NB * P], t=TC, n=NB * P)
        s0 = [arena[:, a0 + i * 1024:a0 + (i + 1) * 1024] for i in range(2)]
        a1 = a0 + TC * NB * P
        qkt = v(arena[:, a1:a1 + NB * S], b=NB, t=S)
        ot0 = v(arena[:, a1:a1 + KC * S], c=KC, t=S)
        a2 = a1 + NB * S
        kcv = v(arena[:, a2:a2 + 4 * S], b=4, t=S)
        pt0 = arena[:, a2:a2 + 1024]
        last = slot[3]
        cw1 = [v(last[:, i * 2048:(i + 1) * 2048], l=16, h=CMP_HID) for i in range(2)]
        b0 = 4096
        cw2 = [last[:, b0 + i * HD:b0 + (i + 1) * HD] for i in range(2)]
        pen = last[:, b0 + 128:b0 + 256]
        pet = v(last[:, b0 + 256:b0 + 320], k=2, l=CMP_LEN)
        blk = [last[:, b0 + 320 + i * 480:b0 + 800 + i * 480].rearrange("p (l g n) -> p l g n", l=16, g=G) for i in range(2)]
        vbd = [v(last[:, i * 256:(i + 1) * 256], j=R, d=HD) for i in range(2)]
        cs = v(last[:, 512:512 + 256], t=TC, h=8, n=16)
        cp = v(last[:, 768:768 + 512], t=TC, h=8, n=32)
        cpt = v(last[:, 1280:1280 + 512], u=4, q=P)
        kcn = last[:, 1792:1792 + 128]
        cu = last[:, 1920:2048]
        hidw = [last[:, 5376 + i * 64:5376 + (i + 1) * 64] for i in range(6)]
        crec = last[:, 5760:5776]

        uq = v(slot[0][:, 0:QL // P * MH * DQK], c=QL // P, n=MH * DQK)
        ukv = v(slot[1][:, 0:KVL // P * MH * 128], c=KVL // P, n=MH * 128)
        win1 = v(slot[2][:, 0:KC * IN1], c=KC, n=IN1)
        qn1 = v(slot[2][:, 0:TC * MH * DQK], t=TC, n=MH * DQK)
        qt1 = v(slot[3][:, 0:MH * S], h=MH, t=S)
        c1 = v(slot[3][:, MH * S:MH * S + TC * IN1], t=TC, n=IN1)
        kt1 = v(arena[:, 0:MH * S], h=MH, t=S)
        kv1 = v(arena[:, MH * S:MH * S + TC * MH * 128], t=TC, n=MH * 128)
        e0 = MH * S + TC * MH * 128
        ct1 = v(arena[:, e0:e0 + 5 * S], c=5, t=S)
        pt1 = arena[:, e0 + 5 * S:e0 + 5 * S + 1024]
        krt = arena[0:ROPE, e0 + 5 * S + 1024:e0 + 5 * S + 1024 + S]
        s1 = [xt[:, i * 1024:(i + 1) * 1024] for i in range(2)]
        nrm = ukv_norm = lnp
        atto = [v(xt, t=TC, n=D), v(slot[3][:, MH * S:MH * S + TC * D], t=TC, n=D)]
        attot = [ot0, xcol]

        acc = v(arena[:, 0:TC * D], t=TC, d=D)
        ys = [arena[:, 2048 + i * D:2048 + (i + 1) * D] for i in range(NPAIR)]
        shh = [arena[:, 2048 + i * DE:2048 + (i + 1) * DE] for i in range(2)]
        ssg = [arena[:, 2560 + i * DE:2560 + (i + 1) * DE] for i in range(2)]
        sht = [v(arena[:, 3072 + i * 256:3328 + i * 256], c=2, t=P) for i in range(2)]
        hh = [arena[0:CAP, 6144 + i * DE:6144 + (i + 1) * DE] for i in range(2)]
        ht = [v(arena[:, 6656 + i * 128:6656 + (i + 1) * 128], c=2, t=CAP) for i in range(2)]
        sg = arena[0:CAP, 6912:6912 + DE]
        gutop = arena[0:CAP, 7168:7680]
        gusum = arena[0:CAP, 7680:8192]
        M0 = 8192
        gate = v(arena[:, M0:M0 + TC * NE], t=TC, e=NE)
        rs = v(arena[:, M0 + 128:M0 + 256], t=TC, e=NE)
        rsb = v(arena[:, M0 + 256:M0 + 384], t=TC, e=NE)
        top8 = arena[:, M0 + 384:M0 + 512].rearrange("p (t g k) -> p t g k", t=TC, g=NG)
        gsc = v(arena[:, M0 + 512:M0 + 544], t=TC, k=16)
        gpick = v(arena[:, M0 + 544:M0 + 576], t=TC, k=16)
        gsel = v(arena[:, M0 + 576:M0 + 592], t=TC, k=NG)
        gneg = v(arena[:, M0 + 592:M0 + 608], t=TC, k=NG)
        m8 = v(arena[:, M0 + 608:M0 + 624], t=TC, k=8)
        esc = v(arena[:, M0 + 640:M0 + 784], t=TC, k=72)
        epick = v(arena[:, M0 + 784:M0 + 928], t=TC, k=72)
        gsum = arena[:, M0 + 928:M0 + 930]
        most, over = arena[:, M0 + 930:M0 + 931], arena[:, M0 + 931:M0 + 934]
        sel = v(arena[:, M0 + 944:M0 + 1072], t=TC, e=NE)
        pre = [v(arena[:, M0 + 128 + i * 128:M0 + 256 + i * 128], t=TC, e=NE) for i in range(2)]
        rank = v(arena[:, M0 + 1072:M0 + 1200], t=TC, e=NE)
        table = v(arena[:, M0 + 1200:M0 + 1456], t=TC, e=NE, n=2)
        onehot = [v(arena[:, M0 + 1456 + i * 256:M0 + 1712 + i * 256], t=TC, e=2, s=CAP) for i in range(2)]
        gslot = v(arena[0:CAP, M0 + 1968:M0 + 1976], k=NSLOT, n=2)
        mcon = arena[:, M0 + 1984:M0 + 1984 + NMOEC]
        rows_all = ctx.enter_context(nc.sbuf_tensor("rows", [P, NPAIR], U32))
        rows_u = [rows_all[:, i:i + 1] for i in range(NPAIR)]
        more_groups = ctx.enter_context(nc.sbuf_tensor("more_groups", [P, 1], U32))
        yd = [nc.dram_tensor(f"y_rows_dram{L}", [TOPK * S, D], F32).ap() for L in range(2)]
        ysum = [v(slot[3], j=TOPK, d=D), v(wbig[:, 0:TOPK * D], j=TOPK, d=D)]

        PARTS0 = (2, 0, 1, 3)
        SRC = [xrow, atto[0], xrow, xrow, atto[1], xrow]
        DST = [xcol, attot[0], xcol, xcol, attot[1], xcol]

        def unit0(n):
            branch, qc, g = n // 4, n // 2 % 2, n % 2
            qb, kb, vc = [(0, 4, C_VA), (5, 9, C_VS), (5, 10, C_VW)][branch]
            rows = slice(HD * g, HD * g + HD)
            return dict(
                n=n, qc=qc, scale=HD ** -0.5, mask=K_SWA if branch == 0 else K_CAUSAL, sink=branch == 0,
                q=[qkt[rows, qb + j, qc * P:(qc + 1) * P] for j in range(R)],
                k=[qkt[rows, kb, 0:(qc + 1) * P]] * R,
                v=[[qkv[:, c, vc + HD * g:vc + HD * g + HD]] * R for c in range(qc + 1)])

        def unit1(n):
            qc, hg = n // 4, n % 4
            hs = range(4 * hg, 4 * hg + 4)
            return dict(
                n=n, qc=qc, scale=DQK ** -0.5, mask=K_CAUSAL, sink=False,
                q=[qt1[0:DQK, h, qc * P:(qc + 1) * P] for h in hs],
                k=[kt1[0:DQK, h, 0:(qc + 1) * P] for h in hs],
                v=[[kv1[:, c, h * 128 + NOPE:(h + 1) * 128] for h in hs] for c in range(qc + 1)])

        UNITS = [[unit0(n) for n in range(12)], [unit1(n) for n in range(8)]]
        SBUFS = [s0, s1]
        PTBUF = [pt0, pt1]

        block = ctx.enter_context(nc.Block())

        def router_loads(sp, L):
            sp.dma_start(v(rw[:, :], c=KC, e=NE), router_w[L].rearrange("(p c) e -> p c e", c=KC)).then_inc(sem["router_in"], 16)
            sp.dma_start(rbias[:, :], router_bias[L:L + 1, :].partition_broadcast(P)[:, 0, :]).then_inc(sem["router_in"], 16)

        def norm_loads(sp, name, g, b, L):
            sp.dma_start(lng, g[L:L + 1, :].partition_broadcast(P)[:, 0, :]).then_inc(sem[name], 16)
            sp.dma_start(lnb, b[L:L + 1, :].partition_broadcast(P)[:, 0, :]).then_inc(sem[name], 16)

        def load_gate_up(sp, dst, g, u, s):
            for i, w in enumerate((g, u)):
                sp.dma_start(dst[:, i * KC * DE:(i + 1) * KC * DE], w.rearrange("(p c) f -> p (c f)", c=KC)).then_inc(s, 16)

        def load_down(sp, dst, d, s):
            sp.dma_start(dst[:, 2 * KC * DE:SLOT], d.rearrange("(p c) n -> p (c n)", c=DE // P)).then_inc(s, 16)

        def load_shared(sp, L):
            load_gate_up(sp, wbig, s_gate[L], s_up[L], sem["shared_in"])
            load_down(sp, wbig, s_down[L], sem["shared_in"])

        def one(w, L, e):
            return w[L, bass.ds(e, 1)].rearrange("a k n -> (a k) n")

        def expert_gate_up(sp, L, k, e):
            load_gate_up(sp, slot[k], one(e_gate, L, e), one(e_up, L, e), sem[f"gu{k}_in{L}"])

        def expert_down(sp, L, k, e):
            load_down(sp, slot[k], one(e_down, L, e), sem[f"dn{k}_in{L}"])

        def load_expert(sp, L, k, e):
            expert_gate_up(sp, L, k, e)
            expert_down(sp, L, k, e)

        def refills(sp, L):
            n_groups = sp.value_load(more_groups[0:1, 0:1], min_val=0, max_val=3 * GROUPS) + GROUPS

            def group(i, first):
                for k in range(NSLOT):
                    n = i * NSLOT + k
                    sp.wait_ge(sem[f"lo_dve{L}"], (n + 1) * NCHUNK)
                    expert_gate_up(sp, L, k, (n + NSLOT) % NE)
                    if not first or k:
                        sp.wait_ge(sem[f"down_pe{L}"], n)
                        expert_down(sp, L, (k - 1) % NSLOT, (n - 1 + NSLOT) % NE)

            group(0, True)
            with sp.Fori(1, n_groups - 1) as i:
                group(i, False)
            sp.wait_ge(sem[f"down_pe{L}"], (n_groups - 1) * NSLOT)
            expert_down(sp, L, NSLOT - 1, NE - 1)

        def mixture_loads(sp, L):
            sp.wait_ge(sem["out_pe"], TC * (L + 1))
            load_shared(sp, L)
            load_expert(sp, L, 3, 3)
            sp.dma_start(mcon, moe_const).then_inc(sem["moec_in"], 16)
            sp.wait_ge(sem["lnmix_dve"], TC * (L + 1))
            norm_loads(sp, "ln_ffn_in", ln_ffn_g, ln_ffn_b, L)
            sp.wait_ge(sem["groups_dve"], L + 1)
            refills(sp, L)

        def sum_loads(sp, L):
            n_groups = sp.value_load(more_groups[0:1, 0:1], min_val=0, max_val=3 * GROUPS) + GROUPS
            for k in range(NPAIR):
                sp.wait_ge(sem[f"scatter{k}_out{L}"], n_groups * 16)
            src = yd[L].rearrange("(j t p) d -> t p j d", j=TOPK, t=TC)
            for tc in range(TC):
                for j in range(SUMS):
                    ranks = slice(j * TOPK // SUMS, (j + 1) * TOPK // SUMS)
                    sp.dma_start(ysum[tc][:, ranks, :], src[tc][:, ranks, :]).then_inc(sem[f"sum{tc}{j}_in"], 16)

        @block.sync
        def _(sp):
            def rows(w, c):
                return w.rearrange("(p c) n -> p c n", c=c)

            sp.dma_start(cst[:, :], const).then_inc(sem["const_in"], 16)
            sp.dma_start(xrow, x[0].rearrange("(t p) d -> p t d", p=P)).then_inc(sem["x_in"], 16)
            sp.dma_start(sinkb, sinks.partition_broadcast(P)[:, 0, :]).then_inc(sem["x_in"], 16)
            w0 = rows(w_in0[0], KC)
            win0 = v(ring[:, 0:KC * IN0], c=KC, n=IN0)
            for c in range(KC):
                sp.dma_start(win0[:, c, :], w0[:, c, :]).then_inc(sem[f"win_in{c // 2}"], 16)
            for i, (pe, w1, w2) in enumerate(((pe_k, ck1, ck2), (pe_v, cv1, cv2))):
                sp.dma_start(pen[0:CMP_LEN, i * HD:(i + 1) * HD], pe[0]).then_inc(sem["pe_in"], 16)
                for lh in range(2):
                    sp.dma_start(cw1[i][HD * lh:HD * lh + HD, :, :],
                                 w1[0, lh * 1024:lh * 1024 + 1024, :].rearrange("(l d) h -> d l h", d=HD))\
                      .then_inc(sem["cmpw_in"], 16)
                sp.dma_start(cw2[i], w2[0]).then_inc(sem["cmpw_in"], 16)
            router_loads(sp, 0)
            norm_loads(sp, "ln_mix_in", ln_mix_g, ln_mix_b, 0)
            sp.dma_start(wout, rows(w_out0[0], KC)).then_inc(sem["wout_in"], 16)
            sp.wait_ge(sem["proj_pe0"], 8)
            sp.wait_ge(sem["gates_pe"], 1)
            for k in range(3):
                load_expert(sp, 0, k, k)
            mixture_loads(sp, 0)
            n_groups = sp.value_load(more_groups[0:1, 0:1], min_val=0, max_val=3 * GROUPS) + GROUPS
            sp.wait_ge(sem["down_pe0"], n_groups * NSLOT - 3)
            sp.dma_start(uq, rows(w_uq[0], QL // P)).then_inc(sem["wuq_in"], 16)
            sp.wait_ge(sem["down_pe0"], n_groups * NSLOT - 2)
            sp.dma_start(ukv, rows(w_ukv[0], KVL // P)).then_inc(sem["wukv_in"], 16)
            sp.wait_ge(sem["down_pe0"], n_groups * NSLOT - 1)
            sp.dma_start(win1, rows(w_in1[0], KC)).then_inc(sem["win1_in"], 16)
            sum_loads(sp, 0)
            sp.wait_ge(sem["gate_dve"], 1)
            router_loads(sp, 1)
            sp.wait_ge(sem["lnffn_dve"], TC)
            sp.dma_start(lnp[:, 0:QL], q_norm.partition_broadcast(P)[:, 0, :]).then_inc(sem["small1_in"], 16)
            sp.dma_start(lnp[:, QL:QL + KVL], kv_norm.partition_broadcast(P)[:, 0, :]).then_inc(sem["small1_in"], 16)
            sp.dma_start(wout, rows(w_out1[0], KC)).then_inc(sem["wout_in"], 16)
            sp.wait_ge(sem["rms_dve"], TC)
            norm_loads(sp, "ln_mix_in", ln_mix_g, ln_mix_b, 1)
            sp.wait_ge(sem["q_pe"], 6)
            load_expert(sp, 1, 0, 0)
            sp.wait_ge(sem["kv_pe"], 8)
            load_expert(sp, 1, 1, 1)
            sp.wait_ge(sem["qk_pe"], BOTH["qk_pe"] + 16)
            load_expert(sp, 1, 2, 2)
            mixture_loads(sp, 1)
            sum_loads(sp, 1)
            orows = out[0].rearrange("(t p) d -> p t d", p=P)
            for tc in range(TC):
                sp.wait_ge(sem["lnffn_dve"], BOTH["lnffn_dve"] + tc + 1)
                sp.dma_start(orows[:, tc, :], xrow[:, tc, :]).then_inc(sem["out_done"], 16)
            sp.wait_ge(sem["out_done"], 16 * TC)

        def pe_columns(pe, st, wait=None, base=0):
            for tc in range(TC):
                if wait:
                    pe.wait_ge(sem[wait], base + tc + 1)
                for c in range(KC):
                    o = (c % 2) * S + tc * P
                    mm = pe.transpose(BANK[c // 2][:, o:o + P], SRC[st][:, tc, c:c + (P - 1) * KC + 1:KC], ident)
                    if tc == TC - 1 and c % 2:
                        mm.then_inc(sem["xt_pe"], 1)

        def columns_ready(eng, st):
            eng.wait_ge(sem["xt_act"], 2 * st + 2)
            eng.wait_ge(sem["xt_dve"], 2 * st + 2)

        def pe_attention(pe, L):
            units = UNITS[L]
            n = len(units)
            for u in range(n + 2):
                if u < n:
                    U = units[u]
                    if u >= 2:
                        pe.wait_ge(sem["max_dve"], L * BOTH["max_dve"] + 2 * (u - 1))
                    sc = v(PS[u % 2][:, 0:R * (U["qc"] + 1) * P], j=R, k=(U["qc"] + 1) * P)
                    for j in range(R):
                        mm = pe.matmul(sc[:, j, :], U["q"][j], U["k"][j], start=True, stop=True)
                    mm.then_inc(sem["score_pe"], 1)
                if u >= 2:
                    U = units[u - 2]
                    pe.wait_ge(sem["ptr_act"], L * BOTH["ptr_act"] + u - 1)
                    if U["n"] // 2 >= 2:
                        pe.wait_ge(sem["o_dve"], L * BOTH["o_dve"] + U["n"] // 2 - 1)
                    w = (U["qc"] + 1) * P
                    pt = v(PTBUF[L][:, 0:R * w], j=R, k=w)
                    ob = BANK[6 + U["n"] // 2 % 2]
                    for j in range(R):
                        o = (U["n"] % 2) * R * HD + j * HD
                        for c in range(U["qc"] + 1):
                            mm = pe.matmul(ob[:, o:o + HD], pt[:, j, c * P:(c + 1) * P], U["v"][c][j],
                                           start=c == 0, stop=c == U["qc"])
                    mm.then_inc(sem["pv_pe"], 1)
                if 1 <= u <= n:
                    U = units[u - 1]
                    pe.wait_ge(sem["exp_act"], L * BOTH["exp_act"] + u)
                    if u >= 2:
                        pe.wait_ge(sem["ptr_act"], L * BOTH["ptr_act"] + u - 1)
                    w = (U["qc"] + 1) * P
                    s = v(SBUFS[L][(u - 1) % 2][:, 0:R * w], j=R, k=w)
                    po = v(PS[2][:, 0:R * w], j=R, k=w)
                    for j in range(R):
                        for c in range(U["qc"] + 1):
                            mm = pe.transpose(po[:, j, c * P:(c + 1) * P], s[:, j, c * P:(c + 1) * P], ident)
                    mm.then_inc(sem["ptr_pe"], 1)

        def pe_out(pe, L):
            pe.wait_ge(sem["wout_in"], L * BOTH["wout_in"] + 16)
            columns_ready(pe, 1 + 3 * L)
            for tc in range(TC):
                for half in range(2):
                    for c in range(KC):
                        mm = pe.matmul(PS[2 + tc][:, half * 512:(half + 1) * 512], attot[L][:, c, tc * P:(tc + 1) * P],
                                       wout[:, c, half * 512:(half + 1) * 512], start=c == 0, stop=c == KC - 1)
                mm.then_inc(sem["out_pe"], 1)

        def pe_logits(pe, L):
            columns_ready(pe, 2 + 3 * L)
            pe.wait_ge(sem["router_in"], L * BOTH["router_in"] + 32)
            r = v(rw[:, :], c=KC, e=NE)
            for tc in range(TC):
                for c in range(KC):
                    mm = pe.matmul(BANK[0][:, tc * NE:(tc + 1) * NE], xcol[:, c, tc * P:(tc + 1) * P], r[:, c, :],
                                   start=c == 0, stop=c == KC - 1)
            mm.then_inc(sem["logit_pe"], 1)

        def pe_shared(pe, L):
            gu, dn = expert(wbig[:, 0:SLOT])
            pe.wait_ge(sem["shared_in"], 48 * (L + 1))
            pe.wait_ge(sem["sig_act"], L + 1)
            for tc in range(TC):
                for c in range(KC):
                    mm = pe.matmul(v(BANK[tc], m=2, f=DE), xcol[:, c, tc * P:(tc + 1) * P], gu[:, c, :, :],
                                   start=c == 0, stop=c == KC - 1)
                mm.then_inc(sem["sgu_pe"], 1)
            pe.wait_ge(sem["gate_dve"], L + 1)
            pe.wait_ge(sem["moec_in"], 16 * (L + 1))
            before, ones = mcon[:, M_BEFORE:M_BEFORE + P], mcon[:, M_ONES:M_ONES + P]
            pe.matmul(BANK[2][:, 0:NE], before, sel[:, 0, :], start=True, stop=True)
            pe.matmul(BANK[2][:, NE:2 * NE], ones, sel[:, 0, :], start=True, stop=False)
            pe.matmul(BANK[2][:, NE:2 * NE], before, sel[:, 1, :], start=False, stop=True)
            pe.matmul(BANK[2][:, 2 * NE:3 * NE], ones, sel[:, 0, :], start=True, stop=False)
            pe.matmul(BANK[2][:, 2 * NE:3 * NE], ones, sel[:, 1, :], start=False, stop=True).then_inc(sem["rank_pe"], 1)
            for tc in range(TC):
                pe.wait_ge(sem["sh_dve"], TC * L + tc + 1)
                if tc:
                    pe.wait_ge(sem["rank_dve"], L + 1)
                for c in range(2):
                    mm = pe.transpose(BANK[3 - tc][:, c * P:(c + 1) * P], shh[tc][:, c:c + 2 * P - 1:2], ident)
                mm.then_inc(sem["sht_pe"], 1)
                pe.wait_ge(sem["sht_act"], TC * L + tc + 1)
                for half in range(2):
                    for c in range(2):
                        mm = pe.matmul(PS[2 + tc][:, half * 512:(half + 1) * 512], sht[tc][:, c, :],
                                       dn[:, c, half * 512:(half + 1) * 512], start=c == 0, stop=c == 1)
                mm.then_inc(sem["sdown_pe"], 1)

        def steps(eng, L, step):
            n_groups = eng.value_load(more_groups[0:1, 0:1], min_val=0, max_val=3 * GROUPS) + GROUPS

            def group(i, first, last):
                for k in range(NSLOT):
                    def have(d):
                        return (not last or k + d < NSLOT) and (not first or k + d >= 0)
                    step(i * NSLOT + k, k, have)

            group(0, True, False)
            with eng.Fori(1, n_groups - 1) as i:
                group(i, False, False)
            group(n_groups - 1, False, True)
            return n_groups

        def pe_gather(pe, L, n, k, part):
            if part == 0:
                pe.wait_ge(sem[f"pick_dve{L}"], pairs_before(n, k) + 1)
            pick = onehot[k // 2 % 2].rearrange("p t e s -> p t (e s)")
            for c in range(part * KC // 2, (part + 1) * KC // 2):
                for tc in range(TC):
                    mm = pe.matmul(PS[0][:, c * P:(c + 1) * P], xrow[:, tc, c:c + (P - 1) * KC + 1:KC],
                                   pick[:, tc, :], start=tc == 0, stop=tc == TC - 1)
            if part == 1:
                mm.then_inc(sem[f"gather_pe{L}"], 1)
                for tc in range(TC):
                    mm = pe.matmul(BANK[5][:, 0:4], pick[:, tc, :], table[:, tc, bass.ds(n % NE, 2), :],
                                   start=tc == 0, stop=tc == TC - 1)
                mm.then_inc(sem[f"slots_pe{L}"], 1)

        def pe_down(pe, L, n, k, early):
            pe.wait_ge(sem[f"ht_act{L}"], n + 1)
            pe.wait_ge(sem[f"dn{k % NSLOT}_in{L}"], (uses_before(n, k) + 1) * 16)
            if not early:
                pe.wait_ge(sem[f"ya_act{L}"], n)
                pe.wait_ge(sem[f"yd_dve{L}"], n)
            dn = expert(slot[k % NSLOT])[1]
            for half in range(2):
                for c in range(2):
                    mm = pe.matmul(PS[3][0:CAP, half * 512:(half + 1) * 512], ht[k % 2][:, c, :],
                                   dn[:, c, half * 512:(half + 1) * 512], start=c == 0, stop=c == 1)
            mm.then_inc(sem[f"down_pe{L}"], 1)

        def pe_experts(pe, L):
            pe_gather(pe, L, 0, 0, 0)
            pe.wait_ge(sem["acc_dve"], TC * L + 1)
            pe_gather(pe, L, 0, 0, 1)

            def step(n, k, have):
                pe.wait_ge(sem[f"xlo_dve{L}"], pairs_before(n, k) + 1)
                if have(-2):
                    pe.wait_ge(sem[f"sum_dve{L}"], n - 1)
                bank = BANK[2 + k % 2]
                for j in range(NCHUNK):
                    pe.wait_ge(sem[f"lo_dve{L}"], n * NCHUNK + j + 1)
                    for c in range(j * KC // NCHUNK, (j + 1) * KC // NCHUNK):
                        for w in (whi, wlo):
                            mm = pe.matmul(bank, xe[:, k % 2, c, :], w[:, c * 2 * DE:(c + 1) * 2 * DE],
                                           start=c == 0 and w is whi, stop=c == KC - 1 and w is wlo)
                    mm.then_inc(sem[f"gu_pe{L}"], 1)
                if k % 2 == 0 and have(2):
                    pe_gather(pe, L, n + 2, k + 2, 0)
                if k % 2 == 1 and have(1):
                    pe.wait_ge(sem[f"gates_dve{L}"], pairs_before(n, k) + 1)
                    pe_gather(pe, L, n + 1, k + 1, 1)
                if have(-1):
                    pe_down(pe, L, n - 1, k + 3, early=not have(-2))
                pe.wait_ge(sem[f"h_dve{L}"], n + 1)
                if have(-1):
                    pe.wait_ge(sem[f"ht_act{L}"], n)
                pe.nop(nofuse=True)
                pe.wait_ge(sem["const_in"], 16)
                for c in range(2):
                    mm = pe.transpose(BANK[4][:, c * CAP:(c + 1) * CAP], hh[k % 2][:, c:c + 2 * P - 1:2],
                                      ident[0:CAP, 0:CAP])
                mm.then_inc(sem[f"ht_pe{L}"], 1)

            n_groups = steps(pe, L, step)
            pe_down(pe, L, n_groups * NSLOT - 1, 3, early=False)

        def half_rows(pairs, k):
            return pairs[k // 2][CAP * (k % 2):CAP * (k % 2) + CAP]

        def pairs_before(n, k):
            return (n - k) // 2 + k // 2

        def uses_before(n, k):
            return (n - k) // NSLOT + k // NSLOT

        def pe_moe_steps(pe, L):
            pe_shared(pe, L)
            pe_experts(pe, L)

        @block.tensor
        def _(pe):
            pe.wait_ge(sem["const_in"], 16)
            pe.wait_ge(sem["x_in"], 32)
            pe_columns(pe, 0)
            columns_ready(pe, 0)
            win0 = v(ring[:, 0:KC * IN0], c=KC, n=IN0)
            def project(n, tc, c):
                return pe.matmul(BANK[2 * n + tc], xcol[:, c, tc * P:(tc + 1) * P], win0[:, c, n * 512:(n + 1) * 512],
                                 start=c == 0, stop=c == KC - 1)

            for c in range(KC // 2):
                pe.wait_ge(sem[f"win_in{c // 2}"], 32)
                for n in range(4):
                    for tc in range(TC):
                        project(n, tc, c)
            for n in PARTS0:
                for tc in range(TC):
                    for c in range(KC // 2, KC):
                        pe.wait_ge(sem[f"win_in{c // 2}"], 32)
                        mm = project(n, tc, c)
                    mm.then_inc(sem["proj_pe0"], 1)
                if n == 0:
                    pe.wait_ge(sem["proj_act0"], 1)
                    pe.wait_ge(sem["proj_dve0"], 1)
                    for i, c in enumerate((C_KC, C_VC)):
                        for g in range(G):
                            for tc in range(TC):
                                o = g * S + tc * P
                                mm = pe.transpose(BANK[4 + i][0:HD, o:o + P], qkv[:, tc, c + g * HD:c + (g + 1) * HD], ident)
                        mm.then_inc(sem["kcv_pe"], 1)
                    pe.wait_ge(sem["pe_in"], 32)
                    pe.wait_ge(sem["proj_dve0"], 2)
                    for i in range(2):
                        mm = pe.transpose(BANK[1][0:HD, i * CMP_LEN:(i + 1) * CMP_LEN], pen[0:CMP_LEN, i * HD:(i + 1) * HD],
                                          ident[0:CMP_LEN, 0:CMP_LEN])
                    mm.then_inc(sem["pet_pe"], 1)
                if n == 1:
                    pe.wait_ge(sem["cmpw_in"], 96)
                    pe.wait_ge(sem["blk_dve"], 8)
                    pe.wait_ge(sem["pet_act"], 1)
                    for i in range(2):
                        for l in range(16):
                            mm = pe.matmul(BANK[1][:, i * 32:i * 32 + G * NCMP], cw1[i][:, l, :],
                                           blk[i][:, l, :, :].rearrange("p g n -> p (g n)"), start=l == 0, stop=l == 15)
                    mm.then_inc(sem["hid_pe"], 1)
            pe.wait_ge(sem["proj_act0"], 2)
            for tc in range(TC):
                for c in range(KC):
                    mm = pe.matmul(BANK[0][:, tc * 32:tc * 32 + NGATE], xcol[:, c, tc * P:(tc + 1) * P],
                                   win0[:, c, C_GT:C_GT + NGATE], start=c == 0, stop=c == KC - 1)
            mm.then_inc(sem["gates_pe"], 1)
            pe.wait_ge(sem["gelu_dve"], 1)
            for i in range(2):
                for g in range(G):
                    o = 128 + i * 128 + g * HD
                    mm = pe.matmul(BANK[1][0:NCMP, o:o + HD], hidw[5][:, i * 32 + g * NCMP:i * 32 + (g + 1) * NCMP],
                                   cw2[i], start=True, stop=True)
            mm.then_inc(sem["kv2_pe"], 1)
            pe.wait_ge(sem["rope_dve0"], TC)
            for u in range(6):
                bank = BANK[(2, 3, 6, 7, 4, 5)[u]]
                if u >= 4:
                    pe.wait_ge(sem["kcv_act"], u - 3)
                for b in range(2 * u, min(2 * u + 2, NB)):
                    for tc in range(TC):
                        o = (b % 2) * S + tc * P
                        mm = pe.transpose(bank[:, o:o + P], rope[:, tc, b * P:(b + 1) * P], ident)
                mm.then_inc(sem["qk_pe"], 1)
            pe.wait_ge(sem["kcn_dve"], 1)
            pe.transpose(BANK[0][:, 0:NCMP], kcn[0:NCMP, :], ident[0:NCMP, 0:NCMP]).then_inc(sem["kct_pe"], 1)
            pe.wait_ge(sem["kct_dve"], 1)
            pe.wait_ge(sem["qk_act"], 6)
            for h in range(8):
                for tc in range(TC):
                    rows = slice(HD * (h // R), HD * (h // R) + HD)
                    o = tc * R * 16 + h % R * 16
                    mm = pe.matmul(BANK[(0, 5)[h // R]][:, o:o + NCMP], qkt[rows, 5 + h % R, tc * P:(tc + 1) * P],
                                   kcmpt[rows, :], start=True, stop=True)
            mm.then_inc(sem["csc_pe"], 1)
            pe.wait_ge(sem["cp_dve"], 1)
            for i in range(4):
                tc, g = i // 2, i % 2
                mm = pe.transpose(BANK[1][:, i * P:(i + 1) * P], cp[:, tc, g * R:(g + 1) * R, :], ident)
            mm.then_inc(sem["cpt_pe"], 1)
            pe.wait_ge(sem["cpt_act"], 1)
            pe.wait_ge(sem["vbd_dve"], 1)
            for tc in range(TC):
                for g in range(G):
                    mm = pe.matmul(BANK[4 + tc][:, g * 256:(g + 1) * 256], cpt[:, tc * 2 + g, :],
                                   vbd[g].rearrange("p j d -> p (j d)"), start=True, stop=True)
            mm.then_inc(sem["csc_pe"], 1)
            pe.wait_ge(sem["cmp_dve"], 1)
            pe_attention(pe, 0)
            pe.wait_ge(sem["o_dve"], 6)
            pe_columns(pe, 1)
            pe_out(pe, 0)
            pe_columns(pe, 2, "lnmix_dve")
            pe_logits(pe, 0)
            pe_moe_steps(pe, 0)
            pe_columns(pe, 3, "lnffn_dve")
            columns_ready(pe, 3)
            pe.wait_ge(sem["win1_in"], 16)
            for tc in range(TC):
                for n, w in ((0, 512), (512, IN1 - 512)):
                    for c in range(KC):
                        mm = pe.matmul(PS[2 + tc][:, n:n + w], xcol[:, c, tc * P:(tc + 1) * P], win1[:, c, n:n + w],
                                       start=c == 0, stop=c == KC - 1)
                mm.then_inc(sem["proj_pe1"], 1)
            pe.wait_ge(sem["rms_dve"], TC)
            for c in range(5):
                for tc in range(TC):
                    o = (c % 2) * S + tc * P
                    if c < 3:
                        src = c1[:, tc, c:c + 3 * P - 2:3]
                    else:
                        src = c1[:, tc, QL + c - 3:QL + c - 3 + 2 * P - 1:2]
                    mm = pe.transpose(BANK[c // 2][:, o:o + P], src, ident)
                if c % 2 or c == 4:
                    mm.then_inc(sem["cnt_pe"], 1)
            pe.wait_ge(sem["krope_dve"], TC)
            for tc in range(TC):
                mm = pe.transpose(BANK[3][0:ROPE, tc * P:(tc + 1) * P], c1[:, tc, QL + KVL:IN1], ident)
            mm.then_inc(sem["krt_pe"], 1)
            pe.wait_ge(sem["cnt_act"], 3)
            pe.wait_ge(sem["krt_act"], 1)
            pe.wait_ge(sem["wuq_in"], 16)
            for i in range(6):
                tc, n = i // 3, i % 3
                for c in range(3):
                    mm = pe.matmul(BANK[i], ct1[:, c, tc * P:(tc + 1) * P], uq[:, c, n * 512:(n + 1) * 512],
                                   start=c == 0, stop=c == 2)
                mm.then_inc(sem["q_pe"], 1)
            pe.wait_ge(sem["wukv_in"], 16)
            for i in range(8):
                tc, n = i // 4, i % 4
                b = (i + 6) % 8
                if i >= 2:
                    pe.wait_ge(sem["q_act"], i - 1)
                for c in range(2):
                    mm = pe.matmul(BANK[b], ct1[:, 3 + c, tc * P:(tc + 1) * P], ukv[:, c, n * 512:(n + 1) * 512],
                                   start=c == 0, stop=c == 1)
                mm.then_inc(sem["kv_pe"], 1)
            pe.wait_ge(sem["kv_act"], 8)
            pe.wait_ge(sem["qrope_dve"], TC)
            for u in range(16):
                if u >= 4:
                    pe.wait_ge(sem["qk_act"], BOTH["qk_act"] + u - 3)
                hs = [u // 2 * 2, u // 2 * 2 + 1]
                hs = [2 * (u % 8), 2 * (u % 8) + 1]
                for i, h in enumerate(hs):
                    for tc in range(TC):
                        o = i * S + tc * P
                        if u < 8:
                            mm = pe.transpose(BANK[u % 4][0:NOPE, o:o + P], kv1[:, tc, h * 128:h * 128 + NOPE], ident)
                        else:
                            mm = pe.transpose(BANK[u % 4][0:DQK, o:o + P], qn1[:, tc, h * DQK:(h + 1) * DQK], ident)
                mm.then_inc(sem["qk_pe"], 1)
            pe.wait_ge(sem["qk_act"], BOTH["qk_act"] + 16)
            pe.wait_ge(sem["kfull_dve"], 1)
            pe_attention(pe, 1)
            pe.wait_ge(sem["o_dve"], BOTH["o_dve"] + 4)
            pe_columns(pe, 4)
            pe_out(pe, 1)
            pe_columns(pe, 5, "lnmix_dve", BOTH["lnmix_dve"])
            pe_logits(pe, 1)
            pe_moe_steps(pe, 1)

        def act_columns(act, st):
            for b in (0, 2):
                act.wait_ge(sem["xt_pe"], 4 * st + b + 1)
                nc.scalar.copy(DST[st][:, 2 * b:2 * b + 2, :], v(BANK[b], c=2, t=S)).then_inc(sem["xt_act"], 1)

        def act_attention(act, L):
            units = UNITS[L]
            n = len(units)
            for u in range(n + 1):
                if u < n:
                    U = units[u]
                    w = (U["qc"] + 1) * P
                    s = v(SBUFS[L][u % 2][:, 0:R * w], j=R, k=w)
                    act.wait_ge(sem["max_dve"], L * BOTH["max_dve"] + 2 * u + 2)
                    for j in range(R):
                        i = u * R + j
                        ins = nc.scalar.activation(s[:, j, :], s[:, j, :], ACT.Exp, bias=nmax[:, i:i + 1],
                                                   accum_out=sums[:, i:i + 1])
                    ins.then_inc(sem["exp_act"], 1)
                    if U["sink"] and u == 3:
                        act.wait_ge(sem["sink_dve"], 5)
                        nc.scalar.activation(esink, esink, ACT.Exp).then_inc(sem["sink_act"], 1)
                if u >= 1:
                    U = units[u - 1]
                    w = (U["qc"] + 1) * P
                    act.wait_ge(sem["ptr_pe"], L * BOTH["ptr_pe"] + u)
                    if u >= 2:
                        act.wait_ge(sem["pv_pe"], L * BOTH["pv_pe"] + u - 1)
                    nc.scalar.copy(PTBUF[L][:, 0:R * w], PS[2][:, 0:R * w]).then_inc(sem["ptr_act"], 1)

        def act_logits(act, L):
            act.wait_ge(sem["logit_pe"], L * BOTH["logit_pe"] + 1)
            nc.scalar.activation(rs, v(BANK[0][:, 0:TC * NE], t=TC, e=NE), ACT.Exp, scale=-1.0).then_inc(sem["sig_act"], 1)

        def act_moe(act, L):
            for tc in range(TC):
                act.wait_ge(sem["sgu_pe"], TC * L + tc + 1)
                nc.scalar.activation(ssg[tc], BANK[tc][:, 0:DE], ACT.Silu).then_inc(sem["ssilu_act"], 1)
            for tc in range(TC):
                act.wait_ge(sem["sht_pe"], TC * L + tc + 1)
                nc.scalar.copy(sht[tc], v(BANK[3 - tc][:, 0:2 * P], c=2, t=P)).then_inc(sem["sht_act"], 1)

            def high(n, k, j, used=True):
                if j == 0:
                    act.wait_ge(sem[f"gu{k % NSLOT}_in{L}"], (uses_before(n, k) + 1) * 32)
                if used:
                    act.wait_ge(sem[f"gu_pe{L}"], (n - 1) * NCHUNK + j + 1)
                part = slot[k % NSLOT][:, 0:2 * KC * DE].rearrange("p (m c f) -> p c m f", m=2, c=KC)
                c = slice(j * KC // NCHUNK, (j + 1) * KC // NCHUNK)
                nc.scalar.copy(whi[:, j * CW:(j + 1) * CW].rearrange("p (c m f) -> p c m f", m=2, f=DE), part[:, c])\
                    .then_inc(sem[f"hi_act{L}"], 1)

            def x_high(n, k):
                act.wait_ge(sem[f"gather_pe{L}"], pairs_before(n, k) + 1)
                nc.scalar.copy(xe[:, :, :, 0:CAP].rearrange("p e c s -> p c e s"), PS[0][:, :].rearrange("p (c e s) -> p c e s", c=KC, e=2))\
                    .then_inc(sem[f"xhi_act{L}"], 1)

            def y_half(n, k):
                act.wait_ge(sem[f"down_pe{L}"], n + 1)
                nc.scalar.copy(half_rows(ys, k)[:, 0:512], PS[3][0:CAP, 0:512]).then_inc(sem[f"ya_act{L}"], 1)

            act.wait_ge(sem["sdown_pe"], TC * (L + 1))
            for j in range(NCHUNK):
                high(0, 0, j, used=False)
            x_high(0, 0)

            def step(n, k, have):
                if have(1):
                    high(n + 1, k + 1, 0)
                    high(n + 1, k + 1, 1)
                act.wait_ge(sem[f"gu_pe{L}"], (n + 1) * NCHUNK)
                if have(-1):
                    act.wait_ge(sem[f"sum_dve{L}"], n)
                nc.scalar.copy(gutop, BANK[2 + k % 2][0:CAP, :]).then_inc(sem[f"top_act{L}"], 1)
                if have(1):
                    high(n + 1, k + 1, 2)
                act.wait_ge(sem[f"sum_dve{L}"], n + 1)
                if have(-1):
                    act.wait_ge(sem[f"h_dve{L}"], n)
                nc.scalar.activation(sg, gusum[:, 0:DE], ACT.Silu).then_inc(sem[f"silu_act{L}"], 1)
                if have(1):
                    if k % 2:
                        x_high(n + 1, k + 1)
                    high(n + 1, k + 1, 3)
                if have(-1):
                    y_half(n - 1, (k - 1) % NSLOT)
                if have(-4):
                    act.wait_ge(sem[f"scatter{k // 2}_out{L}"], uses_before(n, k) * 16)
                act.wait_ge(sem[f"ht_pe{L}"], n + 1)
                nc.scalar.copy(ht[k % 2], v(BANK[4][:, 0:2 * CAP], c=2, t=CAP)).then_inc(sem[f"ht_act{L}"], 1)

            n_groups = steps(act, L, step)
            y_half(n_groups * NSLOT - 1, 3)

        @block.scalar
        def _(act):
            act_columns(act, 0)
            for i, n in enumerate(PARTS0):
                act.wait_ge(sem["proj_pe0"], 2 * i + 1)
                nc.scalar.copy(qkv[:, 0, n * 512:(n + 1) * 512], BANK[2 * n]).then_inc(sem["proj_act0"], 1)
                if n == 0:
                    for i in range(2):
                        act.wait_ge(sem["kcv_pe"], i + 1)
                        nc.scalar.copy(kcv[0:HD, 2 * i:2 * i + 2, :], v(BANK[4 + i][0:HD, :], g=G, t=S)).then_inc(sem["kcv_act"], 1)
                    act.wait_ge(sem["pet_pe"], 1)
                    nc.scalar.copy(pet[0:HD, :, :], v(BANK[1][0:HD, 0:2 * CMP_LEN], k=2, l=CMP_LEN)).then_inc(sem["pet_act"], 1)
                if n == 1:
                    act.wait_ge(sem["hid_pe"], 1)
                    hv = [v(h, k=2, n=32)[:, :, 0:G * NCMP] for h in hidw]
                    nc.scalar.copy(hv[0], v(BANK[1][:, 0:64], k=2, n=32)[:, :, 0:G * NCMP]).then_inc(sem["hid_act"], 1)
                    act.wait_ge(sem["gin_dve"], 1)
                    nc.scalar.activation(hv[3], hv[2], ACT.Exp, scale=-GELU_C).then_inc(sem["gexp_act"], 1)
            act.wait_ge(sem["gates_pe"], 1)
            nc.scalar.activation(v(gates, t=TC, n=NGATE), v(BANK[0][:, 0:64], t=TC, n=32)[:, :, 0:NGATE], ACT.Exp, scale=-1.0)\
                .then_inc(sem["gates_act"], 1)
            for u in range(6):
                act.wait_ge(sem["qk_pe"], u + 1)
                bank = BANK[(2, 3, 6, 7, 4, 5)[u]]
                w = min(2, NB - 2 * u)
                nc.scalar.copy(qkt[:, 2 * u:2 * u + w, :], v(bank[:, 0:w * S], b=w, t=S)).then_inc(sem["qk_act"], 1)
            act.wait_ge(sem["csub_dve"], 1)
            nc.scalar.activation(cs[:, :, :, 0:NCMP], cs[:, :, :, 0:NCMP], ACT.Exp).then_inc(sem["cexp_act"], 1)
            act.wait_ge(sem["cpt_pe"], 1)
            nc.scalar.copy(cpt, v(BANK[1], u=4, q=P)).then_inc(sem["cpt_act"], 1)
            act_attention(act, 0)
            act_columns(act, 1)
            act_columns(act, 2)
            act_logits(act, 0)
            act_moe(act, 0)
            act_columns(act, 3)
            for tc in range(TC):
                act.wait_ge(sem["proj_pe1"], tc + 1)
                nc.scalar.copy(c1[:, tc, :], PS[2 + tc][:, 0:IN1]).then_inc(sem["proj_act1"], 1)
            for i in range(3):
                act.wait_ge(sem["cnt_pe"], i + 1)
                w = 2 if i < 2 else 1
                nc.scalar.copy(ct1[:, 2 * i:2 * i + w, :], v(BANK[i][:, 0:w * S], c=w, t=S)).then_inc(sem["cnt_act"], 1)
            act.wait_ge(sem["krt_pe"], 1)
            nc.scalar.copy(krt, BANK[3][0:ROPE, 0:S]).then_inc(sem["krt_act"], 1)
            for i in range(6):
                act.wait_ge(sem["q_pe"], i + 1)
                nc.scalar.copy(qn1[:, i // 3, i % 3 * 512:(i % 3 + 1) * 512], BANK[i]).then_inc(sem["q_act"], 1)
            for i in range(8):
                act.wait_ge(sem["kv_pe"], i + 1)
                nc.scalar.copy(kv1[:, i // 4, i % 4 * 512:(i % 4 + 1) * 512], BANK[(i + 6) % 8]).then_inc(sem["kv_act"], 1)
            for u in range(16):
                act.wait_ge(sem["qk_pe"], BOTH["qk_pe"] + u + 1)
                h = 2 * (u % 8)
                if u < 8:
                    nc.scalar.copy(kt1[0:NOPE, h:h + 2, :], v(BANK[u % 4][0:NOPE, :], h=2, t=S)).then_inc(sem["qk_act"], 1)
                else:
                    nc.scalar.copy(qt1[0:DQK, h:h + 2, :], v(BANK[u % 4][0:DQK, :], h=2, t=S)).then_inc(sem["qk_act"], 1)
            act_attention(act, 1)
            act_columns(act, 4)
            act_columns(act, 5)
            act_logits(act, 1)
            act_moe(act, 1)

        def pool_moe(pool, L):
            def scatter(n, k):
                pool.wait_ge(sem[f"ya_act{L}"], n + 1)
                pool.wait_ge(sem[f"yd_dve{L}"], n + 1)
                pool.nop(nofuse=True)
                pool.wait_ge(sem["groups_dve"], L + 1)
                pool.indirect_dma_start(
                    out=yd[L], out_offset=bass.IndirectOffsetOnAxis(ap=rows_u[k // 2], axis=0),
                    in_=ys[k // 2], in_offset=None,
                    bounds_check=TOPK * S - 1, oob_is_err=False).then_inc(sem[f"scatter{k // 2}_out{L}"], 16)

            pool.wait_ge(sem["groups_dve"], L + 1)
            steps(pool, L, lambda n, k, have: scatter(n, k) if k % 2 else None)

        @block.gpsimd
        def _(pool):
            pool.memset(power, -0.5).then_inc(sem["power_pool"], 1)
            pool.wait_ge(sem["hid_pe"], 1)
            pool.memset(last[:, 0:512], 0.0).then_inc(sem["zero_pool"], 1)
            pool.memset(last[:, 768:768 + 512], 0.0).then_inc(sem["zero_pool"], 1)
            pool.wait_ge(sem["power_pool"], 1)
            def roots(a, b, n=1):
                for i in range(a, b):
                    pool.wait_ge(sem["var_dve"], i + 1)
                    pool.tensor_tensor(root[:, 0:n], var[:, 0:n], power[:, 0:n], ALU.pow).then_inc(sem["root_pool"], 1)

            roots(0, 2)
            pool_moe(pool, 0)
            roots(2, 4)
            roots(4, 6, 2)
            roots(6, 8)
            pool_moe(pool, 1)
            roots(8, 10)

        @block.vector
        def _(dve):
            chain = [0]

            def link(ins):
                chain[0] += 1
                ins.then_inc(sem["dve_chain"], 1)
                dve.wait_ge(sem["dve_chain"], chain[0])

            marks = {}

            def mark(ins, name):
                ins.then_inc(sem[name], 1)
                marks[name] = marks.get(name, 0) + 1

            def settle(name):
                dve.wait_ge(sem[name], marks[name])

            V = nc.vector

            def columns(st):
                for b in (1, 3):
                    dve.wait_ge(sem["xt_pe"], 4 * st + b + 1)
                    mark(V.tensor_copy(DST[st][:, 2 * b:2 * b + 2, :], v(BANK[b], c=2, t=S)), "xt_dve")

            def bc(ap, shape):
                return ap.to_broadcast(shape)

            def apply_rope(src, dsts, cos, sin, heads, half, done=None):
                d = 2 * half
                n = heads * d
                t = v(tmp[:, 0:n], h=heads, d=d)
                u = v(tmp[:, 640:640 + n], h=heads, d=d)
                pr = src.shape[0]
                t, u = t[0:pr], u[0:pr]
                cb = cos[:, None, :].to_broadcast([pr, heads, d])
                sbc = sin[:, None, :].to_broadcast([pr, heads, d])
                V.tensor_tensor(t, src, cb, ALU.mult)
                link(V.tensor_tensor(u, src, sbc, ALU.mult))
                ins = None
                for a, b, (o1, o2), view in dsts:
                    V.tensor_tensor(o1, view(t[:, a:b, 0:half]), view(u[:, a:b, half:d]), ALU.subtract)
                    ins = V.tensor_tensor(o2, view(t[:, a:b, half:d]), view(u[:, a:b, 0:half]), ALU.add)
                    if b < heads or done is None:
                        link(ins)
                if done is not None:
                    mark(ins, done)
                    settle(done)

            roots = [0]

            def inverse_root(issue):
                roots[0] += 1
                mark(issue(), "var_dve")
                dve.wait_ge(sem["root_pool"], roots[0])

            def layer_norm(L, part, st):
                dve.wait_ge(sem[f"ln_{part}_in"], 32 * (L + 1))
                for tc in range(TC):
                    if part == "mix":
                        dve.wait_ge(sem["out_pe"], L * BOTH["out_pe"] + tc + 1)
                    r = xrow[:, tc, :]
                    if part == "mix":
                        link(V.scalar_tensor_tensor(r, r, ALPHA, PS[2 + tc][:, :], ALU.mult, ALU.add))
                    else:
                        dve.wait_ge(sem["acc_dve"], TC * (L + 1))
                        for j in range(TOPK):
                            if j % (TOPK // SUMS) == 0:
                                dve.wait_ge(sem[f"sum{tc}{j * SUMS // TOPK}_in"], 16 * (L + 1))
                            link(V.tensor_tensor(r, r if j else acc[:, tc, :], ysum[tc][:, j, :], ALU.add))
                    V.bn_stats(stats[:, 0:6], r[:, 0:512])
                    link(V.bn_stats(stats[:, 6:12], r[:, 512:1024]))
                    link(V.bn_aggr(mv, stats))
                    roots[0] += 1
                    mark(V.tensor_scalar(var[:, 0:1], mv[:, 1:2], LN_EPS, None, ALU.add), "var_dve")
                    link(V.scalar_tensor_tensor(r, r, mv[:, 0:1], lng, ALU.subtract, ALU.mult))
                    dve.wait_ge(sem["root_pool"], roots[0])
                    mark(V.scalar_tensor_tensor(r, r, root[:, 0:1], lnb, ALU.mult, ALU.add), f"ln{part}_dve")

            def attention(L):
                units = UNITS[L]
                n = len(units)
                for u in range(n + 4):
                    if u < n:
                        U = units[u]
                        w = (U["qc"] + 1) * P
                        s = v(SBUFS[L][u % 2][:, 0:R * w], j=R, k=w)
                        sc = v(PS[u % 2][:, 0:R * w], j=R, k=w)
                        mask = cst[:, U["mask"] + 2 * P - w:U["mask"] + 2 * P]
                        dve.wait_ge(sem["score_pe"], L * BOTH["score_pe"] + u + 1)
                        if u >= 2:
                            dve.wait_ge(sem["ptr_pe"], L * BOTH["ptr_pe"] + u - 1)
                        ins = V.scalar_tensor_tensor(s, sc, U["scale"], mask[:, None, :].to_broadcast([P, R, w]),
                                                     ALU.mult, ALU.add)
                        mark(ins, "max_dve")
                        dve.wait_ge(sem["max_dve"], L * BOTH["max_dve"] + 2 * u + 1)
                        m = nmax[:, u * R:(u + 1) * R]
                        ins = V.tensor_reduce(m, s, AX_X, ALU.max, negate=True)
                        if U["sink"]:
                            link(ins)
                            sk = nsink[:, u % 2 * R:(u % 2 + 1) * R]
                            ins = V.tensor_tensor(m, m, sk, ALU.min)
                            mark(ins, "max_dve")
                            dve.wait_ge(sem["max_dve"], L * BOTH["max_dve"] + 2 * u + 2)
                            mark(V.tensor_tensor(esink[:, u * R:(u + 1) * R], m, sk, ALU.subtract), "sink_dve")
                        else:
                            mark(ins, "max_dve")
                    if u >= 4 and u % 2 == 0 or u == n + 3:
                        pair = (u - 4) // 2 if u < n + 3 else n // 2 - 1
                        if u >= n + 3 or u < n + 3:
                            output(L, pair) if pair not in done[L] else None
                            done[L].add(pair)

            done = [set(), set()]

            def output(L, pair):
                dve.wait_ge(sem["pv_pe"], L * BOTH["pv_pe"] + 2 * pair + 2)
                ob = v(BANK[6 + pair % 2], h=8, d=HD)
                s8 = sums[:, pair * 8:pair * 8 + 8]
                r8 = rec[:, pair % 2 * 8:pair % 2 * 8 + 8]
                if L:
                    qc, part = pair // 2, pair % 2 * 512
                else:
                    qc, part = pair % 2, 0 if pair < 2 else 512
                if L == 0 and pair < 2:
                    dve.wait_ge(sem["sink_act"], 1)
                    link(V.tensor_tensor(s8, s8, esink[:, pair * 8:pair * 8 + 8], ALU.add))
                link(V.reciprocal(r8, s8))
                if L == 0 and pair >= 2:
                    gt = gates[:, qc * NGATE + 8 * (pair // 2):qc * NGATE + 8 * (pair // 2) + 8]
                    link(V.tensor_tensor(r8, r8, gt, ALU.mult))
                dst = v(atto[L][:, qc, part:part + 512], h=8, d=HD)
                rb = r8[:, :, None].to_broadcast([P, 8, HD])
                if L == 0 and pair >= 2:
                    o = v(tmp[:, 0:512], h=8, d=HD)
                    link(V.tensor_tensor(o, ob, rb, ALU.mult))
                    mark(V.tensor_tensor(dst, dst, o, ALU.add), "o_dve")
                    dve.wait_ge(sem["o_dve"], L * BOTH["o_dve"] + pair + 1)
                else:
                    mark(V.tensor_tensor(dst, ob, rb, ALU.mult), "o_dve")

            def routing(L):
                dve.wait_ge(sem["sig_act"], L * BOTH["sig_act"] + 1)
                dve.wait_ge(sem["router_in"], L * BOTH["router_in"] + 32)
                link(V.tensor_scalar(rs, rs, 1.0, None, ALU.add))
                link(V.reciprocal(rs, rs))
                link(V.tensor_tensor(rsb, rs, rbias[:, None, :].to_broadcast([P, TC, NE]), ALU.add))
                for tc in range(TC):
                    for g in range(NG):
                        ins = V.max(top8[:, tc, g, :], rsb[:, tc, g * EPG:(g + 1) * EPG])
                V.memset(esc[:, :, NE:], LOWEST)
                V.memset(gsc[:, :, NG:], LOWEST)
                link(ins)
                link(V.tensor_tensor(gsc[:, :, 0:NG], top8[:, :, :, 0], top8[:, :, :, 1], ALU.add))
                for tc in range(TC):
                    ins = V.max(m8[:, tc, :], gsc[:, tc, 0:NG])
                link(ins)
                link(V.memset(m8[:, :, TOPG:], LOWEST))
                for tc in range(TC):
                    ins = V.match_replace(gpick[:, tc, :], m8[:, tc, :], gsc[:, tc, :], PICKED)
                link(ins)
                link(V.tensor_scalar(gsel, gpick[:, :, 0:NG], PICKED / 2, None, ALU.is_ge))
                link(V.tensor_scalar(gneg, gsel, 1.0, -NEG, ALU.subtract, ALU.mult))
                for tc in range(TC):
                    e3 = v(esc[:, tc, 0:NE], g=NG, k=EPG)
                    V.tensor_tensor(e3, v(rsb[:, tc, :], g=NG, k=EPG), gsel[:, tc, :, None].to_broadcast([P, NG, EPG]), ALU.mult).then_inc(sem["dve_chain"], 1)
                    chain[0] += 1
                dve.wait_ge(sem["dve_chain"], chain[0])
                for tc in range(TC):
                    e3 = v(esc[:, tc, 0:NE], g=NG, k=EPG)
                    ins = V.tensor_tensor(e3, e3, gneg[:, tc, :, None].to_broadcast([P, NG, EPG]), ALU.add)
                link(ins)
                for tc in range(TC):
                    ins = V.max(m8[:, tc, :], esc[:, tc, 0:NE])
                link(ins)
                link(V.memset(m8[:, :, TOPK:], LOWEST))
                for tc in range(TC):
                    ins = V.match_replace(epick[:, tc, :], m8[:, tc, :], esc[:, tc, :], PICKED)
                link(ins)
                link(V.tensor_scalar(sel, epick[:, :, 0:NE], PICKED / 2, None, ALU.is_ge))
                link(V.tensor_tensor(gate, sel, rs, ALU.mult))
                link(V.tensor_reduce(gsum, gate, AX_X, ALU.add))
                link(V.reciprocal(gsum, gsum))
                for tc in range(TC):
                    ins = V.tensor_scalar(gate[:, tc, :], gate[:, tc, :], gsum[:, tc:tc + 1], ROUTED_SCALE, ALU.mult, ALU.mult)
                mark(ins, "gate_dve")
                dve.wait_ge(sem["gate_dve"], L * BOTH["gate_dve"] + 1)

            def moe(L):
                for tc in range(TC):
                    dve.wait_ge(sem["ssilu_act"], TC * L + tc + 1)
                    mark(V.tensor_tensor(shh[tc], ssg[tc], BANK[tc][:, DE:2 * DE], ALU.mult), "sh_dve")
                dve.wait_ge(sem["rank_pe"], L + 1)
                link(V.tensor_reduce(most, BANK[2][:, 2 * NE:3 * NE], AX_X, ALU.max))
                link(V.tensor_tensor(over, most.to_broadcast([P, 3]), mcon[:, M_PASS:M_PASS + 3], ALU.is_gt))
                link(V.tensor_reduce(most, over, AX_X, ALU.add))
                mark(V.tensor_scalar(more_groups[:, :], most, float(GROUPS), None, ALU.mult), "groups_dve")
                link(V.scalar_tensor_tensor(rank, v(BANK[2][:, 0:2 * NE], t=TC, e=NE), 1.0, sel, ALU.add, ALU.mult))
                mark(V.tensor_scalar(rank, rank, 1.0, None, ALU.subtract), "rank_dve")
                src = sel
                for i in range(6):
                    w, dst = 1 << i, pre[i % 2]
                    V.tensor_copy(dst[:, :, 0:w], src[:, :, 0:w])
                    link(V.tensor_tensor(dst[:, :, w:], src[:, :, w:], src[:, :, 0:NE - w], ALU.add))
                    src = dst
                link(V.tensor_tensor(pre[0], src, sel, ALU.subtract))
                tok = mcon[:, M_TOK:M_TOK + TC]
                V.tensor_copy(table[:, :, :, 0], gate)
                for tc in range(TC):
                    ins = V.tensor_scalar(table[:, tc, :, 1], pre[0][:, tc, :], float(S), tok[:, tc:tc + 1], ALU.mult, ALU.add)
                link(ins)
                settle("rank_dve")

                def pick(n, k, early):
                    if not early:
                        dve.wait_ge(sem[f"slots_pe{L}"], pairs_before(n, k) - 1)
                    iota = mcon[:, None, None, bass.ds(n // NE * CAP + M_IOTA, CAP)]
                    mine = rank[:, :, bass.ds(n % NE, 2), None]
                    V.tensor_tensor(onehot[k // 2 % 2], iota.to_broadcast([P, TC, 2, CAP]), mine.to_broadcast([P, TC, 2, CAP]),
                                    ALU.is_equal).then_inc(sem[f"pick_dve{L}"], 1)

                def gates_in(n, k, early):
                    dve.wait_ge(sem[f"slots_pe{L}"], pairs_before(n, k) + 1)
                    if not early:
                        dve.wait_ge(sem[f"yd_dve{L}"], n - 2)
                    for e in range(2):
                        ins = V.tensor_copy(gslot[:, (k + e) % NSLOT, :], BANK[5][CAP * e:CAP * e + CAP, 2 * e:2 * e + 2])
                    ins.then_inc(sem[f"gates_dve{L}"], 1)

                def low(n, k, j):
                    dve.wait_ge(sem[f"hi_act{L}"], n * NCHUNK + j + 1)
                    part = slot[k % NSLOT][:, 0:2 * KC * DE].rearrange("p (m c f) -> p c m f", m=2, c=KC)
                    c = slice(j * KC // NCHUNK, (j + 1) * KC // NCHUNK)
                    hi = whi[:, j * CW:(j + 1) * CW].bitcast(F32).rearrange("p (c m f) -> p c m f", m=2, f=DE)
                    V.tensor_tensor(wlo[:, j * CW:(j + 1) * CW].rearrange("p (c m f) -> p c m f", m=2, f=DE),
                                    part[:, c], hi, ALU.subtract).then_inc(sem[f"lo_dve{L}"], 1)

                def x_low(n, k):
                    dve.wait_ge(sem[f"xhi_act{L}"], pairs_before(n, k) + 1)
                    V.tensor_tensor(xe[:, :, :, CAP:2 * CAP].rearrange("p e c s -> p c e s"),
                                    PS[0][:, :].rearrange("p (c e s) -> p c e s", c=KC, e=2),
                                    xe[:, :, :, 0:CAP].bitcast(F32).rearrange("p e c s -> p c e s"), ALU.subtract)\
                        .then_inc(sem[f"xlo_dve{L}"], 1)

                def y_half(n, k):
                    dve.wait_ge(sem[f"down_pe{L}"], n + 1)
                    V.tensor_scalar(half_rows(rows_u, k), gslot[:, k, 1:2], NOWHERE, None, ALU.add)
                    V.tensor_copy(half_rows(ys, k)[:, 512:1024], PS[3][0:CAP, 512:1024]).then_inc(sem[f"yd_dve{L}"], 1)

                pick(0, 0, True)
                pick(2, 2, True)
                for tc in range(TC):
                    dve.wait_ge(sem["sdown_pe"], TC * L + tc + 1)
                    V.scalar_tensor_tensor(acc[:, tc, :], xrow[:, tc, :], ALPHA, PS[2 + tc][:, :], ALU.mult, ALU.add)\
                        .then_inc(sem["acc_dve"], 1)
                for j in range(NCHUNK):
                    low(0, 0, j)
                x_low(0, 0)
                gates_in(0, 0, True)

                def step(n, k, have):
                    if k % 2 == 0 and have(4):
                        pick(n + 4, k + 4, False)
                    if have(1):
                        low(n + 1, k + 1, 0)
                    dve.wait_ge(sem[f"top_act{L}"], n + 1)
                    if have(-1):
                        dve.wait_ge(sem[f"silu_act{L}"], n)
                        dve.wait_ge(sem[f"h_dve{L}"], n)
                    V.tensor_tensor(gusum, BANK[2 + k % 2][CAP:2 * CAP, :], gutop, ALU.add).then_inc(sem[f"sum_dve{L}"], 1)
                    if have(1):
                        low(n + 1, k + 1, 1)
                    dve.wait_ge(sem[f"silu_act{L}"], n + 1)
                    dve.wait_ge(sem[f"gates_dve{L}"], pairs_before(n, k) + 1)
                    if have(-2):
                        dve.wait_ge(sem[f"ht_pe{L}"], n - 1)
                    V.scalar_tensor_tensor(hh[k % 2], sg, gslot[:, k, 0:1], gusum[:, DE:2 * DE],
                                           ALU.mult, ALU.mult).then_inc(sem[f"h_dve{L}"], 1)
                    if have(1):
                        if k % 2:
                            x_low(n + 1, k + 1)
                        low(n + 1, k + 1, 2)
                        low(n + 1, k + 1, 3)
                        if k % 2:
                            gates_in(n + 1, k + 1, not have(-3))
                    if have(-4):
                        dve.wait_ge(sem[f"scatter{k // 2}_out{L}"], uses_before(n, k) * 16)
                    if have(-1):
                        y_half(n - 1, (k - 1) % NSLOT)

                n_groups = steps(dve, L, step)
                y_half(n_groups * NSLOT - 1, 3)

            dve.wait_ge(sem["x_in"], 32)
            mark(V.tensor_scalar(nsink, sinkb, -1.0, None, ALU.mult), "sink_dve")
            columns(0)
            hv = [v(h, k=2, n=32)[:, :, 0:G * NCMP] for h in hidw]

            def windows():
                dve.wait_ge(sem["kcv_act"], 2)
                dve.wait_ge(sem["pet_act"], 1)
                for i in range(2):
                    for lh in range(2):
                        for g in range(G):
                            src = kcv[0:HD, 2 * i + g, lh * 16:lh * 16 + NCMP * CMP_STRIDE]\
                                .rearrange("p (n l) -> p l n", l=CMP_STRIDE)
                            pos = pet[0:HD, i, lh * 16:(lh + 1) * 16]
                            mark(V.tensor_tensor(blk[i][HD * lh:HD * lh + HD, :, g, :], src,
                                                 pos[:, :, None].to_broadcast([HD, 16, NCMP]), ALU.add), "blk_dve")

            def gelu_inner():
                dve.wait_ge(sem["hid_act"], 1)
                link(V.tensor_tensor(hv[1], hv[0], hv[0], ALU.mult))
                link(V.tensor_scalar(hv[1], hv[1], 0.044715, 1.0, ALU.mult, ALU.add))
                mark(V.tensor_tensor(hv[2], hv[1], hv[0], ALU.mult), "gin_dve")

            def gelu_outer():
                dve.wait_ge(sem["gexp_act"], 1)
                link(V.tensor_scalar(hv[4], hv[3], 1.0, None, ALU.add))
                link(V.reciprocal(hv[4], hv[4]))
                mark(V.tensor_tensor(hv[5], hv[0], hv[4], ALU.mult), "gelu_dve")

            same = lambda a: a
            by_group = lambda a: a.rearrange("p (g j) d -> p g j d", g=G)

            def tables(tc):
                return cst[:, K_COS + tc * HD:K_COS + (tc + 1) * HD], cst[:, K_SIN + tc * HD:K_SIN + (tc + 1) * HD]

            def out_q(tc, b):
                o = rope[:, tc, b * P:(b + R) * P].rearrange("p (j g d) -> p g j d", j=R, g=G)
                return o[:, :, :, 0:HALF], o[:, :, :, HALF:HD]

            def out_k(tc, b):
                o = v(rope[:, tc, b * P:(b + 1) * P], g=G, d=HD)
                return o[:, :, 0:HALF], o[:, :, HALF:HD]

            def copied(i):
                dve.wait_ge(sem["proj_act0"], i)
                dve.wait_ge(sem["proj_dve0"], i)

            for i, n in enumerate(PARTS0):
                dve.wait_ge(sem["proj_pe0"], 2 * i + 2)
                mark(V.tensor_copy(qkv[:, 1, n * 512:(n + 1) * 512], BANK[2 * n + 1]), "proj_dve0")
                if n == 0:
                    windows()
                if n == 1:
                    copied(3)
                    for tc in range(TC):
                        apply_rope(v(qkv[:, tc, C_QA:C_VA], h=10, d=HD),
                                   [(0, 8, out_q(tc, 0), by_group), (8, 10, out_k(tc, 4), same)], *tables(tc), 10, HALF)
                        if tc == 1:
                            gelu_inner()
                        apply_rope(v(qkv[:, tc, C_QB:C_KC], h=8, d=HD), [(0, 8, out_q(tc, 5), by_group)],
                                   *tables(tc), 8, HALF)
                    gelu_outer()
            copied(4)
            for tc in range(TC):
                apply_rope(v(qkv[:, tc, C_KS:C_VS], h=2, d=HD), [(0, 2, out_k(tc, 9), same)], *tables(tc), 2, HALF)
                apply_rope(v(qkv[:, tc, C_KW:C_VW], h=2, d=HD), [(0, 2, out_k(tc, 10), same)], *tables(tc), 2, HALF,
                           "rope_dve0")
            dve.wait_ge(sem["gates_act"], 1)
            link(V.tensor_scalar(gates, gates, 1.0, None, ALU.add))
            link(V.reciprocal(gates, gates))
            dve.wait_ge(sem["kv2_pe"], 1)
            dve.wait_ge(sem["zero_pool"], 2)
            cos, sin = cst[0:NCMP, K_CCOS:K_CCOS + HD], cst[0:NCMP, K_CSIN:K_CSIN + HD]
            ck = v(kcn[0:NCMP, :], g=G, d=HD)
            apply_rope(v(BANK[1][0:NCMP, 128:256], g=G, d=HD),
                       [(0, 2, (ck[:, :, 0:HALF], ck[:, :, HALF:HD]), same)], cos, sin, 2, HALF, "kcn_dve")
            for g in range(G):
                for j in range(R):
                    ins = V.tensor_copy(vbd[g][32 * j:32 * j + NCMP, j, :], BANK[1][0:NCMP, 256 + g * HD:256 + (g + 1) * HD])
            mark(ins, "vbd_dve")
            dve.wait_ge(sem["kct_pe"], 1)
            mark(V.tensor_copy(kcmpt, BANK[0][:, 0:NCMP]), "kct_dve")
            dve.wait_ge(sem["csc_pe"], 1)
            c8 = cs[:, :, :, 0:NCMP]
            for tc in range(TC):
                add = cst[:, K_CADD + tc * NCMP:K_CADD + (tc + 1) * NCMP]
                for g in range(G):
                    sc = v(BANK[(0, 5)[g]][:, 0:128], t=TC, j=R, n=16)
                    ins = V.scalar_tensor_tensor(c8[:, tc, g * R:(g + 1) * R, :], sc[:, tc, :, 0:NCMP], HD ** -0.5,
                                                 add[:, None, :].to_broadcast([P, R, NCMP]), ALU.mult, ALU.add)
            link(ins)
            cm = v(crec, t=TC, h=8)
            link(V.tensor_reduce(cm, c8, AX_X, ALU.max))
            mark(V.tensor_tensor(c8, c8, cm[:, :, :, None].to_broadcast([P, TC, 8, NCMP]), ALU.subtract), "csub_dve")
            dve.wait_ge(sem["cexp_act"], 1)
            for tc in range(TC):
                mul = cst[:, K_CMUL + tc * NCMP:K_CMUL + (tc + 1) * NCMP]
                ins = V.tensor_tensor(cp[:, tc, :, 0:NCMP], c8[:, tc], mul[:, None, :].to_broadcast([P, 8, NCMP]), ALU.mult)
            mark(ins, "cp_dve")
            dve.wait_ge(sem["cp_dve"], 1)
            link(V.tensor_reduce(cm, cp[:, :, :, 0:NCMP], AX_X, ALU.add))
            link(V.tensor_scalar(crec, crec, 1e-30, None, ALU.max))
            link(V.reciprocal(crec, crec))
            link(V.tensor_tensor(cm, cm, v(gates, t=TC, n=NGATE)[:, :, 0:8], ALU.mult))
            dve.wait_ge(sem["csc_pe"], 2)
            for tc in range(TC):
                ins = V.tensor_tensor(v(atto[0][:, tc, 512:1024], h=8, d=HD), v(BANK[4 + tc], h=8, d=HD),
                                      cm[:, tc, :, None].to_broadcast([P, 8, HD]), ALU.mult)
            mark(ins, "cmp_dve")
            settle("cmp_dve")
            attention(0)
            columns(1)
            layer_norm(0, "mix", 2)
            columns(2)
            routing(0)
            moe(0)
            layer_norm(0, "ffn", 3)
            columns(3)
            dve.wait_ge(sem["small1_in"], 32)
            for tc in range(TC):
                dve.wait_ge(sem["proj_act1"], tc + 1)
                parts = ((0, QL), (QL, QL + KVL))
                link(V.tensor_tensor(tmp[:, 0:QL + KVL], c1[:, tc, 0:QL + KVL], c1[:, tc, 0:QL + KVL], ALU.mult))
                for i, (a, b) in enumerate(parts):
                    link(V.tensor_reduce(ssq[:, i:i + 1], tmp[:, a:b], AX_X, ALU.add))
                a, b = parts[0]
                link(V.tensor_scalar(var[:, 0:1], ssq[:, 0:1], 1.0 / (b - a), RMS_EPS, ALU.mult, ALU.add))
                a, b = parts[1]
                inverse_root(lambda: V.tensor_scalar(var[:, 1:2], ssq[:, 1:2], 1.0 / (b - a), RMS_EPS, ALU.mult, ALU.add))
                for i, (a, b) in enumerate(parts):
                    r = c1[:, tc, a:b]
                    link(V.tensor_scalar(r, r, root[:, i:i + 1], None, ALU.mult))
                    ins = V.tensor_tensor(r, r, lnp[:, a:b], ALU.mult)
                mark(ins, "rms_dve")
            for tc in range(TC):
                cos = cst[:, K_COS1 + tc * ROPE:K_COS1 + (tc + 1) * ROPE]
                sin = cst[:, K_SIN1 + tc * ROPE:K_SIN1 + (tc + 1) * ROPE]
                o = v(c1[:, tc, QL + KVL:IN1], h=1, d=ROPE)
                apply_rope(o, [(0, 1, (o[:, :, 0:16], o[:, :, 16:32]), same)], cos, sin, 1, 16, "krope_dve")
            dve.wait_ge(sem["krt_act"], 1)
            mark(V.tensor_copy(kt1[NOPE:DQK, :, :], krt[:, None, :].to_broadcast([ROPE, MH, S])), "kfull_dve")
            for tc in range(TC):
                dve.wait_ge(sem["q_act"], 3 * tc + 3)
                cos = cst[:, K_COS1 + tc * ROPE:K_COS1 + (tc + 1) * ROPE]
                sin = cst[:, K_SIN1 + tc * ROPE:K_SIN1 + (tc + 1) * ROPE]
                o = v(qn1[:, tc, :], h=MH, d=DQK)[:, :, NOPE:DQK]
                apply_rope(o, [(0, MH, (o[:, :, 0:16], o[:, :, 16:32]), same)], cos, sin, MH, 16, "qrope_dve")
            attention(1)
            columns(4)
            layer_norm(1, "mix", 5)
            columns(5)
            routing(1)
            moe(1)
            layer_norm(1, "ffn", 6)


_INS = ['x', 'swa_nsa_w_in', 'swa_sinks', 'nsa_cmp_pe_k', 'nsa_cmp_k_w1', 'nsa_cmp_k_w2', 'nsa_cmp_pe_v',
        'nsa_cmp_v_w1', 'nsa_cmp_v_w2', 'swa_nsa_w_out', 'mla_w_in', 'mla_q_norm', 'mla_kv_norm', 'mla_w_uq',
        'mla_w_ukv', 'mla_w_out', 'ln_mix_g', 'ln_mix_b', 'ln_ffn_g', 'ln_ffn_b', 'router_w', 'router_bias',
        'expert_w_gate', 'expert_w_up', 'expert_w_down', 'shared_w_gate', 'shared_w_up', 'shared_w_down']


def kernel(**inputs):
    import concourse.bacc as bacc
    from concourse.bass_utils import run_bass_kernel_spmd

    nc = bacc.Bacc("TRN2", target_bir_lowering=False, num_devices=1)
    arrays, args = {}, []
    for name in _INS + ["constants", "mixture_constants"]:
        if name == "constants":
            a = constants()
        elif name == "mixture_constants":
            a = mixture_constants()
        else:
            a = np.ascontiguousarray(inputs[name])
        arrays[f"in_{name}"] = a
        args.append(nc.dram_tensor(f"in_{name}", a.shape, mybir.dt.from_np(a.dtype), kind="ExternalInput").ap())
    out = nc.dram_tensor("out_0", (1, S, D), F32, kind="ExternalOutput").ap()
    bass_hybrid_block(nc, *args, out)
    r = run_bass_kernel_spmd(nc, [arrays], core_ids=[0])
    return r.results[0]["out_0"]
```

```python
from contextlib import ExitStack

import numpy as np

import concourse.bass as bass
from concourse import mybir

F32 = mybir.dt.float32
F32R = mybir.dt.float32r
U32 = mybir.dt.uint32
ALU = mybir.AluOpType
ACT = mybir.ActivationFunctionType
AX_X = mybir.AxisListType.X

P = 128
S, D = 256, 1024
TC = S // P
KC = D // P
HD, HALF = 64, 32
G, R = 2, 4
MIX0 = (512, 128, 128, 512, 128, 128, 128, 128, 128, 128, 24)
COL = [int(c) for c in np.cumsum((0,) + MIX0)]
(C_QA, C_KA, C_VA, C_QB, C_KC, C_VC, C_KS, C_VS, C_KW, C_VW, C_GT) = COL[:11]
IN0 = COL[11]
NGATE = MIX0[10]
CMP_LEN, CMP_STRIDE, CMP_HID = 32, 16, 128
NCMP = (S - CMP_LEN) // CMP_STRIDE + 1
WINDOW = 128
MH, NOPE, ROPE, MV = 16, 64, 32, 64
DQK = NOPE + ROPE
QL, KVL = 384, 256
IN1 = QL + KVL + ROPE
NE, NG, EPG, TOPG, TOPK, DE = 64, 8, 8, 4, 6, 256
ROUTED_SCALE = 2.5
LN_EPS, RMS_EPS = 1e-5, 1e-6
ALPHA = (2 * 2) ** 0.25
THETA = 10000.0
NEG = -1e30
LOWEST, PICKED = -3e38, 3e38
GELU_C = 2.0 * float(np.sqrt(2.0 / np.pi))
NSLOT = 4
SUMS = 3
NPAIR = NSLOT // 2
SLOT = 3 * D * DE // P

K_ID, K_CAUSAL, K_SWA, K_COS, K_SIN = 0, 128, 384, 640, 768
K_COS1, K_SIN1, K_CCOS, K_CSIN, K_CADD, K_CMUL = 896, 960, 1024, 1088, 1152, 1182
NCONST = 1212


CAP = 64
M_BEFORE, M_ONES, M_IOTA, M_TOK, M_PASS = 0, 128, 256, 576, 578
NMOEC = 581
NOWHERE = 4096.0
NCHUNK = 4
CW = 2 * KC * DE // NCHUNK
GROUPS = NE // NSLOT


def mixture_constants():
    c = np.zeros((P, NMOEC), np.float32)
    c[:, M_BEFORE:M_BEFORE + P] = np.arange(P)[:, None] < np.arange(P)[None, :]
    c[:, M_ONES:M_ONES + P] = 1.0
    c[:, M_IOTA:M_IOTA + 320] = np.arange(320)[None, :]
    c[:, M_TOK:M_TOK + TC] = np.arange(P)[:, None] + P * np.arange(TC)[None, :] - NOWHERE
    c[:, M_PASS:M_PASS + 3] = CAP * np.arange(1, 4)[None, :]
    return c


def constants():
    c = np.zeros((P, NCONST), np.float32)
    q = np.arange(P)[:, None]
    k = np.arange(P)[None, :]
    c[:, K_ID:K_ID + P] = np.eye(P)
    c[:, K_CAUSAL + P:K_CAUSAL + 2 * P] = np.where(k <= q, 0.0, NEG)
    c[:, K_SWA:K_SWA + P] = np.where(k > q, 0.0, NEG)
    c[:, K_SWA + P:K_SWA + 2 * P] = np.where(k <= q, 0.0, NEG)

    def table(pos, d):
        inv = np.float32(THETA) ** (np.float32(-2.0) * np.arange(d // 2, dtype=np.float32) / np.float32(d))
        ang = pos.astype(np.float32)[:, None] * inv.astype(np.float32)[None, :]
        return np.tile(np.cos(ang), 2), np.tile(np.sin(ang), 2)

    for tc in range(TC):
        pos = np.arange(tc * P, tc * P + P)
        for (kc, ks), d in (((K_COS, K_SIN), HD), ((K_COS1, K_SIN1), ROPE)):
            cos, sin = table(pos, d)
            c[:, kc + tc * d:kc + tc * d + d] = cos
            c[:, ks + tc * d:ks + tc * d + d] = sin
    cos, sin = table(np.arange(NCMP) * CMP_STRIDE + CMP_LEN - 1, HD)
    c[:NCMP, K_CCOS:K_CCOS + HD] = cos
    c[:NCMP, K_CSIN:K_CSIN + HD] = sin
    end = np.arange(NCMP) * CMP_STRIDE + CMP_LEN - 1
    for tc in range(TC):
        seen = end[None, :] <= (np.arange(P) + tc * P)[:, None]
        c[:, K_CADD + tc * NCMP:K_CADD + (tc + 1) * NCMP] = np.where(seen, 0.0, NEG)
        c[:, K_CMUL + tc * NCMP:K_CMUL + (tc + 1) * NCMP] = seen
    return c


BOTH = dict(
    ln_mix_in=32, ln_ffn_in=32, wout_in=16, shared_in=48, router_in=32, moec_in=16, qk_pe=6, qk_act=6, score_pe=12,
    max_dve=24, exp_act=12, ptr_pe=12, ptr_act=12, pv_pe=12, o_dve=4, norm_dve=12, out_pe=2, lnmix_dve=2, lnffn_dve=2,
    logit_pe=1, sig_act=1, gate_dve=1, sgu_pe=2, ssilu_act=2, sh_dve=2, sht_pe=2, sht_act=2, sdown_pe=2,
    rank_pe=1, rank_dve=1, groups_dve=1, acc_dve=2, **{f"sum{tc}{j}_in": 16 for tc in range(TC) for j in range(SUMS)}, xt_pe=8, xt_act=6, xt_dve=2)
EACH = ["pick_dve", "slots_pe", "gates_dve", "gather_pe", "xhi_act", "xlo_dve",
        "hi_act", "lo_dve", "gu_pe", "top_act", "sum_dve", "silu_act", "h_dve", "ht_pe", "ht_act", "down_pe",
        "ya_act", "yd_dve"] + [f"scatter{k}_out" for k in range(NPAIR)] + [f"{part}{k}_in" for part in ("gu", "dn") for k in range(NSLOT)]
SEMS = (
    ["const_in", "x_in", "cmpw_in", "small1_in"]
    + [f"win_in{c}" for c in range(4)]
    + list(BOTH) + [f"{n}{L}" for L in range(2) for n in EACH]
    + ["proj_pe0", "proj_act0", "proj_dve0", "rope_dve0", "proj_pe1", "proj_act1",
       "pet_pe", "pet_act", "gates_pe", "gates_act", "kcv_pe", "kcv_act", "blk_dve",
       "hid_pe", "hid_act", "gelu_dve", "gin_dve", "gexp_act", "kv2_pe", "kcn_dve", "kct_pe", "kct_dve",
       "vbd_dve", "zero_pool", "csc_pe", "csub_dve", "cexp_act", "cp_dve", "cpt_pe", "cpt_act",
       "sink_dve", "win1_in", "wuq_in", "wukv_in",
       "var_dve", "root_pool", "power_pool", "rms_dve", "cnt_pe", "cnt_act", "q_pe", "q_act", "kv_pe", "kv_act",
       "krope_dve", "krt_pe", "krt_act", "qrope_dve", "kfull_dve", "dve_chain", "out_done"]
)


def bass_hybrid_block(nc, x, w_in0, sinks, pe_k, ck1, ck2, pe_v, cv1, cv2, w_out0, w_in1, q_norm,
                      kv_norm, w_uq, w_ukv, w_out1, ln_mix_g, ln_mix_b, ln_ffn_g, ln_ffn_b,
                      router_w, router_bias, e_gate, e_up, e_down, s_gate, s_up, s_down, const, moe_const, out):
    ctx = ExitStack()
    with ctx:
        def sb(name, cols):
            return ctx.enter_context(nc.sbuf_tensor(name, [P, cols], F32))

        sem = {n: ctx.enter_context(nc.semaphore(n)) for n in SEMS}
        cst = sb("cst", NCONST)
        xn = sb("x_rows", TC * D)
        at_room = (nc.sbuf_base + 31) // 32 * 32
        room = sb("room", KC * S + 8 * D)
        xt, wbig = room[:, 0:KC * S], room[:, KC * S:KC * S + 8 * D]
        xe = nc.alloc_sbuf_tensor_at("x_parts", [P, 2 * KC * P], F32R, offset=at_room)\
            .rearrange("p (e c m) -> p e c m", e=2, c=KC)
        whi = nc.alloc_sbuf_tensor_at("w_high", [P, 2 * KC * DE], F32R, offset=at_room + 8192)
        wlo = nc.alloc_sbuf_tensor_at("w_low", [P, 2 * KC * DE], F32R, offset=at_room + 8192 + 16384)
        ring = sb("ring", NSLOT * SLOT)
        lnp = sb("lnp", 2 * D)
        arena = sb("arena", 10800)
        tmp = sb("tmp", 1280)
        rw = sb("rw", KC * NE)
        rbias = sb("rbias", NE)
        small = sb("small", 256)

        PS = [ctx.enter_context(nc.psum_tensor(f"psum{i}", [P, 1024], F32)) for i in range(4)]
        BANK = [PS[i // 2][:, 512 * (i % 2):512 * (i % 2) + 512] for i in range(8)]

        def v(ap, **k):
            names = list(k)
            return ap.rearrange("p (" + " ".join(names) + ") -> p " + " ".join(names), **k)

        ident = cst[:, K_ID:K_ID + P]
        xrow = v(xn[:, :], t=TC, d=D)
        xcol = v(xt, c=KC, t=S)
        slot = [ring[:, i * SLOT:(i + 1) * SLOT] for i in range(NSLOT)]
        lng, lnb = lnp[:, 0:D], lnp[:, D:2 * D]
        wout = v(wbig, c=KC, d=D)

        def expert(w):
            gu = w[:, 0:2 * KC * DE].rearrange("p (m c f) -> p c m f", m=2, c=KC)
            return gu, w[:, 2 * KC * DE:SLOT].rearrange("p (c d) -> p c d", c=DE // P)

        at = [0]

        def take(n):
            at[0] += n
            return small[:, at[0] - n:at[0]]

        stats, mv = take(12), take(2)
        var, root, power = take(2), take(2), take(2)
        gates = take(TC * NGATE)
        nmax = take(12 * R)
        sums = take(12 * R)
        rec = take(16)
        nsink, sinkb = take(8), take(8)
        esink = take(16)
        kcmpt = take(G * NCMP)
        ssq = take(4)

        qkv = v(arena[:, 0:TC * IN0], t=TC, n=IN0)
        a0 = TC * IN0
        NB = 11
        rope = v(arena[:, a0:a0 + TC * NB * P], t=TC, n=NB * P)
        s0 = [arena[:, a0:a0 + 1024], arena[:, a0 + 1024:a0 + 2048], slot[3][:, 2048:3072]]
        a1 = a0 + TC * NB * P
        qkt = v(arena[:, a1:a1 + NB * S], b=NB, t=S)
        a2 = a1 + NB * S
        kcv = v(arena[:, a2:a2 + 4 * S], b=4, t=S)
        pt0 = arena[:, a2:a2 + 1024]
        gate_cols = arena[0:NGATE, a2:a2 + S]
        last = slot[3]
        cw1 = [v(last[:, i * 2048:(i + 1) * 2048], l=16, h=CMP_HID) for i in range(2)]
        b0 = 4096
        cw2 = [last[:, b0 + i * HD:b0 + (i + 1) * HD] for i in range(2)]
        pen = last[:, b0 + 128:b0 + 256]
        pet = v(last[:, b0 + 256:b0 + 320], k=2, l=CMP_LEN)
        blk = [last[:, b0 + 320 + i * 480:b0 + 800 + i * 480].rearrange("p (l g n) -> p l g n", l=16, g=G) for i in range(2)]
        vbd = [v(last[:, i * 256:(i + 1) * 256], j=R, d=HD) for i in range(2)]
        cs = v(last[:, 512:512 + 256], t=TC, h=8, n=16)
        cp = v(last[:, 768:768 + 512], t=TC, h=8, n=32)
        cpt = v(last[:, 1280:1280 + 512], u=4, q=P)
        kcn = last[:, 1792:1792 + 128]
        cu = last[:, 1920:2048]
        hidw = [last[:, 5376 + i * 64:5376 + (i + 1) * 64] for i in range(6)]
        crec = last[:, 5760:5776]

        uq = v(slot[0][:, 0:QL // P * MH * DQK], c=QL // P, n=MH * DQK)
        ukv = v(slot[1][:, 0:KVL // P * MH * 128], c=KVL // P, n=MH * 128)
        win1 = v(slot[2][:, 0:KC * IN1], c=KC, n=IN1)
        qn1 = v(slot[2][:, 0:TC * MH * DQK], t=TC, n=MH * DQK)
        qt1 = v(slot[3][:, 0:MH * S], h=MH, t=S)
        c1 = v(slot[3][:, MH * S:MH * S + TC * IN1], t=TC, n=IN1)
        kt1 = v(arena[:, 0:MH * S], h=MH, t=S)
        kv1 = v(arena[:, MH * S:MH * S + TC * MH * 128], t=TC, n=MH * 128)
        e0 = MH * S + TC * MH * 128
        ct1_flat = arena[:, e0:e0 + 5 * S]
        ct1 = v(ct1_flat, c=5, t=S)
        RMS_PARTS = ((0, QL), (QL, QL + KVL))
        pt1 = arena[:, e0 + 5 * S:e0 + 5 * S + 1024]
        krt = arena[0:ROPE, e0 + 5 * S + 1024:e0 + 5 * S + 1024 + S]
        s1 = [xt[:, 0:1024], xt[:, 1024:2048], arena[:, e0:e0 + 1024]]
        attot = [xcol, v(slot[3][:, MH * S:MH * S + TC * D], c=KC, t=S)]

        acc = v(arena[:, 0:TC * D], t=TC, d=D)
        ys = [arena[:, 2048 + i * D:2048 + (i + 1) * D] for i in range(NPAIR)]
        shh = [arena[:, 2048 + i * DE:2048 + (i + 1) * DE] for i in range(2)]
        ssg = [arena[:, 2560 + i * DE:2560 + (i + 1) * DE] for i in range(2)]
        sht = [v(arena[:, 3072 + i * 256:3328 + i * 256], c=2, t=P) for i in range(2)]
        shared_down = arena[:, 4096:4096 + DE // P * D]
        hh = [arena[0:CAP, 6144 + i * DE:6144 + (i + 1) * DE] for i in range(2)]
        ht = [v(arena[:, 6656 + i * 128:6656 + (i + 1) * 128], c=2, t=CAP) for i in range(2)]
        sg = arena[0:CAP, 6912:6912 + DE]
        gutop = arena[0:CAP, 7168:7680]
        gusum = arena[0:CAP, 7680:8192]
        M0 = 8192
        gate = v(arena[:, M0:M0 + TC * NE], t=TC, e=NE)
        rs = v(arena[:, M0 + 128:M0 + 256], t=TC, e=NE)
        rsb = v(arena[:, M0 + 256:M0 + 384], t=TC, e=NE)
        top8 = arena[:, M0 + 384:M0 + 512].rearrange("p (t g k) -> p t g k", t=TC, g=NG)
        gsc = v(arena[:, M0 + 512:M0 + 544], t=TC, k=16)
        gpick = v(arena[:, M0 + 544:M0 + 576], t=TC, k=16)
        gsel = v(arena[:, M0 + 576:M0 + 592], t=TC, k=NG)
        gneg = v(arena[:, M0 + 592:M0 + 608], t=TC, k=NG)
        m8 = v(arena[:, M0 + 608:M0 + 624], t=TC, k=8)
        esc = v(arena[:, M0 + 640:M0 + 784], t=TC, k=72)
        epick = v(arena[:, M0 + 784:M0 + 928], t=TC, k=72)
        gsum = arena[:, M0 + 928:M0 + 930]
        most, over = arena[:, M0 + 930:M0 + 931], arena[:, M0 + 931:M0 + 934]
        sel = v(arena[:, M0 + 944:M0 + 1072], t=TC, e=NE)
        pre = [v(arena[:, M0 + 128 + i * 128:M0 + 256 + i * 128], t=TC, e=NE) for i in range(2)]
        rank = v(arena[:, M0 + 1072:M0 + 1200], t=TC, e=NE)
        table = v(arena[:, M0 + 1200:M0 + 1456], t=TC, e=NE, n=2)
        onehot = [v(arena[:, M0 + 1456 + i * 256:M0 + 1712 + i * 256], t=TC, e=2, s=CAP) for i in range(2)]
        gslot = v(arena[0:CAP, M0 + 1968:M0 + 1976], k=NSLOT, n=2)
        mcon = arena[:, M0 + 1984:M0 + 1984 + NMOEC]
        rows_all = ctx.enter_context(nc.sbuf_tensor("rows", [P, NPAIR], U32))
        rows_u = [rows_all[:, i:i + 1] for i in range(NPAIR)]
        more_groups = ctx.enter_context(nc.sbuf_tensor("more_groups", [P, 1], U32))
        yd = [nc.dram_tensor(f"y_rows_dram{L}", [TOPK * S, D], F32).ap() for L in range(2)]
        ysum = [v(slot[3], j=TOPK, d=D), v(wbig[:, 0:TOPK * D], j=TOPK, d=D)]

        PARTS0 = (2, 0, 1, 3)
        def unit0(n):
            m = n - 4
            branch, qc, g = (0, n // 2, n % 2) if n < 4 else (1 + m // 2 % 2, m // 4, m % 2)
            qb, kb, vc = [(0, 4, C_VA), (5, 9, C_VS), (5, 10, C_VW)][branch]
            rows = slice(HD * g, HD * g + HD)
            return dict(
                n=n, qc=qc, branch=branch, g=g, scale=HD ** -0.5, mask=K_SWA if branch == 0 else K_CAUSAL, sink=branch == 0,
                q=[qkt[rows, qb + j, qc * P:(qc + 1) * P] for j in range(R)],
                k=[qkt[rows, kb, 0:(qc + 1) * P]] * R,
                v=[qkv[:, c, vc + HD * g:vc + HD * g + HD] for c in range(qc + 1)])

        def unit1(n):
            qc, hg = n // 4, n % 4
            hs = range(4 * hg, 4 * hg + 4)
            return dict(
                n=n, qc=qc, scale=DQK ** -0.5, mask=K_CAUSAL, sink=False,
                q=[qt1[0:DQK, h, qc * P:(qc + 1) * P] for h in hs],
                k=[kt1[0:DQK, h, 0:(qc + 1) * P] for h in hs],
                v=[[kv1[:, c, h * 128 + NOPE:(h + 1) * 128] for h in hs] for c in range(qc + 1)])

        UNITS = [[unit0(n) for n in range(12)], [unit1(n) for n in range(8)]]
        SBUFS = [s0, s1]
        PTBUF = [pt0, pt1]

        block = ctx.enter_context(nc.Block())

        def router_loads(sp, L):
            sp.dma_start(v(rw[:, :], c=KC, e=NE), router_w[L].rearrange("(p c) e -> p c e", c=KC)).then_inc(sem["router_in"], 16)
            sp.dma_start(rbias[:, :], router_bias[L:L + 1, :].partition_broadcast(P)[:, 0, :]).then_inc(sem["router_in"], 16)

        def norm_loads(sp, name, g, b, L):
            sp.dma_start(lng, g[L:L + 1, :].partition_broadcast(P)[:, 0, :]).then_inc(sem[name], 16)
            sp.dma_start(lnb, b[L:L + 1, :].partition_broadcast(P)[:, 0, :]).then_inc(sem[name], 16)

        def load_gate_up(sp, dst, g, u, s):
            for i, w in enumerate((g, u)):
                sp.dma_start(dst[:, i * KC * DE:(i + 1) * KC * DE], w.rearrange("(p c) f -> p (c f)", c=KC)).then_inc(s, 16)

        def load_down(sp, dst, d, s):
            sp.dma_start(dst[:, 2 * KC * DE:SLOT], d.rearrange("(p c) n -> p (c n)", c=DE // P)).then_inc(s, 16)

        def load_shared(sp, L):
            load_gate_up(sp, wbig, s_gate[L], s_up[L], sem["shared_in"])
            sp.dma_start(shared_down, s_down[L].rearrange("(p c) n -> p (c n)", c=DE // P)).then_inc(sem["shared_in"], 16)

        def one(w, L, e):
            return w[L, bass.ds(e, 1)].rearrange("a k n -> (a k) n")

        def expert_gate_up(sp, L, k, e):
            load_gate_up(sp, slot[k], one(e_gate, L, e), one(e_up, L, e), sem[f"gu{k}_in{L}"])

        def expert_down(sp, L, k, e):
            load_down(sp, slot[k], one(e_down, L, e), sem[f"dn{k}_in{L}"])

        def load_expert(sp, L, k, e):
            expert_gate_up(sp, L, k, e)
            expert_down(sp, L, k, e)

        def refills(sp, L):
            n_groups = sp.value_load(more_groups[0:1, 0:1], min_val=0, max_val=3 * GROUPS) + GROUPS

            def group(i, first):
                for k in range(NSLOT):
                    n = i * NSLOT + k
                    sp.wait_ge(sem[f"lo_dve{L}"], (n + 1) * NCHUNK)
                    expert_gate_up(sp, L, k, (n + NSLOT) % NE)
                    if not first or k:
                        sp.wait_ge(sem[f"down_pe{L}"], n)
                        expert_down(sp, L, (k - 1) % NSLOT, (n - 1 + NSLOT) % NE)

            group(0, True)
            with sp.Fori(1, n_groups - 1) as i:
                group(i, False)
            sp.wait_ge(sem[f"down_pe{L}"], (n_groups - 1) * NSLOT)
            expert_down(sp, L, NSLOT - 1, NE - 1)

        def mixture_loads(sp, L):
            sp.wait_ge(sem["out_pe"], TC * (L + 1))
            load_shared(sp, L)
            load_expert(sp, L, 3, 3)
            sp.dma_start(mcon, moe_const).then_inc(sem["moec_in"], 16)
            sp.wait_ge(sem["lnmix_dve"], TC * (L + 1))
            norm_loads(sp, "ln_ffn_in", ln_ffn_g, ln_ffn_b, L)
            sp.wait_ge(sem["groups_dve"], L + 1)
            refills(sp, L)

        def sum_loads(sp, L):
            n_groups = sp.value_load(more_groups[0:1, 0:1], min_val=0, max_val=3 * GROUPS) + GROUPS
            for k in range(NPAIR):
                sp.wait_ge(sem[f"scatter{k}_out{L}"], n_groups * 16)
            src = yd[L].rearrange("(j t p) d -> t p j d", j=TOPK, t=TC)
            for tc in range(TC):
                for j in range(SUMS):
                    ranks = slice(j * TOPK // SUMS, (j + 1) * TOPK // SUMS)
                    sp.dma_start(ysum[tc][:, ranks, :], src[tc][:, ranks, :]).then_inc(sem[f"sum{tc}{j}_in"], 16)

        WIN_PARTS = (1, 2, 2, 3)

        def win_part(c):
            return min((c + 1) // 2, 3)

        @block.sync
        def _(sp):
            def rows(w, c):
                return w.rearrange("(p c) n -> p c n", c=c)

            sp.dma_start(cst[:, :], const).then_inc(sem["const_in"], 16)
            sp.dma_start(xrow, x[0].rearrange("(t p) d -> p t d", p=P)).then_inc(sem["x_in"], 16)
            sp.dma_start(sinkb, sinks.partition_broadcast(P)[:, 0, :]).then_inc(sem["x_in"], 16)
            w0 = rows(w_in0[0], KC)
            win0 = v(ring[:, 0:KC * IN0], c=KC, n=IN0)
            for c in range(KC):
                sp.dma_start(win0[:, c, :], w0[:, c, :]).then_inc(sem[f"win_in{win_part(c)}"], 16)
            for i, (pe, w1, w2) in enumerate(((pe_k, ck1, ck2), (pe_v, cv1, cv2))):
                sp.dma_start(pen[0:CMP_LEN, i * HD:(i + 1) * HD], pe[0]).then_inc(sem["cmpw_in"], 16)
                for lh in range(2):
                    sp.dma_start(cw1[i][HD * lh:HD * lh + HD, :, :],
                                 w1[0, lh * 1024:lh * 1024 + 1024, :].rearrange("(l d) h -> d l h", d=HD))\
                      .then_inc(sem["cmpw_in"], 16)
                sp.dma_start(cw2[i], w2[0]).then_inc(sem["cmpw_in"], 16)
            router_loads(sp, 0)
            norm_loads(sp, "ln_mix_in", ln_mix_g, ln_mix_b, 0)
            sp.dma_start(wout, w_out0[0].rearrange("(c p) n -> p c n", p=P)).then_inc(sem["wout_in"], 16)
            sp.wait_ge(sem["proj_pe0"], 8)
            sp.wait_ge(sem["gates_pe"], 1)
            for k in range(3):
                load_expert(sp, 0, k, k)
            mixture_loads(sp, 0)
            sum_loads(sp, 0)
            n_groups = sp.value_load(more_groups[0:1, 0:1], min_val=0, max_val=3 * GROUPS) + GROUPS
            sp.wait_ge(sem["down_pe0"], n_groups * NSLOT - 1)
            sp.dma_start(win1, rows(w_in1[0], KC)).then_inc(sem["win1_in"], 16)
            sp.dma_start(uq, rows(w_uq[0], QL // P)).then_inc(sem["wuq_in"], 16)
            sp.dma_start(ukv, rows(w_ukv[0], KVL // P)).then_inc(sem["wukv_in"], 16)
            sp.wait_ge(sem["gate_dve"], 1)
            router_loads(sp, 1)
            sp.wait_ge(sem["lnffn_dve"], TC)
            sp.dma_start(lnp[:, 0:QL], q_norm.partition_broadcast(P)[:, 0, :]).then_inc(sem["small1_in"], 16)
            sp.dma_start(lnp[:, QL:QL + KVL], kv_norm.partition_broadcast(P)[:, 0, :]).then_inc(sem["small1_in"], 16)
            sp.dma_start(wout, w_out1[0].rearrange("(c p) n -> p c n", p=P)).then_inc(sem["wout_in"], 16)
            sp.wait_ge(sem["rms_dve"], TC)
            norm_loads(sp, "ln_mix_in", ln_mix_g, ln_mix_b, 1)
            sp.wait_ge(sem["q_pe"], 6)
            load_expert(sp, 1, 0, 0)
            sp.wait_ge(sem["kv_pe"], 8)
            load_expert(sp, 1, 1, 1)
            sp.wait_ge(sem["qk_pe"], BOTH["qk_pe"] + 16)
            load_expert(sp, 1, 2, 2)
            mixture_loads(sp, 1)
            sum_loads(sp, 1)
            orows = out[0].rearrange("(t p) d -> p t d", p=P)
            for tc in range(TC):
                sp.wait_ge(sem["lnffn_dve"], BOTH["lnffn_dve"] + tc + 1)
                sp.dma_start(orows[:, tc, :], xrow[:, tc, :]).then_inc(sem["out_done"], 16)
            sp.wait_ge(sem["out_done"], 16 * TC)

        def pe_columns(pe, st, tc, wait=None, base=0):
            if wait:
                pe.wait_ge(sem[wait], base + tc + 1)
            for c in range(KC):
                mm = pe.transpose(BANK[2 * tc + c // 4][:, c % 4 * P:(c % 4 + 1) * P],
                                  xrow[:, tc, c:c + (P - 1) * KC + 1:KC], ident)
                if c % 4 == 3:
                    mm.then_inc(sem["xt_pe"], 1)

        def columns_ready(eng, st, tc):
            eng.wait_ge(sem["xt_act"], 3 * st + 2 + tc)
            if tc:
                eng.wait_ge(sem["xt_dve"], st + 1)

        def pe_compressed(pe):
            pe.wait_ge(sem["cp_dve"], 1)
            pe.wait_ge(sem["o_dve"], 2)
            for i in range(4):
                tc, g = i // 2, i % 2
                mm = pe.transpose(BANK[6][:, i * P:(i + 1) * P], cp[:, tc, g * R:(g + 1) * R, :], ident)
            mm.then_inc(sem["cpt_pe"], 1)
            pe.wait_ge(sem["cpt_act"], 1)
            pe.wait_ge(sem["vbd_dve"], 1)
            for tc in range(TC):
                for g in range(G):
                    for j in range(2):
                        o = g * 256 + j * P
                        pe.matmul(BANK[6 + tc][:, o:o + P], vbd[g][:, 2 * j:2 * j + 2, :].rearrange("p j d -> p (j d)"),
                                  cpt[:, tc * 2 + g, :], start=g == 0 and j == 0, stop=False)

        def pe_attention(pe, L):
            units = UNITS[L]
            n = len(units)
            for u in range(n + 3):
                if u < n:
                    U = units[u]
                    if u >= 2:
                        pe.wait_ge(sem["max_dve"], L * BOTH["max_dve"] + 2 * (u - 1))
                    sc = v(PS[u % 2][:, 0:R * (U["qc"] + 1) * P], j=R, k=(U["qc"] + 1) * P)
                    for j in range(R):
                        mm = pe.matmul(sc[:, j, :], U["q"][j], U["k"][j], start=True, stop=True)
                    mm.then_inc(sem["score_pe"], 1)
                if L == 0 and u == 7:
                    pe_compressed(pe)
                if u >= n:
                    if u == n:
                        pe.wait_ge(sem["wout_in"], L * BOTH["wout_in"] + 16)
                        pe.wait_ge(sem["o_dve"], BOTH["o_dve"] + 2 if L else 3)
                        pe.wait_ge(sem["max_dve"], L * BOTH["max_dve"] + 2 * n)
                    pe_out_part(pe, L, 0, range((u - n) * 4, (u - n) * 4 + (4 if u < n + 2 else 8)))
                if u >= 3:
                    U = units[u - 3]
                    pe.wait_ge(sem["ptr_act"], L * BOTH["ptr_act"] + u - 2)
                    if L and u - 3 >= 4:
                        pe.wait_ge(sem["o_dve"], BOTH["o_dve"] + (u - 3) // 2 - 1)
                    w = (U["qc"] + 1) * P
                    pt = v(PTBUF[L][:, 0:R * w], j=R, k=w)
                    if L:
                        ob = v(BANK[6 + U["n"] // 2 % 2][:, U["n"] % 2 * 256:U["n"] % 2 * 256 + 256], j=2, q=P)
                        for j in range(R):
                            for c in range(U["qc"] + 1):
                                mm = pe.matmul(ob[HD * (j % 2):HD * (j % 2) + HD, j // 2, :], U["v"][c][j],
                                               pt[:, j, c * P:(c + 1) * P], start=c == 0, stop=c == U["qc"])
                    else:
                        ob = v(BANK[6 + U["qc"]][:, U["g"] * 256:U["g"] * 256 + 256], j=2, q=P)
                        for odd in range(2):
                            for c in range(U["qc"] + 1):
                                first = c == 0 and U["branch"] == 0
                                last = c == U["qc"] and (U["branch"] == 0 or U["branch"] == 2 and U["g"] == G - 1)
                                mm = pe.matmul(ob[HD * odd:HD * odd + HD, :, :], U["v"][c],
                                               pt[:, odd:R:2, c * P:(c + 1) * P], start=first, stop=last)
                    mm.then_inc(sem["pv_pe"], 1)
                if 2 <= u <= n + 1:
                    U = units[u - 2]
                    pe.wait_ge(sem["norm_dve"], L * BOTH["norm_dve"] + u - 1)
                    if u >= 3:
                        pe.wait_ge(sem["ptr_act"], L * BOTH["ptr_act"] + u - 2)
                    w = (U["qc"] + 1) * P
                    s = v(SBUFS[L][(u - 2) % 3][:, 0:R * w], j=R, k=w)
                    po = v(PS[2][:, 0:R * w], j=R, k=w)
                    for j in range(R):
                        for c in range(U["qc"] + 1):
                            mm = pe.transpose(po[:, j, c * P:(c + 1) * P], s[:, j, c * P:(c + 1) * P], ident)
                    mm.then_inc(sem["ptr_pe"], 1)

        OUT = (PS[0], PS[3])

        def pe_out_part(pe, L, tc, steps_):
            for i in steps_:
                half, c = i // KC, i % KC
                mm = pe.matmul(OUT[tc][:, half * 512:(half + 1) * 512], attot[L][:, c, tc * P:(tc + 1) * P],
                               wout[:, c, half * 512:(half + 1) * 512], start=c == 0, stop=c == KC - 1)
                if i == 2 * KC - 1:
                    mm.then_inc(sem["out_pe"], 1)

        def pe_out(pe, L):
            pe.wait_ge(sem["o_dve"], (L + 1) * BOTH["o_dve"])
            pe_out_part(pe, L, 1, range(2 * KC))

        def pe_logits(pe, L):
            pe.wait_ge(sem["router_in"], L * BOTH["router_in"] + 32)
            r = v(rw[:, :], c=KC, e=NE)
            for tc in range(TC):
                pe_columns(pe, 1 + 2 * L, tc, "lnmix_dve", TC * L)
                columns_ready(pe, 1 + 2 * L, tc)
                for c in range(KC):
                    mm = pe.matmul(BANK[0][:, tc * NE:(tc + 1) * NE], xcol[:, c, tc * P:(tc + 1) * P], r[:, c, :],
                                   start=c == 0, stop=c == KC - 1)
            mm.then_inc(sem["logit_pe"], 1)

        def pe_shared(pe, L):
            gu = v(wbig[:, 0:2 * KC * DE], m=2, c=KC, f=DE)
            pe.wait_ge(sem["shared_in"], 48 * (L + 1))
            pe.wait_ge(sem["sig_act"], L + 1)
            for tc in range(TC):
                for c in range(KC):
                    mm = pe.matmul(v(BANK[tc], m=2, f=DE), xcol[:, c, tc * P:(tc + 1) * P], gu[:, :, c, :],
                                   start=c == 0, stop=c == KC - 1)
                mm.then_inc(sem["sgu_pe"], 1)
            pe.wait_ge(sem["gate_dve"], L + 1)
            pe.wait_ge(sem["moec_in"], 16 * (L + 1))
            before, ones = mcon[:, M_BEFORE:M_BEFORE + P], mcon[:, M_ONES:M_ONES + P]
            pe.matmul(BANK[2][:, 0:NE], before, sel[:, 0, :], start=True, stop=True)
            pe.matmul(BANK[2][:, NE:2 * NE], ones, sel[:, 0, :], start=True, stop=False)
            pe.matmul(BANK[2][:, NE:2 * NE], before, sel[:, 1, :], start=False, stop=True)
            pe.matmul(BANK[2][:, 2 * NE:3 * NE], ones, sel[:, 0, :], start=True, stop=False)
            pe.matmul(BANK[2][:, 2 * NE:3 * NE], ones, sel[:, 1, :], start=False, stop=True).then_inc(sem["rank_pe"], 1)
            for tc in range(TC):
                pe.wait_ge(sem["sh_dve"], TC * L + tc + 1)
                if tc:
                    pe.wait_ge(sem["rank_dve"], L + 1)
                for c in range(2):
                    mm = pe.transpose(BANK[3 - tc][:, c * P:(c + 1) * P], shh[tc][:, c:c + 2 * P - 1:2], ident)
                mm.then_inc(sem["sht_pe"], 1)

        def pe_shared_down(pe, L, tc):
            pe.wait_ge(sem["sht_act"], TC * (L + 1))
            if tc:
                pe.wait_ge(sem["acc_dve"], TC * L + tc)
            dn = v(shared_down, c=DE // P, d=D)
            for half in range(2):
                for c in range(2):
                    mm = pe.matmul(PS[3][:, half * 512:(half + 1) * 512], sht[tc][:, c, :],
                                   dn[:, c, half * 512:(half + 1) * 512], start=c == 0, stop=c == 1)
            mm.then_inc(sem["sdown_pe"], 1)

        def steps(eng, L, step):
            n_groups = eng.value_load(more_groups[0:1, 0:1], min_val=0, max_val=3 * GROUPS) + GROUPS

            def group(i, first, last):
                for k in range(NSLOT):
                    def have(d):
                        return (not last or k + d < NSLOT) and (not first or k + d >= 0)
                    step(i * NSLOT + k, k, have)

            group(0, True, False)
            with eng.Fori(1, n_groups - 1) as i:
                group(i, False, False)
            group(n_groups - 1, False, True)
            return n_groups

        def pe_gather(pe, L, n, k, part):
            if part == 0:
                pe.wait_ge(sem[f"pick_dve{L}"], pairs_before(n, k) + 1)
            pick = onehot[k // 2 % 2].rearrange("p t e s -> p t (e s)")
            for c in range(part * KC // 2, (part + 1) * KC // 2):
                for tc in range(TC):
                    mm = pe.matmul(PS[0][:, c * P:(c + 1) * P], xrow[:, tc, c:c + (P - 1) * KC + 1:KC],
                                   pick[:, tc, :], start=tc == 0, stop=tc == TC - 1)
            if part == 1:
                mm.then_inc(sem[f"gather_pe{L}"], 1)

        def pe_slots(pe, L, n, k):
            pick = onehot[k // 2 % 2].rearrange("p t e s -> p t (e s)")
            for tc in range(TC):
                mm = pe.matmul(BANK[5][:, 0:4], pick[:, tc, :], table[:, tc, bass.ds(n % NE, 2), :],
                               start=tc == 0, stop=tc == TC - 1)
            mm.then_inc(sem[f"slots_pe{L}"], 1)

        def pe_down(pe, L, n, k, early):
            pe.wait_ge(sem[f"ht_act{L}"], n + 1)
            pe.wait_ge(sem[f"dn{k % NSLOT}_in{L}"], (uses_before(n, k) + 1) * 16)
            if early:
                pe.wait_ge(sem["acc_dve"], TC * (L + 1))
            else:
                pe.wait_ge(sem[f"ya_act{L}"], n)
                pe.wait_ge(sem[f"yd_dve{L}"], n)
            dn = expert(slot[k % NSLOT])[1]
            for half in range(2):
                for c in range(2):
                    mm = pe.matmul(PS[3][0:CAP, half * 512:(half + 1) * 512], ht[k % 2][:, c, :],
                                   dn[:, c, half * 512:(half + 1) * 512], start=c == 0, stop=c == 1)
            mm.then_inc(sem[f"down_pe{L}"], 1)

        def pe_experts(pe, L):
            pe_gather(pe, L, 0, 0, 0)
            pe_gather(pe, L, 0, 0, 1)
            pe_shared_down(pe, L, 0)

            def step(n, k, have):
                pe.wait_ge(sem[f"xlo_dve{L}"], pairs_before(n, k) + 1)
                if have(-2):
                    pe.wait_ge(sem[f"sum_dve{L}"], n - 1)
                bank = BANK[2 + k % 2]
                for j in range(NCHUNK):
                    pe.wait_ge(sem[f"lo_dve{L}"], n * NCHUNK + j + 1)
                    for c in range(j * KC // NCHUNK, (j + 1) * KC // NCHUNK):
                        for w in (whi, wlo):
                            mm = pe.matmul(bank, xe[:, k % 2, c, :], w[:, c * 2 * DE:(c + 1) * 2 * DE],
                                           start=c == 0 and w is whi, stop=c == KC - 1 and w is wlo)
                    mm.then_inc(sem[f"gu_pe{L}"], 1)
                if not have(-1):
                    pe.wait_ge(sem[f"pick_dve{L}"], 2)
                    pe_slots(pe, L, 0, 0)
                    pe_shared_down(pe, L, 1)
                if k % 2 == 0 and have(2):
                    pe_gather(pe, L, n + 2, k + 2, 0)
                if k % 2 == 1 and have(1):
                    pe.wait_ge(sem[f"gates_dve{L}"], pairs_before(n, k) + 1)
                    pe_gather(pe, L, n + 1, k + 1, 1)
                    pe_slots(pe, L, n + 1, k + 1)
                if have(-1):
                    pe_down(pe, L, n - 1, k + 3, early=not have(-2))
                pe.wait_ge(sem[f"h_dve{L}"], n + 1)
                if have(-1):
                    pe.wait_ge(sem[f"ht_act{L}"], n)
                pe.nop(nofuse=True)
                pe.wait_ge(sem["const_in"], 16)
                for c in range(2):
                    mm = pe.transpose(BANK[4][:, c * CAP:(c + 1) * CAP], hh[k % 2][:, c:c + 2 * P - 1:2],
                                      ident[0:CAP, 0:CAP])
                mm.then_inc(sem[f"ht_pe{L}"], 1)

            n_groups = steps(pe, L, step)
            pe_down(pe, L, n_groups * NSLOT - 1, 3, early=False)

        def half_rows(pairs, k):
            return pairs[k // 2][CAP * (k % 2):CAP * (k % 2) + CAP]

        def pairs_before(n, k):
            return (n - k) // 2 + k // 2

        def uses_before(n, k):
            return (n - k) // NSLOT + k // NSLOT

        def pe_moe_steps(pe, L):
            pe_shared(pe, L)
            pe_experts(pe, L)

        @block.tensor
        def _(pe):
            pe.wait_ge(sem["const_in"], 16)
            pe.wait_ge(sem["x_in"], 32)
            for tc in range(TC):
                pe_columns(pe, 0, tc)
            columns_ready(pe, 0, 1)
            win0 = v(ring[:, 0:KC * IN0], c=KC, n=IN0)
            def project(n, tc, c):
                return pe.matmul(BANK[2 * n + tc], xcol[:, c, tc * P:(tc + 1) * P], win0[:, c, n * 512:(n + 1) * 512],
                                 start=c == 0, stop=c == KC - 1)

            for c in range(KC // 2):
                pe.wait_ge(sem[f"win_in{win_part(c)}"], WIN_PARTS[win_part(c)] * 16)
                for n in range(4):
                    for tc in range(TC):
                        project(n, tc, c)
            for n in PARTS0:
                for tc in range(TC):
                    for c in range(KC // 2, KC):
                        pe.wait_ge(sem[f"win_in{win_part(c)}"], WIN_PARTS[win_part(c)] * 16)
                        mm = project(n, tc, c)
                    mm.then_inc(sem["proj_pe0"], 1)
                if n == 0:
                    pe.wait_ge(sem["proj_act0"], 1)
                    pe.wait_ge(sem["proj_dve0"], 1)
                    for i, c in enumerate((C_KC, C_VC)):
                        for g in range(G):
                            for tc in range(TC):
                                o = g * S + tc * P
                                mm = pe.transpose(BANK[4 + i][0:HD, o:o + P], qkv[:, tc, c + g * HD:c + (g + 1) * HD], ident)
                        mm.then_inc(sem["kcv_pe"], 1)
                    pe.wait_ge(sem["cmpw_in"], 128)
                    pe.wait_ge(sem["proj_dve0"], 2)
                    for i in range(2):
                        mm = pe.transpose(BANK[1][0:HD, i * CMP_LEN:(i + 1) * CMP_LEN], pen[0:CMP_LEN, i * HD:(i + 1) * HD],
                                          ident[0:CMP_LEN, 0:CMP_LEN])
                    mm.then_inc(sem["pet_pe"], 1)
                if n == 1:
                    pe.wait_ge(sem["cmpw_in"], 128)
                    pe.wait_ge(sem["blk_dve"], 8)
                    pe.wait_ge(sem["pet_act"], 1)
                    for i in range(2):
                        for l in range(16):
                            mm = pe.matmul(BANK[1][:, i * 32:i * 32 + G * NCMP], cw1[i][:, l, :],
                                           blk[i][:, l, :, :].rearrange("p g n -> p (g n)"), start=l == 0, stop=l == 15)
                    mm.then_inc(sem["hid_pe"], 1)
            pe.wait_ge(sem["proj_act0"], 2)
            for c in range(KC):
                mm = pe.matmul(BANK[0][0:NGATE, 0:S], win0[:, c, C_GT:C_GT + NGATE], xcol[:, c, :],
                               start=c == 0, stop=c == KC - 1)
            mm.then_inc(sem["gates_pe"], 1)
            pe.wait_ge(sem["gelu_dve"], 1)
            for i in range(2):
                for g in range(G):
                    o = 128 + i * 128 + g * HD
                    mm = pe.matmul(BANK[1][0:NCMP, o:o + HD], hidw[5][:, i * 32 + g * NCMP:i * 32 + (g + 1) * NCMP],
                                   cw2[i], start=True, stop=True)
            mm.then_inc(sem["kv2_pe"], 1)
            pe.wait_ge(sem["gates_act"], 1)
            for tc in range(TC):
                mm = pe.transpose(BANK[0][:, tc * 32:tc * 32 + NGATE], gate_cols[:, tc * P:(tc + 1) * P],
                                  ident[0:NGATE, 0:NGATE])
            mm.then_inc(sem["gates_pe"], 1)
            pe.wait_ge(sem["rope_dve0"], TC)
            for u in range(6):
                bank = BANK[(2, 3, 6, 7, 4, 5)[u]]
                if u >= 4:
                    pe.wait_ge(sem["kcv_act"], u - 3)
                for b in range(2 * u, min(2 * u + 2, NB)):
                    for tc in range(TC):
                        o = (b % 2) * S + tc * P
                        mm = pe.transpose(bank[:, o:o + P], rope[:, tc, b * P:(b + 1) * P], ident)
                mm.then_inc(sem["qk_pe"], 1)
            pe.wait_ge(sem["kcn_dve"], 1)
            pe.transpose(BANK[0][:, 0:NCMP], kcn[0:NCMP, :], ident[0:NCMP, 0:NCMP]).then_inc(sem["kct_pe"], 1)
            pe.wait_ge(sem["kct_dve"], 1)
            pe.wait_ge(sem["qk_act"], 6)
            for j in range(R):
                for tc in range(TC):
                    o = tc * P + j * 32
                    mm = pe.matmul(BANK[5][:, o:o + G * NCMP], qkt[:, 5 + j, tc * P:(tc + 1) * P], kcmpt, start=True, stop=True)
            mm.then_inc(sem["csc_pe"], 1)
            pe_attention(pe, 0)
            pe_out(pe, 0)
            pe_logits(pe, 0)
            pe_moe_steps(pe, 0)
            for tc in range(TC):
                pe_columns(pe, 2, tc, "lnffn_dve")
                columns_ready(pe, 2, tc)
                pe.wait_ge(sem["win1_in"], 16)
                for n, w in ((0, 512), (512, IN1 - 512)):
                    for c in range(KC):
                        mm = pe.matmul(PS[2 + tc][:, n:n + w], xcol[:, c, tc * P:(tc + 1) * P], win1[:, c, n:n + w],
                                       start=c == 0, stop=c == KC - 1)
                mm.then_inc(sem["proj_pe1"], 1)
            pe.wait_ge(sem["rms_dve"], TC)
            for c in range(5):
                for tc in range(TC):
                    o = (c % 2) * S + tc * P
                    if c < 3:
                        src = c1[:, tc, c:c + 3 * P - 2:3]
                    else:
                        src = c1[:, tc, QL + c - 3:QL + c - 3 + 2 * P - 1:2]
                    mm = pe.transpose(BANK[c // 2][:, o:o + P], src, ident)
                if c % 2 or c == 4:
                    mm.then_inc(sem["cnt_pe"], 1)
            pe.wait_ge(sem["krope_dve"], TC)
            for tc in range(TC):
                mm = pe.transpose(BANK[3][0:ROPE, tc * P:(tc + 1) * P], c1[:, tc, QL + KVL:IN1], ident)
            mm.then_inc(sem["krt_pe"], 1)
            pe.wait_ge(sem["cnt_act"], 3)
            pe.wait_ge(sem["krt_act"], 1)
            pe.wait_ge(sem["wuq_in"], 16)
            for i in range(6):
                tc, n = i // 3, i % 3
                for c in range(3):
                    mm = pe.matmul(BANK[i], ct1[:, c, tc * P:(tc + 1) * P], uq[:, c, n * 512:(n + 1) * 512],
                                   start=c == 0, stop=c == 2)
                mm.then_inc(sem["q_pe"], 1)
            pe.wait_ge(sem["wukv_in"], 16)
            for i in range(8):
                tc, n = i // 4, i % 4
                b = (i + 6) % 8
                if i >= 2:
                    pe.wait_ge(sem["q_act"], i - 1)
                for c in range(2):
                    mm = pe.matmul(BANK[b], ct1[:, 3 + c, tc * P:(tc + 1) * P], ukv[:, c, n * 512:(n + 1) * 512],
                                   start=c == 0, stop=c == 1)
                mm.then_inc(sem["kv_pe"], 1)
            pe.wait_ge(sem["kv_act"], 8)
            pe.wait_ge(sem["qrope_dve"], TC)
            for u in range(16):
                if u >= 4:
                    pe.wait_ge(sem["qk_act"], BOTH["qk_act"] + u - 3)
                hs = [u // 2 * 2, u // 2 * 2 + 1]
                hs = [2 * (u % 8), 2 * (u % 8) + 1]
                for i, h in enumerate(hs):
                    for tc in range(TC):
                        o = i * S + tc * P
                        if u < 8:
                            mm = pe.transpose(BANK[u % 4][0:NOPE, o:o + P], kv1[:, tc, h * 128:h * 128 + NOPE], ident)
                        else:
                            mm = pe.transpose(BANK[u % 4][0:DQK, o:o + P], qn1[:, tc, h * DQK:(h + 1) * DQK], ident)
                mm.then_inc(sem["qk_pe"], 1)
            pe.wait_ge(sem["qk_act"], BOTH["qk_act"] + 16)
            pe.wait_ge(sem["kfull_dve"], 1)
            pe_attention(pe, 1)
            pe_out(pe, 1)
            pe_logits(pe, 1)
            pe_moe_steps(pe, 1)

        def act_columns(act, st):
            for b in range(3):
                tc, c = b // 2, b % 2 * 4
                act.wait_ge(sem["xt_pe"], 4 * st + b + 1)
                nc.scalar.copy(xcol[:, c:c + 4, tc * P:(tc + 1) * P], v(BANK[b], c=4, t=P)).then_inc(sem["xt_act"], 1)

        def act_attention(act, L):
            units = UNITS[L]
            n = len(units)
            for u in range(n + 2):
                if L == 0 and u == 7:
                    act.wait_ge(sem["cpt_pe"], 1)
                    nc.scalar.copy(cpt, v(BANK[6], u=4, q=P)).then_inc(sem["cpt_act"], 1)
                if u < n:
                    U = units[u]
                    w = (U["qc"] + 1) * P
                    s = v(SBUFS[L][u % 3][:, 0:R * w], j=R, k=w)
                    act.wait_ge(sem["max_dve"], L * BOTH["max_dve"] + 2 * u + 2)
                    for j in range(R):
                        i = u * R + j
                        ins = nc.scalar.activation(s[:, j, :], s[:, j, :], ACT.Exp, bias=nmax[:, i:i + 1],
                                                   accum_out=sums[:, i:i + 1])
                    if U["sink"]:
                        act.wait_ge(sem["sink_dve"], u + 2)
                        e4 = esink[:, u * R:(u + 1) * R]
                        ins = nc.scalar.activation(e4, e4, ACT.Exp)
                    ins.then_inc(sem["exp_act"], 1)
                if u >= 2:
                    U = units[u - 2]
                    w = (U["qc"] + 1) * P
                    act.wait_ge(sem["ptr_pe"], L * BOTH["ptr_pe"] + u - 1)
                    if u >= 3:
                        act.wait_ge(sem["pv_pe"], L * BOTH["pv_pe"] + u - 2)
                    nc.scalar.copy(PTBUF[L][:, 0:R * w], PS[2][:, 0:R * w]).then_inc(sem["ptr_act"], 1)

        def act_logits(act, L):
            act.wait_ge(sem["logit_pe"], L * BOTH["logit_pe"] + 1)
            nc.scalar.activation(rs, v(BANK[0][:, 0:TC * NE], t=TC, e=NE), ACT.Exp, scale=-1.0).then_inc(sem["sig_act"], 1)

        def act_moe(act, L):
            for tc in range(TC):
                act.wait_ge(sem["sgu_pe"], TC * L + tc + 1)
                nc.scalar.activation(ssg[tc], BANK[tc][:, 0:DE], ACT.Silu).then_inc(sem["ssilu_act"], 1)
            def high(n, k, j, used=True):
                if j == 0:
                    act.wait_ge(sem[f"gu{k % NSLOT}_in{L}"], (uses_before(n, k) + 1) * 32)
                if used:
                    act.wait_ge(sem[f"gu_pe{L}"], (n - 1) * NCHUNK + j + 1)
                part = slot[k % NSLOT][:, 0:2 * KC * DE].rearrange("p (m c f) -> p c m f", m=2, c=KC)
                c = slice(j * KC // NCHUNK, (j + 1) * KC // NCHUNK)
                nc.scalar.copy(whi[:, j * CW:(j + 1) * CW].rearrange("p (c m f) -> p c m f", m=2, f=DE), part[:, c])\
                    .then_inc(sem[f"hi_act{L}"], 1)

            def x_high(n, k):
                act.wait_ge(sem[f"gather_pe{L}"], pairs_before(n, k) + 1)
                nc.scalar.copy(xe[:, :, :, 0:CAP].rearrange("p e c s -> p c e s"), PS[0][:, :].rearrange("p (c e s) -> p c e s", c=KC, e=2))\
                    .then_inc(sem[f"xhi_act{L}"], 1)

            def y_half(n, k):
                act.wait_ge(sem[f"down_pe{L}"], n + 1)
                nc.scalar.copy(half_rows(ys, k)[:, 0:512], PS[3][0:CAP, 0:512]).then_inc(sem[f"ya_act{L}"], 1)

            act.wait_ge(sem["sgu_pe"], TC * (L + 1))
            high(0, 0, 0, used=False)
            high(0, 0, 1, used=False)
            for tc in range(TC):
                act.wait_ge(sem["sht_pe"], TC * L + tc + 1)
                nc.scalar.copy(sht[tc], v(BANK[3 - tc][:, 0:2 * P], c=2, t=P)).then_inc(sem["sht_act"], 1)
            high(0, 0, 2, used=False)
            high(0, 0, 3, used=False)
            x_high(0, 0)

            def step(n, k, have):
                if have(1):
                    high(n + 1, k + 1, 0)
                    high(n + 1, k + 1, 1)
                act.wait_ge(sem[f"gu_pe{L}"], (n + 1) * NCHUNK)
                if have(-1):
                    act.wait_ge(sem[f"sum_dve{L}"], n)
                nc.scalar.copy(gutop, BANK[2 + k % 2][0:CAP, :]).then_inc(sem[f"top_act{L}"], 1)
                if have(1):
                    high(n + 1, k + 1, 2)
                act.wait_ge(sem[f"sum_dve{L}"], n + 1)
                if have(-1):
                    act.wait_ge(sem[f"h_dve{L}"], n)
                nc.scalar.activation(sg, gusum[:, 0:DE], ACT.Silu).then_inc(sem[f"silu_act{L}"], 1)
                if have(1):
                    if k % 2:
                        x_high(n + 1, k + 1)
                    high(n + 1, k + 1, 3)
                if have(-1):
                    y_half(n - 1, (k - 1) % NSLOT)
                if have(-4):
                    act.wait_ge(sem[f"scatter{k // 2}_out{L}"], uses_before(n, k) * 16)
                act.wait_ge(sem[f"ht_pe{L}"], n + 1)
                nc.scalar.copy(ht[k % 2], v(BANK[4][:, 0:2 * CAP], c=2, t=CAP)).then_inc(sem[f"ht_act{L}"], 1)

            n_groups = steps(act, L, step)
            y_half(n_groups * NSLOT - 1, 3)

        @block.scalar
        def _(act):
            act_columns(act, 0)
            for i, n in enumerate(PARTS0):
                act.wait_ge(sem["proj_pe0"], 2 * i + 1)
                nc.scalar.copy(qkv[:, 0, n * 512:(n + 1) * 512], BANK[2 * n]).then_inc(sem["proj_act0"], 1)
                if n == 0:
                    for i in range(2):
                        act.wait_ge(sem["kcv_pe"], i + 1)
                        nc.scalar.copy(kcv[0:HD, 2 * i:2 * i + 2, :], v(BANK[4 + i][0:HD, :], g=G, t=S)).then_inc(sem["kcv_act"], 1)
                    act.wait_ge(sem["pet_pe"], 1)
                    nc.scalar.copy(pet[0:HD, :, :], v(BANK[1][0:HD, 0:2 * CMP_LEN], k=2, l=CMP_LEN)).then_inc(sem["pet_act"], 1)
                if n == 1:
                    act.wait_ge(sem["hid_pe"], 1)
                    hv = [v(h, k=2, n=32)[:, :, 0:G * NCMP] for h in hidw]
                    nc.scalar.copy(hv[0], v(BANK[1][:, 0:64], k=2, n=32)[:, :, 0:G * NCMP]).then_inc(sem["hid_act"], 1)
                    act.wait_ge(sem["gin_dve"], 1)
                    nc.scalar.activation(hv[3], hv[2], ACT.Exp, scale=-GELU_C).then_inc(sem["gexp_act"], 1)
            act.wait_ge(sem["gates_pe"], 1)
            nc.scalar.activation(gate_cols, BANK[0][0:NGATE, 0:S], ACT.Exp, scale=-1.0).then_inc(sem["gates_act"], 1)
            for u in range(6):
                act.wait_ge(sem["qk_pe"], u + 1)
                bank = BANK[(2, 3, 6, 7, 4, 5)[u]]
                w = min(2, NB - 2 * u)
                nc.scalar.copy(qkt[:, 2 * u:2 * u + w, :], v(bank[:, 0:w * S], b=w, t=S)).then_inc(sem["qk_act"], 1)
            act.wait_ge(sem["csub_dve"], 1)
            nc.scalar.activation(cs[:, :, :, 0:NCMP], cs[:, :, :, 0:NCMP], ACT.Exp).then_inc(sem["cexp_act"], 1)
            act_attention(act, 0)
            act_columns(act, 1)
            act_logits(act, 0)
            act_moe(act, 0)
            act_columns(act, 2)
            for tc in range(TC):
                act.wait_ge(sem["proj_pe1"], tc + 1)
                for i, (a, b) in enumerate(RMS_PARTS):
                    ins = nc.scalar.activation(ct1_flat[:, tc * (QL + KVL) + a:tc * (QL + KVL) + b], PS[2 + tc][:, a:b],
                                               ACT.Square, accum_out=ssq[:, 2 * tc + i:2 * tc + i + 1])
                ins.then_inc(sem["proj_act1"], 1)
                nc.scalar.copy(c1[:, tc, :], PS[2 + tc][:, 0:IN1]).then_inc(sem["proj_act1"], 1)
            for i in range(3):
                act.wait_ge(sem["cnt_pe"], i + 1)
                w = 2 if i < 2 else 1
                nc.scalar.copy(ct1[:, 2 * i:2 * i + w, :], v(BANK[i][:, 0:w * S], c=w, t=S)).then_inc(sem["cnt_act"], 1)
            act.wait_ge(sem["krt_pe"], 1)
            nc.scalar.copy(krt, BANK[3][0:ROPE, 0:S]).then_inc(sem["krt_act"], 1)
            for i in range(6):
                act.wait_ge(sem["q_pe"], i + 1)
                nc.scalar.copy(qn1[:, i // 3, i % 3 * 512:(i % 3 + 1) * 512], BANK[i]).then_inc(sem["q_act"], 1)
            for i in range(8):
                act.wait_ge(sem["kv_pe"], i + 1)
                nc.scalar.copy(kv1[:, i // 4, i % 4 * 512:(i % 4 + 1) * 512], BANK[(i + 6) % 8]).then_inc(sem["kv_act"], 1)
            for u in range(16):
                act.wait_ge(sem["qk_pe"], BOTH["qk_pe"] + u + 1)
                h = 2 * (u % 8)
                if u < 8:
                    nc.scalar.copy(kt1[0:NOPE, h:h + 2, :], v(BANK[u % 4][0:NOPE, :], h=2, t=S)).then_inc(sem["qk_act"], 1)
                else:
                    nc.scalar.copy(qt1[0:DQK, h:h + 2, :], v(BANK[u % 4][0:DQK, :], h=2, t=S)).then_inc(sem["qk_act"], 1)
            act_attention(act, 1)
            act_columns(act, 3)
            act_logits(act, 1)
            act_moe(act, 1)

        def pool_moe(pool, L):
            def scatter(n, k):
                pool.wait_ge(sem[f"ya_act{L}"], n + 1)
                pool.wait_ge(sem[f"yd_dve{L}"], n + 1)
                pool.nop(nofuse=True)
                pool.wait_ge(sem["groups_dve"], L + 1)
                pool.indirect_dma_start(
                    out=yd[L], out_offset=bass.IndirectOffsetOnAxis(ap=rows_u[k // 2], axis=0),
                    in_=ys[k // 2], in_offset=None,
                    bounds_check=TOPK * S - 1, oob_is_err=False).then_inc(sem[f"scatter{k // 2}_out{L}"], 16)

            pool.wait_ge(sem["groups_dve"], L + 1)
            steps(pool, L, lambda n, k, have: scatter(n, k) if k % 2 else None)

        @block.gpsimd
        def _(pool):
            pool.memset(power, -0.5).then_inc(sem["power_pool"], 1)
            pool.memset(kcmpt, 0.0).then_inc(sem["power_pool"], 1)
            pool.wait_ge(sem["hid_pe"], 1)
            pool.memset(last[:, 0:512], 0.0).then_inc(sem["zero_pool"], 1)
            pool.memset(last[:, 768:768 + 512], 0.0).then_inc(sem["zero_pool"], 1)
            pool.wait_ge(sem["power_pool"], 1)
            def roots(a, b, n=1):
                for i in range(a, b):
                    pool.wait_ge(sem["var_dve"], i + 1)
                    pool.tensor_tensor(root[:, 0:n], var[:, 0:n], power[:, 0:n], ALU.pow).then_inc(sem["root_pool"], 1)

            roots(0, 2)
            pool_moe(pool, 0)
            roots(2, 4)
            roots(4, 6, 2)
            roots(6, 8)
            pool_moe(pool, 1)
            roots(8, 10)

        @block.vector
        def _(dve):
            chain = [0]

            def link(ins):
                chain[0] += 1
                ins.then_inc(sem["dve_chain"], 1)
                dve.wait_ge(sem["dve_chain"], chain[0])

            marks = {}

            def mark(ins, name):
                ins.then_inc(sem[name], 1)
                marks[name] = marks.get(name, 0) + 1

            def settle(name):
                dve.wait_ge(sem[name], marks[name])

            V = nc.vector

            def columns(st):
                dve.wait_ge(sem["xt_pe"], 4 * st + 4)
                mark(V.tensor_copy(xcol[:, 4:8, P:2 * P], v(BANK[3], c=4, t=P)), "xt_dve")

            def bc(ap, shape):
                return ap.to_broadcast(shape)

            def apply_rope(src, dsts, cos, sin, heads, half, done=None):
                d = 2 * half
                n = heads * d
                t = v(tmp[:, 0:n], h=heads, d=d)
                u = v(tmp[:, 640:640 + n], h=heads, d=d)
                pr = src.shape[0]
                t, u = t[0:pr], u[0:pr]
                cb = cos[:, None, :].to_broadcast([pr, heads, d])
                sbc = sin[:, None, :].to_broadcast([pr, heads, d])
                V.tensor_tensor(t, src, cb, ALU.mult)
                link(V.tensor_tensor(u, src, sbc, ALU.mult))
                ins = None
                for a, b, (o1, o2), view in dsts:
                    V.tensor_tensor(o1, view(t[:, a:b, 0:half]), view(u[:, a:b, half:d]), ALU.subtract)
                    ins = V.tensor_tensor(o2, view(t[:, a:b, half:d]), view(u[:, a:b, 0:half]), ALU.add)
                    if b < heads or done is None:
                        link(ins)
                if done is not None:
                    mark(ins, done)
                    settle(done)

            roots = [0]

            def inverse_root(issue):
                roots[0] += 1
                mark(issue(), "var_dve")
                dve.wait_ge(sem["root_pool"], roots[0])

            def layer_norm(L, part):
                dve.wait_ge(sem[f"ln_{part}_in"], 32 * (L + 1))
                for tc in range(TC):
                    if part == "mix":
                        dve.wait_ge(sem["out_pe"], L * BOTH["out_pe"] + tc + 1)
                    r = xrow[:, tc, :]
                    if part == "mix":
                        link(V.scalar_tensor_tensor(r, r, ALPHA, OUT[tc][:, :], ALU.mult, ALU.add))
                    else:
                        dve.wait_ge(sem["acc_dve"], TC * (L + 1))
                        for j in range(TOPK):
                            if j % (TOPK // SUMS) == 0:
                                dve.wait_ge(sem[f"sum{tc}{j * SUMS // TOPK}_in"], 16 * (L + 1))
                            link(V.tensor_tensor(r, r if j else acc[:, tc, :], ysum[tc][:, j, :], ALU.add))
                    V.bn_stats(stats[:, 0:6], r[:, 0:512])
                    link(V.bn_stats(stats[:, 6:12], r[:, 512:1024]))
                    link(V.bn_aggr(mv, stats))
                    roots[0] += 1
                    mark(V.tensor_scalar(var[:, 0:1], mv[:, 1:2], LN_EPS, None, ALU.add), "var_dve")
                    link(V.scalar_tensor_tensor(r, r, mv[:, 0:1], lng, ALU.subtract, ALU.mult))
                    dve.wait_ge(sem["root_pool"], roots[0])
                    mark(V.scalar_tensor_tensor(r, r, root[:, 0:1], lnb, ALU.mult, ALU.add), f"ln{part}_dve")

            def attention(L):
                units = UNITS[L]
                n = len(units)
                for u in range(n + 3):
                    if u < n:
                        U = units[u]
                        w = (U["qc"] + 1) * P
                        s = v(SBUFS[L][u % 3][:, 0:R * w], j=R, k=w)
                        sc = v(PS[u % 2][:, 0:R * w], j=R, k=w)
                        mask = cst[:, U["mask"] + 2 * P - w:U["mask"] + 2 * P]
                        dve.wait_ge(sem["score_pe"], L * BOTH["score_pe"] + u + 1)
                        if u >= 3:
                            dve.wait_ge(sem["ptr_pe"], L * BOTH["ptr_pe"] + u - 2)
                        ins = V.scalar_tensor_tensor(s, sc, U["scale"], mask[:, None, :].to_broadcast([P, R, w]),
                                                     ALU.mult, ALU.add)
                        mark(ins, "max_dve")
                        dve.wait_ge(sem["max_dve"], L * BOTH["max_dve"] + 2 * u + 1)
                        m = nmax[:, u * R:(u + 1) * R]
                        ins = V.tensor_reduce(m, s, AX_X, ALU.max, negate=True)
                        if U["sink"]:
                            link(ins)
                            sk = nsink[:, u % 2 * R:(u % 2 + 1) * R]
                            ins = V.tensor_tensor(m, m, sk, ALU.min)
                            mark(ins, "max_dve")
                            dve.wait_ge(sem["max_dve"], L * BOTH["max_dve"] + 2 * u + 2)
                            mark(V.tensor_tensor(esink[:, u * R:(u + 1) * R], m, sk, ALU.subtract), "sink_dve")
                        else:
                            mark(ins, "max_dve")
                    if L == 0 and u == 0:
                        compressed_softmax()
                    if 1 <= u <= n:
                        normalise(L, units[u - 1], u - 1)
                    if L == 0 and u == 10:
                        nsa_columns(0)
                    if u >= 4 and u % 2 == 0 and (L or u <= 6):
                        pair = (u - 4) // 2
                        dve.wait_ge(sem["pv_pe"], L * BOTH["pv_pe"] + 2 * pair + 2)
                        qc, c = (pair // 2, pair % 2 * 4) if L else (pair, 0)
                        mark(V.tensor_copy(attot[L][:, c:c + 4, qc * P:(qc + 1) * P], v(BANK[6 + pair % 2], c=4, q=P)), "o_dve")
                if L == 0:
                    nsa_columns(1)

            def nsa_columns(qc):
                dve.wait_ge(sem["pv_pe"], 8 + 4 * qc)
                mark(V.tensor_copy(attot[0][:, 4:8, qc * P:(qc + 1) * P], v(BANK[6 + qc], c=4, q=P)), "o_dve")

            def compressed_softmax():
                c8, cm = cs[:, :, :, 0:NCMP], v(crec, t=TC, h=8)
                dve.wait_ge(sem["cexp_act"], 1)
                for tc in range(TC):
                    mul = cst[:, K_CMUL + tc * NCMP:K_CMUL + (tc + 1) * NCMP]
                    ins = V.tensor_tensor(cp[:, tc, :, 0:NCMP], c8[:, tc], mul[:, None, :].to_broadcast([P, 8, NCMP]), ALU.mult)
                link(ins)
                link(V.tensor_reduce(cm, cp[:, :, :, 0:NCMP], AX_X, ALU.add))
                link(V.tensor_scalar(crec, crec, 1e-30, None, ALU.max))
                link(V.reciprocal(crec, crec))
                link(V.tensor_tensor(cm, cm, v(gates, t=TC, n=NGATE)[:, :, 0:8], ALU.mult))
                cpn = cp[:, :, :, 0:NCMP]
                mark(V.tensor_tensor(cpn, cpn, cm[:, :, :, None].to_broadcast([P, TC, 8, NCMP]), ALU.mult), "cp_dve")

            def normalise(L, U, u):
                dve.wait_ge(sem["exp_act"], L * BOTH["exp_act"] + u + 1)
                s4 = sums[:, u * R:(u + 1) * R]
                r4 = rec[:, u % 2 * R:u % 2 * R + R]
                if U["sink"]:
                    link(V.tensor_tensor(s4, s4, esink[:, u * R:(u + 1) * R], ALU.add))
                link(V.reciprocal(r4, s4))
                if L == 0 and U["branch"]:
                    o = U["qc"] * NGATE + 8 * U["branch"] + R * U["g"]
                    link(V.tensor_tensor(r4, r4, gates[:, o:o + R], ALU.mult))
                w = (U["qc"] + 1) * P
                s = v(SBUFS[L][u % 3][:, 0:R * w], j=R, k=w)
                mark(V.tensor_tensor(s, s, r4[:, :, None].to_broadcast([P, R, w]), ALU.mult), "norm_dve")

            def routing(L):
                dve.wait_ge(sem["sig_act"], L * BOTH["sig_act"] + 1)
                dve.wait_ge(sem["router_in"], L * BOTH["router_in"] + 32)
                link(V.tensor_scalar(rs, rs, 1.0, None, ALU.add))
                link(V.reciprocal(rs, rs))
                link(V.tensor_tensor(rsb, rs, rbias[:, None, :].to_broadcast([P, TC, NE]), ALU.add))
                for tc in range(TC):
                    for g in range(NG):
                        ins = V.max(top8[:, tc, g, :], rsb[:, tc, g * EPG:(g + 1) * EPG])
                V.memset(esc[:, :, NE:], LOWEST)
                V.memset(gsc[:, :, NG:], LOWEST)
                link(ins)
                link(V.tensor_tensor(gsc[:, :, 0:NG], top8[:, :, :, 0], top8[:, :, :, 1], ALU.add))
                for tc in range(TC):
                    ins = V.max(m8[:, tc, :], gsc[:, tc, 0:NG])
                link(ins)
                link(V.memset(m8[:, :, TOPG:], LOWEST))
                for tc in range(TC):
                    ins = V.match_replace(gpick[:, tc, :], m8[:, tc, :], gsc[:, tc, :], PICKED)
                link(ins)
                link(V.tensor_scalar(gsel, gpick[:, :, 0:NG], PICKED / 2, None, ALU.is_ge))
                link(V.tensor_scalar(gneg, gsel, 1.0, -NEG, ALU.subtract, ALU.mult))
                for tc in range(TC):
                    e3 = v(esc[:, tc, 0:NE], g=NG, k=EPG)
                    V.tensor_tensor(e3, v(rsb[:, tc, :], g=NG, k=EPG), gsel[:, tc, :, None].to_broadcast([P, NG, EPG]), ALU.mult).then_inc(sem["dve_chain"], 1)
                    chain[0] += 1
                dve.wait_ge(sem["dve_chain"], chain[0])
                for tc in range(TC):
                    e3 = v(esc[:, tc, 0:NE], g=NG, k=EPG)
                    ins = V.tensor_tensor(e3, e3, gneg[:, tc, :, None].to_broadcast([P, NG, EPG]), ALU.add)
                link(ins)
                for tc in range(TC):
                    ins = V.max(m8[:, tc, :], esc[:, tc, 0:NE])
                link(ins)
                link(V.memset(m8[:, :, TOPK:], LOWEST))
                for tc in range(TC):
                    ins = V.match_replace(epick[:, tc, :], m8[:, tc, :], esc[:, tc, :], PICKED)
                link(ins)
                link(V.tensor_scalar(sel, epick[:, :, 0:NE], PICKED / 2, None, ALU.is_ge))
                link(V.tensor_tensor(gate, sel, rs, ALU.mult))
                link(V.tensor_reduce(gsum, gate, AX_X, ALU.add))
                link(V.reciprocal(gsum, gsum))
                for tc in range(TC):
                    ins = V.tensor_scalar(gate[:, tc, :], gate[:, tc, :], gsum[:, tc:tc + 1], ROUTED_SCALE, ALU.mult, ALU.mult)
                mark(ins, "gate_dve")
                dve.wait_ge(sem["gate_dve"], L * BOTH["gate_dve"] + 1)

            def moe(L):
                for tc in range(TC):
                    dve.wait_ge(sem["ssilu_act"], TC * L + tc + 1)
                    mark(V.tensor_tensor(shh[tc], ssg[tc], BANK[tc][:, DE:2 * DE], ALU.mult), "sh_dve")
                dve.wait_ge(sem["rank_pe"], L + 1)
                link(V.tensor_reduce(most, BANK[2][:, 2 * NE:3 * NE], AX_X, ALU.max))
                link(V.tensor_tensor(over, most.to_broadcast([P, 3]), mcon[:, M_PASS:M_PASS + 3], ALU.is_gt))
                link(V.tensor_reduce(most, over, AX_X, ALU.add))
                mark(V.tensor_scalar(more_groups[:, :], most, float(GROUPS), None, ALU.mult), "groups_dve")
                link(V.scalar_tensor_tensor(rank, v(BANK[2][:, 0:2 * NE], t=TC, e=NE), 1.0, sel, ALU.add, ALU.mult))
                mark(V.tensor_scalar(rank, rank, 1.0, None, ALU.subtract), "rank_dve")
                def pick(n, k, early):
                    if not early:
                        dve.wait_ge(sem[f"slots_pe{L}"], pairs_before(n, k) - 1)
                    iota = mcon[:, None, None, bass.ds(n // NE * CAP + M_IOTA, CAP)]
                    mine = rank[:, :, bass.ds(n % NE, 2), None]
                    V.tensor_tensor(onehot[k // 2 % 2], iota.to_broadcast([P, TC, 2, CAP]), mine.to_broadcast([P, TC, 2, CAP]),
                                    ALU.is_equal).then_inc(sem[f"pick_dve{L}"], 1)

                def gates_in(n, k, early):
                    dve.wait_ge(sem[f"slots_pe{L}"], pairs_before(n, k) + 1)
                    if not early:
                        dve.wait_ge(sem[f"yd_dve{L}"], n - 2)
                    for e in range(2):
                        ins = V.tensor_copy(gslot[:, (k + e) % NSLOT, :], BANK[5][CAP * e:CAP * e + CAP, 2 * e:2 * e + 2])
                    ins.then_inc(sem[f"gates_dve{L}"], 1)

                def low(n, k, j):
                    dve.wait_ge(sem[f"hi_act{L}"], n * NCHUNK + j + 1)
                    part = slot[k % NSLOT][:, 0:2 * KC * DE].rearrange("p (m c f) -> p c m f", m=2, c=KC)
                    c = slice(j * KC // NCHUNK, (j + 1) * KC // NCHUNK)
                    hi = whi[:, j * CW:(j + 1) * CW].bitcast(F32).rearrange("p (c m f) -> p c m f", m=2, f=DE)
                    V.tensor_tensor(wlo[:, j * CW:(j + 1) * CW].rearrange("p (c m f) -> p c m f", m=2, f=DE),
                                    part[:, c], hi, ALU.subtract).then_inc(sem[f"lo_dve{L}"], 1)

                def x_low(n, k):
                    dve.wait_ge(sem[f"xhi_act{L}"], pairs_before(n, k) + 1)
                    V.tensor_tensor(xe[:, :, :, CAP:2 * CAP].rearrange("p e c s -> p c e s"),
                                    PS[0][:, :].rearrange("p (c e s) -> p c e s", c=KC, e=2),
                                    xe[:, :, :, 0:CAP].bitcast(F32).rearrange("p e c s -> p c e s"), ALU.subtract)\
                        .then_inc(sem[f"xlo_dve{L}"], 1)

                def y_half(n, k):
                    dve.wait_ge(sem[f"down_pe{L}"], n + 1)
                    V.tensor_scalar(half_rows(rows_u, k), gslot[:, k, 1:2], NOWHERE, None, ALU.add)
                    V.tensor_copy(half_rows(ys, k)[:, 512:1024], PS[3][0:CAP, 512:1024]).then_inc(sem[f"yd_dve{L}"], 1)

                def add_shared(tc):
                    dve.wait_ge(sem["sdown_pe"], TC * L + tc + 1)
                    V.scalar_tensor_tensor(acc[:, tc, :], xrow[:, tc, :], ALPHA, PS[3][:, :], ALU.mult, ALU.add)\
                        .then_inc(sem["acc_dve"], 1)

                settle("rank_dve")
                pick(0, 0, True)
                for j in range(NCHUNK):
                    low(0, 0, j)
                x_low(0, 0)
                src = sel
                for i in range(6):
                    w, dst = 1 << i, pre[i % 2]
                    V.tensor_copy(dst[:, :, 0:w], src[:, :, 0:w])
                    link(V.tensor_tensor(dst[:, :, w:], src[:, :, w:], src[:, :, 0:NE - w], ALU.add))
                    src = dst
                link(V.tensor_tensor(pre[0], src, sel, ALU.subtract))
                tok = mcon[:, M_TOK:M_TOK + TC]
                V.tensor_copy(table[:, :, :, 0], gate)
                for tc in range(TC):
                    ins = V.tensor_scalar(table[:, tc, :, 1], pre[0][:, tc, :], float(S), tok[:, tc:tc + 1], ALU.mult, ALU.add)
                link(ins)
                settle("rank_dve")
                pick(2, 2, True)
                add_shared(0)

                def step(n, k, have):
                    if k % 2 == 0 and have(4):
                        pick(n + 4, k + 4, False)
                    if have(1):
                        low(n + 1, k + 1, 0)
                    dve.wait_ge(sem[f"top_act{L}"], n + 1)
                    if have(-1):
                        dve.wait_ge(sem[f"silu_act{L}"], n)
                        dve.wait_ge(sem[f"h_dve{L}"], n)
                    V.tensor_tensor(gusum, BANK[2 + k % 2][CAP:2 * CAP, :], gutop, ALU.add).then_inc(sem[f"sum_dve{L}"], 1)
                    if have(1):
                        low(n + 1, k + 1, 1)
                    if not have(-1):
                        gates_in(0, 0, True)
                        add_shared(1)
                    dve.wait_ge(sem[f"silu_act{L}"], n + 1)
                    dve.wait_ge(sem[f"gates_dve{L}"], pairs_before(n, k) + 1)
                    if have(-2):
                        dve.wait_ge(sem[f"ht_pe{L}"], n - 1)
                    V.scalar_tensor_tensor(hh[k % 2], sg, gslot[:, k, 0:1], gusum[:, DE:2 * DE],
                                           ALU.mult, ALU.mult).then_inc(sem[f"h_dve{L}"], 1)
                    if have(1):
                        if k % 2:
                            x_low(n + 1, k + 1)
                        low(n + 1, k + 1, 2)
                        low(n + 1, k + 1, 3)
                        if k % 2:
                            gates_in(n + 1, k + 1, not have(-3))
                    if have(-4):
                        dve.wait_ge(sem[f"scatter{k // 2}_out{L}"], uses_before(n, k) * 16)
                    if have(-1):
                        y_half(n - 1, (k - 1) % NSLOT)

                n_groups = steps(dve, L, step)
                y_half(n_groups * NSLOT - 1, 3)

            dve.wait_ge(sem["x_in"], 32)
            mark(V.tensor_scalar(nsink, sinkb, -1.0, None, ALU.mult), "sink_dve")
            columns(0)
            hv = [v(h, k=2, n=32)[:, :, 0:G * NCMP] for h in hidw]

            def windows():
                dve.wait_ge(sem["kcv_act"], 2)
                dve.wait_ge(sem["pet_act"], 1)
                for i in range(2):
                    for lh in range(2):
                        for g in range(G):
                            src = kcv[0:HD, 2 * i + g, lh * 16:lh * 16 + NCMP * CMP_STRIDE]\
                                .rearrange("p (n l) -> p l n", l=CMP_STRIDE)
                            pos = pet[0:HD, i, lh * 16:(lh + 1) * 16]
                            mark(V.tensor_tensor(blk[i][HD * lh:HD * lh + HD, :, g, :], src,
                                                 pos[:, :, None].to_broadcast([HD, 16, NCMP]), ALU.add), "blk_dve")

            def gelu_inner():
                dve.wait_ge(sem["hid_act"], 1)
                link(V.tensor_tensor(hv[1], hv[0], hv[0], ALU.mult))
                link(V.tensor_scalar(hv[1], hv[1], 0.044715, 1.0, ALU.mult, ALU.add))
                mark(V.tensor_tensor(hv[2], hv[1], hv[0], ALU.mult), "gin_dve")

            def gelu_outer():
                dve.wait_ge(sem["gexp_act"], 1)
                link(V.tensor_scalar(hv[4], hv[3], 1.0, None, ALU.add))
                link(V.reciprocal(hv[4], hv[4]))
                mark(V.tensor_tensor(hv[5], hv[0], hv[4], ALU.mult), "gelu_dve")

            same = lambda a: a
            by_group = lambda a: a.rearrange("p (g j) d -> p g j d", g=G)

            def tables(tc):
                return cst[:, K_COS + tc * HD:K_COS + (tc + 1) * HD], cst[:, K_SIN + tc * HD:K_SIN + (tc + 1) * HD]

            def out_q(tc, b):
                o = rope[:, tc, b * P:(b + R) * P].rearrange("p (j g d) -> p g j d", j=R, g=G)
                return o[:, :, :, 0:HALF], o[:, :, :, HALF:HD]

            def out_k(tc, b):
                o = v(rope[:, tc, b * P:(b + 1) * P], g=G, d=HD)
                return o[:, :, 0:HALF], o[:, :, HALF:HD]

            def copied(i):
                dve.wait_ge(sem["proj_act0"], i)
                dve.wait_ge(sem["proj_dve0"], i)

            for i, n in enumerate(PARTS0):
                dve.wait_ge(sem["proj_pe0"], 2 * i + 2)
                mark(V.tensor_copy(qkv[:, 1, n * 512:(n + 1) * 512], BANK[2 * n + 1]), "proj_dve0")
                if n == 0:
                    windows()
                if n == 1:
                    copied(3)
                    for tc in range(TC):
                        apply_rope(v(qkv[:, tc, C_QA:C_VA], h=10, d=HD),
                                   [(0, 8, out_q(tc, 0), by_group), (8, 10, out_k(tc, 4), same)], *tables(tc), 10, HALF)
                        if tc == 1:
                            gelu_inner()
                        apply_rope(v(qkv[:, tc, C_QB:C_KC], h=8, d=HD), [(0, 8, out_q(tc, 5), by_group)],
                                   *tables(tc), 8, HALF)
                    gelu_outer()
            copied(4)
            for tc in range(TC):
                apply_rope(v(qkv[:, tc, C_KS:C_VS], h=2, d=HD), [(0, 2, out_k(tc, 9), same)], *tables(tc), 2, HALF)
                apply_rope(v(qkv[:, tc, C_KW:C_VW], h=2, d=HD), [(0, 2, out_k(tc, 10), same)], *tables(tc), 2, HALF,
                           "rope_dve0")
            dve.wait_ge(sem["gates_pe"], 2)
            link(V.tensor_scalar(v(gates, t=TC, n=NGATE), v(BANK[0][:, 0:64], t=TC, n=32)[:, :, 0:NGATE], 1.0, None, ALU.add))
            link(V.reciprocal(gates, gates))
            dve.wait_ge(sem["kv2_pe"], 1)
            dve.wait_ge(sem["zero_pool"], 2)
            cos, sin = cst[0:NCMP, K_CCOS:K_CCOS + HD], cst[0:NCMP, K_CSIN:K_CSIN + HD]
            ck = v(kcn[0:NCMP, :], g=G, d=HD)
            apply_rope(v(BANK[1][0:NCMP, 128:256], g=G, d=HD),
                       [(0, 2, (ck[:, :, 0:HALF], ck[:, :, HALF:HD]), same)], cos, sin, 2, HALF, "kcn_dve")
            for g in range(G):
                for j in range(R):
                    ins = V.tensor_copy(vbd[g][32 * j:32 * j + NCMP, j, :], BANK[1][0:NCMP, 256 + g * HD:256 + (g + 1) * HD])
            mark(ins, "vbd_dve")
            dve.wait_ge(sem["kct_pe"], 1)
            dve.wait_ge(sem["power_pool"], 2)
            for g in range(G):
                ins = V.tensor_copy(kcmpt[g * HD:(g + 1) * HD, g * NCMP:(g + 1) * NCMP], BANK[0][g * HD:(g + 1) * HD, 0:NCMP])
            mark(ins, "kct_dve")
            dve.wait_ge(sem["csc_pe"], 1)
            c8 = cs[:, :, :, 0:NCMP]
            for tc in range(TC):
                add = cst[:, K_CADD + tc * NCMP:K_CADD + (tc + 1) * NCMP]
                for g in range(G):
                    sc = v(BANK[5][:, 0:TC * P], t=TC, j=R, n=32)
                    ins = V.scalar_tensor_tensor(c8[:, tc, g * R:(g + 1) * R, :], sc[:, tc, :, g * NCMP:(g + 1) * NCMP], HD ** -0.5,
                                                 add[:, None, :].to_broadcast([P, R, NCMP]), ALU.mult, ALU.add)
            link(ins)
            cm = v(crec, t=TC, h=8)
            link(V.tensor_reduce(cm, c8, AX_X, ALU.max))
            mark(V.tensor_tensor(c8, c8, cm[:, :, :, None].to_broadcast([P, TC, 8, NCMP]), ALU.subtract), "csub_dve")
            attention(0)
            layer_norm(0, "mix")
            columns(1)
            routing(0)
            moe(0)
            layer_norm(0, "ffn")
            columns(2)
            dve.wait_ge(sem["small1_in"], 32)
            for tc in range(TC):
                dve.wait_ge(sem["proj_act1"], 2 * tc + 1)
                for i, (a, b) in enumerate(RMS_PARTS):
                    def variance():
                        return V.tensor_scalar(var[:, i:i + 1], ssq[:, 2 * tc + i:2 * tc + i + 1], 1.0 / (b - a), RMS_EPS,
                                               ALU.mult, ALU.add)
                    if i == 0:
                        link(variance())
                    else:
                        inverse_root(variance)
                dve.wait_ge(sem["proj_act1"], 2 * tc + 2)
                for i, (a, b) in enumerate(RMS_PARTS):
                    r = c1[:, tc, a:b]
                    ins = V.scalar_tensor_tensor(r, r, root[:, i:i + 1], lnp[:, a:b], ALU.mult, ALU.mult)
                mark(ins, "rms_dve")
            for tc in range(TC):
                cos = cst[:, K_COS1 + tc * ROPE:K_COS1 + (tc + 1) * ROPE]
                sin = cst[:, K_SIN1 + tc * ROPE:K_SIN1 + (tc + 1) * ROPE]
                o = v(c1[:, tc, QL + KVL:IN1], h=1, d=ROPE)
                apply_rope(o, [(0, 1, (o[:, :, 0:16], o[:, :, 16:32]), same)], cos, sin, 1, 16, "krope_dve")
            dve.wait_ge(sem["krt_act"], 1)
            mark(V.tensor_copy(kt1[NOPE:DQK, :, :], krt[:, None, :].to_broadcast([ROPE, MH, S])), "kfull_dve")
            for tc in range(TC):
                dve.wait_ge(sem["q_act"], 3 * tc + 3)
                cos = cst[:, K_COS1 + tc * ROPE:K_COS1 + (tc + 1) * ROPE]
                sin = cst[:, K_SIN1 + tc * ROPE:K_SIN1 + (tc + 1) * ROPE]
                o = v(qn1[:, tc, :], h=MH, d=DQK)[:, :, NOPE:DQK]
                apply_rope(o, [(0, MH, (o[:, :, 0:16], o[:, :, 16:32]), same)], cos, sin, MH, 16, "qrope_dve")
            attention(1)
            layer_norm(1, "mix")
            columns(3)
            routing(1)
            moe(1)
            layer_norm(1, "ffn")


_INS = ['x', 'swa_nsa_w_in', 'swa_sinks', 'nsa_cmp_pe_k', 'nsa_cmp_k_w1', 'nsa_cmp_k_w2', 'nsa_cmp_pe_v',
        'nsa_cmp_v_w1', 'nsa_cmp_v_w2', 'swa_nsa_w_out', 'mla_w_in', 'mla_q_norm', 'mla_kv_norm', 'mla_w_uq',
        'mla_w_ukv', 'mla_w_out', 'ln_mix_g', 'ln_mix_b', 'ln_ffn_g', 'ln_ffn_b', 'router_w', 'router_bias',
        'expert_w_gate', 'expert_w_up', 'expert_w_down', 'shared_w_gate', 'shared_w_up', 'shared_w_down']


def kernel(**inputs):
    import concourse.bacc as bacc
    from concourse.bass_utils import run_bass_kernel_spmd

    nc = bacc.Bacc("TRN2", target_bir_lowering=False, num_devices=1)
    arrays, args = {}, []
    for name in _INS + ["constants", "mixture_constants"]:
        if name == "constants":
            a = constants()
        elif name == "mixture_constants":
            a = mixture_constants()
        else:
            a = np.ascontiguousarray(inputs[name])
        arrays[f"in_{name}"] = a
        args.append(nc.dram_tensor(f"in_{name}", a.shape, mybir.dt.from_np(a.dtype), kind="ExternalInput").ap())
    out = nc.dram_tensor("out_0", (1, S, D), F32, kind="ExternalOutput").ap()
    bass_hybrid_block(nc, *args, out)
    r = run_bass_kernel_spmd(nc, [arrays], core_ids=[0])
    return r.results[0]["out_0"]
```
